# Optimizing a Trainium2 kernel written in Bass

```python
import math
import jax
import jax.numpy as jnp
from jax import lax
import numpy as np
import jax, jax.numpy as jnp

D_MODEL = 1024
BATCH = 1
SEQ = 256
DEPTH = 2

CTX_LEN = 256
GRID_W = 64
HEAD_DIM = 64
N_GROUPS = 4
GROUP_W = D_MODEL // N_GROUPS
MIX_W = N_GROUPS * GROUP_W
HEADS_PER_GROUP = GROUP_W // HEAD_DIM
CHUNK = 128
DIFF_D = HEAD_DIM // 2
NA_ROWS = 8
NA_COLS = 16
NA_QCOLS = 16
NA_KCOLS = 32
N_EXPERTS = 16
EXPERT_FF = D_MODEL
CAPACITY_FACTOR = 2
ROPE_BASE = 10000.0
EPS = 1e-6
DIFF_Q_BLOCK = 128
A_END = 2 * GROUP_W
B_END = A_END + GROUP_W
C_END = B_END + 3 * GROUP_W
IN_W = C_END + 3 * GROUP_W


def rms_norm(x, g=None, eps=EPS):
    xf = x.astype(jnp.float32)
    y = xf * lax.rsqrt(jnp.mean(xf * xf, axis=-1, keepdims=True) + eps)
    if g is not None:
        y = y * g.astype(jnp.float32)
    return y.astype(x.dtype)

def axial_rope_tables(n_tokens, dim):
    half = dim // 2
    inv = 1.0 / (ROPE_BASE ** (jnp.arange(0, half, 2, dtype=jnp.float32) / half))
    t = jnp.arange(n_tokens)
    row = (t // GRID_W).astype(jnp.float32)[:, None] * inv
    col = (t % GRID_W).astype(jnp.float32)[:, None] * inv
    return (jnp.cos(row), jnp.sin(row), jnp.cos(col), jnp.sin(col))

def _rotate(x, cos, sin):
    x1, x2 = jnp.split(x, 2, axis=-1)
    return jnp.concatenate([x1 * cos - x2 * sin, x2 * cos + x1 * sin], axis=-1)

def apply_axial_rope(x, rope):
    n = x.shape[1]
    shp = (1, n) + (1,) * (x.ndim - 3) + (-1,)
    cr, sr, cc, sc = [t.reshape(shp).astype(x.dtype) for t in rope]
    xr, xc = jnp.split(x, 2, axis=-1)
    return jnp.concatenate([_rotate(xr, cr, sr), _rotate(xc, cc, sc)], axis=-1)

def chunk_spatial_gating(p, w_s, b_s):
    bn, n, _ = p.shape
    z = jax.nn.gelu(p)
    u, v = jnp.split(z, 2, axis=-1)
    v = rms_norm(v.reshape(bn, n // CHUNK, CHUNK, HEADS_PER_GROUP, HEAD_DIM))
    sv = jnp.einsum('hpq,bnqhc->bnphc', w_s, v) + b_s.T[None, None, :, :, None]
    return u * sv.reshape(bn, n, GROUP_W)

def fourier_mix(p):
    bn, n, _ = p.shape
    z = p.astype(jnp.float32).reshape(bn, n, HEADS_PER_GROUP, HEAD_DIM)
    f = jnp.fft.fft2(z, axes=(1, 3), norm="ortho").real
    return f.reshape(bn, n, GROUP_W).astype(p.dtype)

def lambda_value(lam, lam_init):
    lf = lam.astype(jnp.float32)
    return jnp.exp(jnp.sum(lf[0] * lf[1])) - jnp.exp(jnp.sum(lf[2] * lf[3])) + lam_init

def diff_attn_core(q, k, v, lam):
    s = jnp.einsum('bqhmd,bkhmd->bhmqk', q, k).astype(jnp.float32) * (DIFF_D ** -0.5)
    a = jax.nn.softmax(s, axis=-1)
    w = a[:, :, 0] - lam * a[:, :, 1]
    return jnp.einsum('bhqk,bkhd->bqhd', w.astype(v.dtype), v)

def ctx_attention(q, k, v):
    s = jnp.einsum('bqhd,bkhd->bhqk', q, k).astype(jnp.float32) * (HEAD_DIM ** -0.5)
    p = jax.nn.softmax(s, axis=-1).astype(v.dtype)
    return jnp.einsum('bhqk,bkhd->bqhd', p, v)

def neighbourhood_attn_latent(q, k, v, kc, vc, rpb):
    bn, n, h, dh = q.shape
    rows = n // GRID_W
    kr = min(NA_ROWS, rows)
    n_cb = GRID_W // NA_QCOLS
    scale = HEAD_DIM ** -0.5
    qg = q.reshape(bn, rows, n_cb, NA_QCOLS, h, dh).transpose(1, 0, 2, 3, 4, 5)
    kg = k.reshape(bn, rows, GRID_W, h, dh)
    vg = v.reshape(bn, rows, GRID_W, h, dh)
    qcol = jnp.arange(GRID_W).reshape(n_cb, NA_QCOLS)
    kstart = jnp.clip(qcol[:, 0] - NA_COLS // 2, 0, GRID_W - NA_KCOLS)
    kcol = kstart[:, None] + jnp.arange(NA_KCOLS)
    wstart = jnp.clip(qcol - NA_COLS // 2, 0, GRID_W - NA_COLS)
    kc3 = kcol[:, None, :]
    valid = (kc3 >= wstart[..., None]) & (kc3 < wstart[..., None] + NA_COLS)
    coff = jnp.clip(kc3 - qcol[..., None], -(NA_COLS - 1), NA_COLS - 1) + NA_COLS - 1
    rpb_c = rpb[:, :, coff]
    n_loc = kr * NA_KCOLS

    def one_row(args):
        r, q_row = args
        rstart = jnp.clip(r - kr // 2, 0, rows - kr)
        k_rows = lax.dynamic_slice_in_dim(kg, rstart, kr, axis=1)
        v_rows = lax.dynamic_slice_in_dim(vg, rstart, kr, axis=1)
        k_blk = k_rows[:, :, kcol]
        v_blk = v_rows[:, :, kcol]
        roff = rstart + jnp.arange(kr) - r + NA_ROWS - 1
        bias = rpb_c[:, roff].transpose(0, 2, 3, 1, 4).astype(jnp.float32)
        s_loc = jnp.einsum('bjqhd,brjkhd->bhjqrk', q_row, k_blk).astype(jnp.float32) * scale + bias
        s_loc = jnp.where(valid[:, :, None, :], s_loc, -jnp.inf)
        s_loc = s_loc.reshape(bn, h, n_cb, NA_QCOLS, n_loc)
        s_ctx = jnp.einsum('bjqhd,bkhd->bhjqk', q_row, kc).astype(jnp.float32) * scale
        p = jax.nn.softmax(jnp.concatenate([s_loc, s_ctx], axis=-1), axis=-1).astype(v.dtype)
        p_loc = p[..., :n_loc].reshape(bn, h, n_cb, NA_QCOLS, kr, NA_KCOLS)
        p_ctx = p[..., n_loc:]
        o = (jnp.einsum('bhjqrk,brjkhd->bjqhd', p_loc, v_blk)
             + jnp.einsum('bhjqk,bkhd->bjqhd', p_ctx, vc))
        return o.reshape(bn, GRID_W, h * dh)

    out = lax.map(one_row, (jnp.arange(rows), qg))
    return out.transpose(1, 0, 2, 3).reshape(bn, n, h * dh)

def token_mixers(hx, hc, w_in, w_out, head_g, sgu_w, sgu_b, dqn, dkn, dlam,
                 nqn, nkn, rpb, rope, lam_init, ctx_out):
    bn, n, _ = hx.shape
    h = HEADS_PER_GROUP
    px = hx @ w_in
    pc = hc @ w_in
    lam = lambda_value(dlam, lam_init)
    head_scale = jnp.asarray(np.array([1.0] * (2 * h) + [1.0 - lam_init] * h + [1.0] * h,
                                      dtype=np.float32), dtype=hx.dtype)

    def groups(p):
        return p[..., :A_END], p[..., A_END:B_END], p[..., B_END:C_END], p[..., C_END:]

    def diff_qkv(p, use_rope):
        m = p.shape[1]
        q, k, v = jnp.split(p, 3, axis=-1)
        q = rms_norm(q.reshape(bn, m, h, 2, DIFF_D), dqn)
        k = rms_norm(k.reshape(bn, m, h, 2, DIFF_D), dkn)
        if use_rope:
            q = apply_axial_rope(q, rope)
            k = apply_axial_rope(k, rope)
        return q, k, v.reshape(bn, m, h, HEAD_DIM)

    def na_qkv(p):
        m = p.shape[1]
        q, k, v = jnp.split(p, 3, axis=-1)
        q = rms_norm(q.reshape(bn, m, h, HEAD_DIM), nqn)
        k = rms_norm(k.reshape(bn, m, h, HEAD_DIM), nkn)
        return q, k, v.reshape(bn, m, h, HEAD_DIM)

    def merge(ya, yb, yc, yd):
        y = jnp.concatenate([ya, yb, yc, yd], axis=-1)
        m = y.shape[1]
        y = rms_norm(y.reshape(bn, m, N_GROUPS * h, HEAD_DIM), head_g.reshape(N_GROUPS * h, HEAD_DIM))
        y = y * head_scale[:, None]
        return y.reshape(bn, m, MIX_W) @ w_out

    aX, bX, cX, dX = groups(px)
    aC, bC, cC, dC = groups(pc)

    cq_c, ck_c, cv_c = diff_qkv(cC, False)
    nq_c, nk_c, nv_c = na_qkv(dC)

    ya = chunk_spatial_gating(aX, sgu_w, sgu_b)
    yb = fourier_mix(bX)
    cq, ck, cv = diff_qkv(cX, True)
    k_all = jnp.concatenate([ck, ck_c], axis=1)
    v_all = jnp.concatenate([cv, cv_c], axis=1)
    qb = cq.reshape(bn, n // DIFF_Q_BLOCK, DIFF_Q_BLOCK, h, 2, DIFF_D).transpose(1, 0, 2, 3, 4, 5)
    yc = lax.map(lambda qblk: diff_attn_core(qblk, k_all, v_all, lam), qb)
    yc = yc.transpose(1, 0, 2, 3, 4).reshape(bn, n, GROUP_W)
    nq, nk, nv = na_qkv(dX)
    yd = neighbourhood_attn_latent(nq, nk, nv, nk_c, nv_c, rpb)
    y_lat = merge(ya, yb, yc, yd)

    if not ctx_out:
        return y_lat, None
    m = hc.shape[1]
    ya_c = chunk_spatial_gating(aC, sgu_w, sgu_b)
    yb_c = fourier_mix(bC)
    yc_c = diff_attn_core(cq_c, ck_c, cv_c, lam).reshape(bn, m, GROUP_W)
    yd_c = ctx_attention(nq_c, nk_c, nv_c).reshape(bn, m, GROUP_W)
    return y_lat, merge(ya_c, yb_c, yc_c, yd_c)

def expert_choice_ffn(x, router_w, wg, wu, wd):
    bn, n, _ = x.shape
    cap = CAPACITY_FACTOR * n // N_EXPERTS
    aff = jax.nn.softmax(jnp.einsum('bnd,de->bne', x, router_w).astype(jnp.float32), axis=-1)
    gate, idx = lax.top_k(aff.transpose(0, 2, 1), cap)
    bidx = jnp.arange(bn)[:, None, None]
    xg = x[bidx, idx]
    hid = jax.nn.silu(jnp.einsum('becd,edf->becf', xg, wg)) * jnp.einsum('becd,edf->becf', xg, wu)
    o = jnp.einsum('becf,efd->becd', hid, wd) * gate[..., None].astype(x.dtype)
    return jnp.zeros_like(x).at[bidx, idx].add(o)

def first_inputs(seed: int = 0) -> dict:
    key = jax.random.key(seed)
    ks = jax.random.split(key, 24)
    f32 = jnp.float32
    L, D, H = DEPTH, D_MODEL, HEADS_PER_GROUP

    def nrm(k, shape, s):
        return jax.random.normal(k, shape, f32) * s

    return {
        "x": nrm(ks[0], (BATCH, SEQ, D), 1.0),
        "c": nrm(ks[1], (BATCH, D), 1.0),
        "ctx": nrm(ks[2], (BATCH, CTX_LEN, D), 1.0),
        "c_ctx": nrm(ks[3], (D,), 1.0),
        "ada_w": nrm(ks[4], (L, D, 6 * D), 0.5 * D ** -0.5),
        "ada_b": nrm(ks[5], (L, 6 * D), 0.02),
        "norm1_g": 1.0 + nrm(ks[6], (L, D), 0.02),
        "norm2_g": 1.0 + nrm(ks[7], (L, D), 0.02),
        "w_in": nrm(ks[8], (L, D, IN_W), D ** -0.5),
        "w_out": nrm(ks[9], (L, MIX_W, D), MIX_W ** -0.5),
        "head_out_g": 1.0 + nrm(ks[10], (L, MIX_W), 0.02),
        "sgu_w": nrm(ks[11], (L, H, CHUNK, CHUNK), CHUNK ** -0.5),
        "sgu_b": 1.0 + nrm(ks[12], (L, H, CHUNK), 0.02),
        "diff_qn_g": 1.0 + nrm(ks[13], (L, DIFF_D), 0.02),
        "diff_kn_g": 1.0 + nrm(ks[14], (L, DIFF_D), 0.02),
        "diff_lambda": nrm(ks[15], (L, 4, DIFF_D), 0.1),
        "na_qn_g": 1.0 + nrm(ks[16], (L, HEAD_DIM), 0.02),
        "na_kn_g": 1.0 + nrm(ks[17], (L, HEAD_DIM), 0.02),
        "na_rpb": nrm(ks[18], (L, H, 2 * NA_ROWS - 1, 2 * NA_COLS - 1), 0.1),
        "router_w": nrm(ks[19], (L, D, N_EXPERTS), D ** -0.5),
        "exp_w_gate": nrm(ks[20], (L, N_EXPERTS, D, EXPERT_FF), D ** -0.5),
        "exp_w_up": nrm(ks[21], (L, N_EXPERTS, D, EXPERT_FF), D ** -0.5),
        "exp_w_down": nrm(ks[22], (L, N_EXPERTS, EXPERT_FF, D), EXPERT_FF ** -0.5),
    }

def first_block(x, c, ctx, c_ctx, ada_w, ada_b, norm1_g, norm2_g, w_in, w_out, head_out_g,
              sgu_w, sgu_b, diff_qn_g, diff_kn_g, diff_lambda, na_qn_g, na_kn_g, na_rpb,
              router_w, exp_w_gate, exp_w_up, exp_w_down):
    n = x.shape[1]
    rope = axial_rope_tables(n, DIFF_D)
    s_c = jax.nn.silu(c)
    s_cc = jax.nn.silu(c_ctx)
    xc = ctx
    for l in range(DEPTH):
        last = l == DEPTH - 1
        lam_init = 0.8 - 0.6 * math.exp(-0.3 * l)
        mod = (s_c @ ada_w[l] + ada_b[l])[:, None, :]
        mod_c = (s_cc @ ada_w[l] + ada_b[l])[None, None, :]
        sh1, sc1, g1, sh2, sc2, g2 = jnp.split(mod, 6, axis=-1)
        csh1, csc1, cg1, csh2, csc2, cg2 = jnp.split(mod_c, 6, axis=-1)
        hx = rms_norm(x, norm1_g[l]) * (1.0 + sc1) + sh1
        hc = rms_norm(xc, norm1_g[l]) * (1.0 + csc1) + csh1
        y_lat, y_ctx = token_mixers(hx, hc, w_in[l], w_out[l], head_out_g[l], sgu_w[l], sgu_b[l],
                                    diff_qn_g[l], diff_kn_g[l], diff_lambda[l],
                                    na_qn_g[l], na_kn_g[l], na_rpb[l], rope, lam_init,
                                    not last)
        x = x + g1 * y_lat
        x = x + g2 * expert_choice_ffn(rms_norm(x, norm2_g[l]) * (1.0 + sc2) + sh2,
                                       router_w[l], exp_w_gate[l], exp_w_up[l], exp_w_down[l])
        if not last:
            xc = xc + cg1 * y_ctx
            xc = xc + cg2 * expert_choice_ffn(rms_norm(xc, norm2_g[l]) * (1.0 + csc2) + csh2,
                                              router_w[l], exp_w_gate[l], exp_w_up[l], exp_w_down[l])
    return x


N_MIXERS = 2
N_LRU_LAYERS = (DEPTH + 1) // 2
N_POOL_LAYERS = DEPTH // 2
D_FF = 11 * D_MODEL // 4
D_RNN = 5 * D_MODEL // 4
LRU_HEADS = 16
LRU_HEAD_DIM = D_RNN // LRU_HEADS
CONV_WIDTH = 4
LRU_C = 8.0
POOL_WINDOWS = (2, 4, 8, 16)
POOL_GROUPS = len(POOL_WINDOWS)
POOL_GROUP_DIM = D_MODEL // POOL_GROUPS
PLE_DIM = 256
RMS_EPS = 1e-6


def rms_norm_2(x, g):
    xf = x.astype(jnp.float32)
    y = xf * lax.rsqrt(jnp.mean(xf * xf, axis=-1, keepdims=True) + RMS_EPS)
    return (y * g.astype(jnp.float32)).astype(x.dtype)

def swiglu(x, w_gate, w_up, w_down):
    return (jax.nn.silu(x @ w_gate) * (x @ w_up)) @ w_down

def _lin_combine(c1, c2):
    a1, b1 = c1
    a2, b2 = c2
    return a1 * a2, a2 * b1 + b2

def rglru_mixer(x, w_in, conv_w, conv_b, w_a, b_a, w_x, b_x, a_param, w_out):
    B, S, _ = x.shape
    z = x @ w_in
    gate_branch, xb = z[..., :D_RNN], z[..., D_RNN:]
    xp = jnp.pad(xb, ((0, 0), (CONV_WIDTH - 1, 0), (0, 0)))
    xc = conv_b + conv_w[0] * xp[:, 0:S]
    for k in range(1, CONV_WIDTH):
        xc = xc + conv_w[k] * xp[:, k:k + S]
    xh = xc.reshape(B, S, LRU_HEADS, LRU_HEAD_DIM)
    r = jax.nn.sigmoid(jnp.einsum('bshi,hij->bshj', xh, w_a).reshape(B, S, D_RNN) + b_a)
    ig = jax.nn.sigmoid(jnp.einsum('bshi,hij->bshj', xh, w_x).reshape(B, S, D_RNN) + b_x)
    log_a = -LRU_C * r.astype(jnp.float32) * jax.nn.softplus(-a_param.astype(jnp.float32))
    a = jnp.exp(log_a)
    mult = jnp.sqrt(-jnp.expm1(2.0 * log_a))
    bterm = mult * (ig * xc).astype(jnp.float32)
    _, h = lax.associative_scan(_lin_combine, (a, bterm), axis=1)
    y = h.astype(x.dtype) * jax.nn.gelu(gate_branch)
    return y @ w_out

def pool_mixer(x, w, b, scale):
    B, S, _ = x.shape
    xf = x.astype(jnp.float32)
    cs = jnp.cumsum(xf, axis=1)
    t = jnp.arange(S)
    outs = []
    for g, win in enumerate(POOL_WINDOWS):
        lo, hi = g * POOL_GROUP_DIM, (g + 1) * POOL_GROUP_DIM
        c = cs[..., lo:hi]
        prev = jnp.pad(c[:, :S - win], ((0, 0), (win, 0), (0, 0)))
        count = jnp.minimum(t + 1, win).astype(jnp.float32)[None, :, None]
        outs.append((c - prev) / count - xf[..., lo:hi])
    u = jnp.stack(outs, axis=2).astype(x.dtype)
    y = jnp.einsum('bsgc,gcd->bsgd', u, w).reshape(B, S, D_MODEL)
    return (y + b) * scale

def second_inputs(seed: int = 0) -> dict:
    key = jax.random.key(seed)
    ks = iter(jax.random.split(key, 40))

    def nrm(shape, scale):
        return scale * jax.random.normal(next(ks), shape, jnp.float32)

    D, F, L = D_MODEL, D_FF, DEPTH
    NL, NP = N_LRU_LAYERS, N_POOL_LAYERS
    x = nrm((BATCH, SEQ, D), 1.0)
    p = nrm((DEPTH, BATCH, SEQ, PLE_DIM), 1.0)
    ffn1_norm = 1.0 + nrm((L, D), 0.1)
    ffn1_w_gate = nrm((L, D, F), D ** -0.5)
    ffn1_w_up = nrm((L, D, F), D ** -0.5)
    ffn1_w_down = nrm((L, F, D), F ** -0.5)
    mix_norm = 1.0 + nrm((L, D), 0.1)
    lru_w_in = nrm((NL, D, 2 * D_RNN), D ** -0.5)
    lru_conv_w = nrm((NL, CONV_WIDTH, D_RNN), CONV_WIDTH ** -0.5)
    lru_conv_b = nrm((NL, D_RNN), 0.01)
    lru_w_a = nrm((NL, LRU_HEADS, LRU_HEAD_DIM, LRU_HEAD_DIM), LRU_HEAD_DIM ** -0.5)
    lru_b_a = nrm((NL, D_RNN), 0.01)
    lru_w_x = nrm((NL, LRU_HEADS, LRU_HEAD_DIM, LRU_HEAD_DIM), LRU_HEAD_DIM ** -0.5)
    lru_b_x = nrm((NL, D_RNN), 0.01)
    u = jax.random.uniform(next(ks), (NL, D_RNN), jnp.float32, minval=0.9, maxval=0.999)
    a0 = u ** (1.0 / LRU_C)
    lru_a_param = jnp.log(a0) - jnp.log1p(-a0)
    lru_w_out = nrm((NL, D_RNN, D), D_RNN ** -0.5)
    pool_w = nrm((NP, POOL_GROUPS, POOL_GROUP_DIM, POOL_GROUP_DIM), POOL_GROUP_DIM ** -0.5)
    pool_b = nrm((NP, D), 0.01)
    pool_scale = 1.0 + nrm((NP, D), 0.1)
    ffn2_norm = 1.0 + nrm((L, D), 0.1)
    ffn2_w_gate = nrm((L, D, F), D ** -0.5)
    ffn2_w_up = nrm((L, D, F), D ** -0.5)
    ffn2_w_down = nrm((L, F, D), F ** -0.5)
    ple_norm = 1.0 + nrm((L, D), 0.1)
    ple_w_gate = nrm((L, D, D), D ** -0.5)
    ple_w_proj = nrm((L, PLE_DIM, D), PLE_DIM ** -0.5)
    final_norm = 1.0 + nrm((D,), 0.1)
    return {"x": x, "p": p,
            "ffn1_norm": ffn1_norm, "ffn1_w_gate": ffn1_w_gate, "ffn1_w_up": ffn1_w_up, "ffn1_w_down": ffn1_w_down,
            "mix_norm": mix_norm,
            "lru_w_in": lru_w_in, "lru_conv_w": lru_conv_w, "lru_conv_b": lru_conv_b,
            "lru_w_a": lru_w_a, "lru_b_a": lru_b_a, "lru_w_x": lru_w_x, "lru_b_x": lru_b_x,
            "lru_a_param": lru_a_param, "lru_w_out": lru_w_out,
            "pool_w": pool_w, "pool_b": pool_b, "pool_scale": pool_scale,
            "ffn2_norm": ffn2_norm, "ffn2_w_gate": ffn2_w_gate, "ffn2_w_up": ffn2_w_up, "ffn2_w_down": ffn2_w_down,
            "ple_norm": ple_norm, "ple_w_gate": ple_w_gate, "ple_w_proj": ple_w_proj,
            "final_norm": final_norm}

def second_block(x, p, ffn1_norm, ffn1_w_gate, ffn1_w_up, ffn1_w_down, mix_norm,
              lru_w_in, lru_conv_w, lru_conv_b, lru_w_a, lru_b_a, lru_w_x, lru_b_x, lru_a_param, lru_w_out,
              pool_w, pool_b, pool_scale,
              ffn2_norm, ffn2_w_gate, ffn2_w_up, ffn2_w_down,
              ple_norm, ple_w_gate, ple_w_proj, final_norm):
    h = x
    for i in range(DEPTH):
        h = h + 0.5 * swiglu(rms_norm_2(h, ffn1_norm[i]), ffn1_w_gate[i], ffn1_w_up[i], ffn1_w_down[i])
        hn = rms_norm_2(h, mix_norm[i])
        j = i // N_MIXERS
        if i % N_MIXERS == 0:
            m = rglru_mixer(hn, lru_w_in[j], lru_conv_w[j], lru_conv_b[j], lru_w_a[j], lru_b_a[j],
                            lru_w_x[j], lru_b_x[j], lru_a_param[j], lru_w_out[j])
        else:
            m = pool_mixer(hn, pool_w[j], pool_b[j], pool_scale[j])
        h = h + m
        h = h + 0.5 * swiglu(rms_norm_2(h, ffn2_norm[i]), ffn2_w_gate[i], ffn2_w_up[i], ffn2_w_down[i])
        gate = jax.nn.sigmoid(rms_norm_2(h, ple_norm[i]) @ ple_w_gate[i])
        h = h + gate * (p[i].astype(h.dtype) @ ple_w_proj[i])
    return rms_norm_2(h, final_norm)


def setup_inputs(seed=0):
    out = dict(first_inputs(seed))
    for name, value in second_inputs(seed + 1).items():
        if name != "x":
            out[name + "_2"] = value
    return out


def reference(
    x, c, ctx, c_ctx, ada_w, ada_b, norm1_g, norm2_g, w_in, w_out, head_out_g, sgu_w, sgu_b,
    diff_qn_g, diff_kn_g, diff_lambda, na_qn_g, na_kn_g, na_rpb, router_w, exp_w_gate, exp_w_up,
    exp_w_down, p_2, ffn1_norm_2, ffn1_w_gate_2, ffn1_w_up_2, ffn1_w_down_2, mix_norm_2,
    lru_w_in_2, lru_conv_w_2, lru_conv_b_2, lru_w_a_2, lru_b_a_2, lru_w_x_2, lru_b_x_2,
    lru_a_param_2, lru_w_out_2, pool_w_2, pool_b_2, pool_scale_2, ffn2_norm_2, ffn2_w_gate_2,
    ffn2_w_up_2, ffn2_w_down_2, ple_norm_2, ple_w_gate_2, ple_w_proj_2, final_norm_2,
):
    x = first_block(
        x, c, ctx, c_ctx, ada_w, ada_b, norm1_g, norm2_g, w_in, w_out, head_out_g, sgu_w, sgu_b,
        diff_qn_g, diff_kn_g, diff_lambda, na_qn_g, na_kn_g, na_rpb, router_w, exp_w_gate,
        exp_w_up, exp_w_down,
    )
    return second_block(
        x, p_2, ffn1_norm_2, ffn1_w_gate_2, ffn1_w_up_2, ffn1_w_down_2, mix_norm_2, lru_w_in_2,
        lru_conv_w_2, lru_conv_b_2, lru_w_a_2, lru_b_a_2, lru_w_x_2, lru_b_x_2, lru_a_param_2,
        lru_w_out_2, pool_w_2, pool_b_2, pool_scale_2, ffn2_norm_2, ffn2_w_gate_2, ffn2_w_up_2,
        ffn2_w_down_2, ple_norm_2, ple_w_gate_2, ple_w_proj_2, final_norm_2,
    )


_drawn_inputs = setup_inputs


def setup_inputs(seed=0):
    import zlib

    import numpy as np

    out = dict(_drawn_inputs(seed))
    spreads = {}
    factors = {'norm1_g': 5.895,
     'norm2_g': 5.801,
     'head_out_g': 4.436,
     'sgu_b': 199.858,
     'diff_qn_g': 8.0,
     'diff_kn_g': 8.0,
     'diff_lambda': 3.467,
     'na_qn_g': 8.0,
     'na_kn_g': 8.0,
     'na_rpb': 8.0,
     'lru_conv_b_2': 167.872,
     'lru_b_a_2': 200.0,
     'lru_b_x_2': 200.0,
     'pool_b_2': 56.217,
     'ple_norm_2': 194.432,
     'ffn1_norm_2': 8.0,
     'mix_norm_2': 5.462,
     'lru_w_a_2': 41.592,
     'lru_w_x_2': 23.392,
     'lru_a_param_2': 37.936,
     'pool_scale_2': 6.268,
     'ffn2_norm_2': 8.0,
     'lru_w_in_2': 8.0,
     'lru_conv_w_2': 8.0,
     'lru_w_out_2': 8.0,
     'ple_w_gate_2': 2.841}
    for name, (base, spread) in spreads.items():
        noise = np.random.default_rng([zlib.crc32(name.encode()), seed]).standard_normal(out[name].shape)
        drawn = base * np.exp(spread * noise) if base else spread * noise
        out[name] = jnp.asarray(drawn.astype(out[name].dtype))
    for name, factor in factors.items():
        out[name] = (out[name] * factor).astype(out[name].dtype)
    return out
```

```python
from contextlib import ExitStack
import math

import numpy as np

import concourse.bass as bass
from concourse import mybir

F32 = mybir.dt.float32
BF16 = mybir.dt.bfloat16
ALU = mybir.AluOpType
ACT = mybir.ActivationFunctionType
AX = mybir.AxisListType.X

P = 128
D = 1024
KT = D // P
N = 256
LAYERS = 2
EPS = 1e-6
HEADS, HEAD = 4, 64
GROUP = HEADS * HEAD
DIFF = HEAD // 2
GRID_W = 64
NA_ROWS, NA_COLS = 8, 16
IN_W = 9 * GROUP
EXPERTS = 16
CAP = 2 * N // EXPERTS
D_FF = 11 * D // 4
FT = D_FF // P
D_RNN = 5 * D // 4
RT = D_RNN // P
LRU_HEAD = D_RNN // 16
CONV = 4
POOLS = (2, 4, 8, 16)
PLE = 256
NEG = -1e30

SLOTS = 6
SLOT = 4096

VEC1 = {"ada_b": 48, "norm1_g": 8, "norm2_g": 8, "head_out_g": 8, "sgu_b": 4}
VEC1_W = sum(VEC1.values())
VEC2 = {"ffn1_norm": 16, "mix_norm": 16, "ffn2_norm": 16, "ple_norm": 16, "conv_w": 40, "conv_b": 10,
        "b_a": 10, "b_x": 10, "a_param": 10, "pool_b": 8, "pool_scale": 8, "final_norm": 8}
VEC2_W = sum(VEC2.values())
ROWS = {"c_gain": 2 * DIFF, "c_gain_swapped": 2 * DIFF, "d_gain": 2 * HEAD, "lambda": 4 * DIFF}
ROWS_W = sum(ROWS.values())
CONST = {"ident": P, "slot_row": CAP, "slot_col": 1, "cos": 4 * DIFF, "sin": 4 * DIFF}
CONST_W = sum(CONST.values())
ATT = {"mask": N, "cos_n": 2 * N, "sin_n": 2 * N, "cs_d": 2 * P}
ATT_W = sum(ATT.values())


def columns(parts, name):
    at = 0
    for key, width in parts.items():
        if key == name:
            return slice(at, at + width)
        at += width
    raise KeyError(name)


def lru_pairs():
    out = []
    for o in range(RT):
        first = o * P // LRU_HEAD * LRU_HEAD
        last = (o * P + P - 1) // LRU_HEAD * LRU_HEAD + LRU_HEAD - 1
        out += [(o, k) for k in range(first // P, last // P + 1)]
    return out


PAIRS = lru_pairs()

COUNTS = {
    "rows_loaded": 32, "att_loaded": 32, "expand_loaded": 16,
    "proj_done": 18, "proj_read_act": 10, "proj_read_dve": 8,
    "mix_squares": 3, "mix_sums": 3, "mix_std": 2, "c_normed": 1, "c_swapped": 2, "v_normed": 1, "qk_ready": 2,
    "qk_turned": 8, "qk_t_act": 4, "qk_t_dve": 4, "sgu_mixed": 1, "sgu_done": 1,
    "fourier_uv": 4, "uv_ready": 4, "fourier_done": 4, "fourier_read": 2,
    "c_scores": 32, "c_max": 32, "c_exp": 32, "c_weights": 16, "c_turned": 16, "c_wt": 16, "c_pv": 16, "c_out": 4,
    "d_scores": 16, "d_max": 16, "d_exp": 16, "d_turned": 16, "d_wt": 16, "d_pv": 16, "d_out": 16,
    "y_squares": 1, "y_sums": 1, "y_std": 1, "y_normed": 1, "y_turned": 8, "y_t": 8, "mix_out": 8, "mix_added": 8,
    "logits": 1, "logits_shifted": 1, "logits_exp": 1, "h_turned": 8, "h_tok_act": 4, "h_tok_dve": 4,
    "aff": 1, "aff_turned": 1, "slots": 1, "slots_turned": 1, "aff_spread": 2, "slots_spread": 2, "aff_bc": 2,
    "gather_ready": 1, "scatter_ready": 4, "gathered": 16, "picked_act": 8, "picked_dve": 8,
    "x_exp": 16, "exp_silu": 16, "exp_hid": 16, "exp_turned": 16, "exp_hid_t": 16, "o_act": 16, "o_dve": 16,
    "moe_out": 8, "moe_added": 8,
}


def before(name, layer):
    return COUNTS[name] * layer


def proj_jobs(layer):
    tiles = range(4)
    own = range(4) if layer == 0 else range(2)
    jobs = [(0, t, 0, 512, "act") for t in own]
    jobs += [(1, t, 0, 512, "dve") if t in own else (1, t, 256, 256, "dve") for t in tiles]
    jobs += [(2, t, 0, 512, "act") if t in own else (2, t, 256, 256, "act") for t in tiles]
    jobs += [(3, t, 0, 512, "dve") for t in tiles]
    jobs += [(4, c, 0, P, "act") for c in range(2)]
    return jobs


def build(nc, dram, out_t):
    ctx = ExitStack()
    with ctx:
        def sb(name, shape, dt=F32):
            return ctx.enter_context(nc.sbuf_tensor(name, shape, dt))

        sems = {}

        def sem(name):
            if name not in sems:
                sems[name] = ctx.enter_context(nc.semaphore(name))
            return sems[name]

        ring = sb("ring", [P, SLOTS, SLOT])
        x_res = sb("x_res", [P, KT, 2 * N])
        h_buf = sb("h_buf", [P, KT, 2 * N])
        arena = sb("arena", [P, 16384])
        const = sb("const", [P, CONST_W])
        vec1 = sb("vec1", [P, LAYERS, VEC1_W])
        vec2 = sb("vec2", [P, VEC2_W])
        rows = sb("rows", [P, ROWS_W])
        router_sb = sb("router_sb", [P, LAYERS, KT, EXPERTS])
        cond_in = sb("cond_in", [P, KT, 2])
        cond = sb("cond", [P, KT, 32])
        mod = sb("mod", [P, LAYERS, 48, 2])
        gain1 = sb("gain1", [P, KT, 2])
        gain2 = sb("gain2", [P, KT, 2])
        rope_cos = sb("rope_cos", [P, 4, 2, DIFF])
        rope_sin = sb("rope_sin", [P, 4, 2, DIFF])
        mean_w = sb("mean_w", [P, P])
        zeros = sb("zeros", [P, 512], BF16)
        eps_col = sb("eps_col", [P, 1])
        small = sb("small", [P, 512])
        ps = ctx.enter_context(nc.psum_tensor("ps", [P, 8, 512], F32))

        def part(lo, hi):
            return arena[:, lo:hi]

        ycat = part(0, 4096).rearrange("p (t f) -> p t f", t=4)
        gated = part(4096, 6144).rearrange("p (t f) -> p t f", t=4)
        uv = part(4096, 6144).rearrange("p (t c w f) -> p t c w f", t=4, c=2, w=2)
        qk_c = part(6144, 8192).rearrange("p (t f) -> p t f", t=4)
        expo = part(6144, 8192).rearrange("p (b f) -> p b f", b=4)
        qk_d = part(8192, 10240).rearrange("p (t f) -> p t f", t=4)
        vals = part(10240, 12288).rearrange("p (t f) -> p t f", t=4)
        y_sq = part(8192, 12288)
        fourier_in = part(12288, 13312).rearrange("p (c f) -> p c f", c=2)
        w_t = part(12288, 13312).rearrange("p (b k f) -> p b k f", b=2, k=4)
        qk_t = part(13312, 15360).rearrange("p (b f) -> p b f", b=4)
        sgu_t = part(15360, 15872).rearrange("p (h f) -> p h f", h=HEADS)
        ada_rows = part(15872, 16384)
        sq_c, sq_v, sq_d = part(0, 2048), part(2048, 3072), part(13312, 15360)
        swapped = part(0, 2048)
        rstd = part(4096, 4608)
        h_flat = h_buf[:, :, :].rearrange("p k t -> p (k t)")
        rel_bias = h_flat[:, 0:2048].rearrange("p (q h f) -> p q h f", q=2, h=HEADS)
        att = h_flat[:, 2048:2048 + ATT_W]
        picked = part(0, 8192).rearrange("p (k e m) -> p k e m", k=KT, e=EXPERTS)
        aff_bc = part(0, 1024)
        expand = part(2048, 2560)
        aff_t, work, sel, cum, slot_id = (part(a, a + N) for a in (3072, 3328, 3584, 3840, 4608))
        h_tok = part(8192, 12288).rearrange("p (t f) -> p t f", t=4)
        o_lat = part(8192, 12288).rearrange("p (g f) -> p g f", g=4)
        o_ctx = h_flat.rearrange("p (g f) -> p g f", g=4)
        scatter = part(12288, 14336).rearrange("p (s g t) -> p s g t", s=2, g=4)
        gather = part(14336, 16384).rearrange("p (t e s) -> p t e s", t=4, e=EXPERTS)
        x_exp = part(14336, 15360)
        hid_exp = part(15360, 15872)
        hid_exp_t = part(15872, 16384)
        rstd2 = part(0, 256)
        silu_f = part(512, 1536).rearrange("p (f t) -> p f t", f=4)
        hid_f = part(1536, 2560).rearrange("p (f t) -> p f t", f=4)
        l_gate = part(2560, 5120).rearrange("p (o t) -> p o t", o=RT)
        l_pad = part(5120, 5120 + RT * 260).rearrange("p (o t) -> p o t", o=RT)
        l_a = part(5120, 7680).rearrange("p (o t) -> p o t", o=RT)
        l_x = part(7760, 10320).rearrange("p (o t) -> p o t", o=RT)
        l_r = part(10320, 12880).rearrange("p (o t) -> p o t", o=RT)
        l_i = part(12880, 15440).rearrange("p (o t) -> p o t", o=RT)
        pool_a = part(2560, 4608).rearrange("p (k t) -> p k t", k=KT)
        pool_b = part(4608, 6656).rearrange("p (k t) -> p k t", k=KT)
        pool_u = part(6656, 8704).rearrange("p (k t) -> p k t", k=KT)
        pool_inv = part(8704, 9728).rearrange("p (g t) -> p g t", g=4)

        ident = const[:, columns(CONST, "ident")]
        slot_row = const[:, columns(CONST, "slot_row")]
        slot_col = const[:, columns(CONST, "slot_col")]

        mix_ss = small[:, 0:112]
        c_max, c_den = small[:, 112:144], small[:, 144:176]
        d_max, d_den = small[:, 176:192], small[:, 192:208]
        y_ss = small[:, 208:272]
        logit = small[:, 320:384]
        r_max, r_sum = small[:, 384:388], small[:, 388:392]
        lam_tmp = small[:, 392:456]
        lam_sum, neg_lam = small[:, 456:458], small[:, 458:459]
        lru_s = [sb(f"lru_s{i}", [P, RT]) for i in range(6)]
        slot_tokens = sb("slot_tokens", [P, 4, EXPERTS])
        top8 = sb("top8", [P, 8])

        def picked_of(l):
            m = 2 * CAP if l == 0 else CAP
            return part(0, KT * EXPERTS * m).rearrange("p (k e m) -> p k e m", k=KT, e=EXPERTS)

        norms = []
        for l in range(LAYERS):
            norms += [(2 * N, 2, True), (2 * N, 2, True) if l == 0 else (N, 1, True)]
        norms += [(N, 1, False)] * (4 * LAYERS + 1)
        scaled_before = [sum(KT * s for _, s, _ in norms[:i]) for i in range(len(norms) + 1)]
        shifted_before = [sum(KT * s for _, s, sh in norms[:i] if sh) for i in range(len(norms) + 1)]
        NORM_END = scaled_before[-1]

        weights_used = sem("weights_used")
        slot_loaded = [sem(f"slot_loaded{i}") for i in range(SLOTS)]

        def slot(n):
            return ring[:, n % SLOTS, :]

        chunk_at = {}
        loads = []
        for l in range(LAYERS):
            if l == 0:
                chunk_at["ada", 0] = len(loads)
                loads += [1] * 12
            chunk_at["w_in", l] = len(loads)
            loads += [1, 1, 1, 2, 1]
            if l == 0:
                chunk_at["ada", 1] = len(loads)
                loads += [1] * 12
            chunk_at["w_out", l] = len(loads)
            loads += [1] * 2
            chunk_at["experts", l] = len(loads)
            loads += [1] * 6 * EXPERTS
        FFN_CHUNKS = 3 * ((FT + 3) // 4)
        for l in range(LAYERS):
            chunk_at["ffn", 2 * l] = len(loads)
            loads += [1] * FFN_CHUNKS
            if l == 0:
                chunk_at["lru", 0] = len(loads)
                loads += [1] * (5 + 2 + 3)
            else:
                chunk_at["pool", 0] = len(loads)
                loads += [1]
            chunk_at["ffn", 2 * l + 1] = len(loads)
            loads += [1] * FFN_CHUNKS
            chunk_at["ple", l] = len(loads)
            loads += [2, 1, 1]

        def loaded_value(n):
            return 16 * sum(loads[n % SLOTS:n + 1:SLOTS])

        block = ctx.enter_context(nc.Block())

        @block.sync
        def _(sp):
            sp.dma_start(x_res[:, :, 0:N], dram["x_t"].rearrange("(k p) t -> p k t", p=P)).then_inc(sem("x_loaded"), 16)
            sp.dma_start(x_res[:, :, N:2 * N], dram["ctx_t"].rearrange("(k p) t -> p k t", p=P)).then_inc(sem("x_loaded"), 16)

            def load(n, src, lo=0, first=True):
                width = 1
                for d in src.shape[1:]:
                    width *= d
                if first and n >= SLOTS:
                    sp.wait_ge(weights_used, n - SLOTS + 1)
                dst = slot(n)[:, lo:lo + width]
                if len(src.shape) == 3:
                    dst = dst.rearrange("p (a b) -> p a b", a=src.shape[1])
                sp.dma_start(dst, src).then_inc(slot_loaded[n % SLOTS], 16)

            def cols(w, lo, hi):
                return w[:, lo:hi].rearrange("(k p) n -> p k n", p=P)

            def krows(w, lo, hi):
                return w[lo * P:hi * P, :].rearrange("(k p) n -> p k n", p=P)

            def ada(l):
                for i in range(12):
                    load(chunk_at["ada", l] + i, cols(dram["ada_w"][l], 512 * i, 512 * i + 512))

            def ffn(i):
                l, which = divmod(i, 2)
                n = chunk_at["ffn", i]
                gate, up, down = (dram[f"ffn{which + 1}_{w}"][l] for w in ("gate", "up", "down"))

                for g in range((FT + 3) // 4):
                    lo, hi = 4 * g, min(4 * g + 4, FT)
                    load(n + 3 * g, cols(gate, lo * P, hi * P))
                    load(n + 3 * g + 1, cols(up, lo * P, hi * P))
                    load(n + 3 * g + 2, krows(down, lo, hi))

            for l in range(LAYERS):
                if l == 0:
                    ada(0)
                n, w = chunk_at["w_in", l], dram["w_in"][l]
                load(n, cols(w, 0, 2 * GROUP))
                load(n + 1, cols(w, 3 * GROUP, 5 * GROUP))
                load(n + 2, cols(w, 6 * GROUP, 8 * GROUP))
                load(n + 3, cols(w, 5 * GROUP, 6 * GROUP))
                load(n + 3, cols(w, 8 * GROUP, 9 * GROUP), lo=KT * GROUP, first=False)
                load(n + 4, cols(w, 2 * GROUP, 3 * GROUP))
                if l == 0:
                    ada(1)
                for i in range(2):
                    load(chunk_at["w_out", l] + i, cols(dram["w_out"][l], 512 * i, 512 * i + 512))
                n = chunk_at["experts", l]
                with sp.Fori(0, EXPERTS // 4) as it:
                    for c in range(24):
                        w = dram[("exp_gate", "exp_up", "exp_down")[c % 6 // 2]]
                        sp.wait_ge(weights_used, it * 24 + (n + c - SLOTS + 1))
                        half = c % 2
                        src = w[l, it * 4 + c // 6, half * 512:half * 512 + 512, :].rearrange("(k p) n -> p k n", p=P)
                        sp.dma_start(slot(n + c).rearrange("p (k n) -> p k n", k=4), src)\
                            .then_inc(slot_loaded[(n + c) % SLOTS], 16)
            for l in range(LAYERS):
                ffn(2 * l)
                if l == 0:
                    n = chunk_at["lru", 0]
                    for i in range(5):
                        load(n + i, cols(dram["lru_in"], 512 * i, 512 * i + 512))
                    load(n + 5, dram["lru_a"])
                    load(n + 6, dram["lru_x"])
                    for i in range(3):
                        load(n + 7 + i, krows(dram["lru_out"], 4 * i, min(4 * i + 4, RT)))
                else:
                    load(chunk_at["pool", 0], dram["pool_w"].rearrange("(j p) n -> p j n", p=P))
                ffn(2 * l + 1)
                n = chunk_at["ple", l]
                load(n, krows(dram["ple_proj"][l], 0, 2))
                load(n, krows(dram["p_t"][l], 0, 2), lo=2 * D, first=False)
                for i in range(2):
                    load(n + 1 + i, cols(dram["ple_gate"][l], 512 * i, 512 * i + 512))
            sp.wait_ge(sem("norm_scaled"), NORM_END)
            sp.dma_start(out_t.rearrange("(k p) t -> p k t", p=P), h_buf[:, :, 0:N]).then_inc(sem("out_stored"), 16)
            sp.wait_ge(sem("out_stored"), 16)

        @block.gpsimd
        def _(pool):
            loaded = sem("setup_loaded")
            pool.dma_start(cond_in[:, :, :], dram["cond_t"]).then_inc(loaded, 16)
            pool.dma_start(const[:, :], dram["const"]).then_inc(loaded, 16)
            pool.dma_start(vec1[:, :, :], dram["vec1"]).then_inc(loaded, 16)
            pool.dma_start(vec2[:, :], dram["vec2"]).then_inc(loaded, 16)
            pool.dma_start(router_sb[:, :, :, :].rearrange("p l k e -> p l (k e)"), dram["router"]).then_inc(loaded, 16)
            for l in range(LAYERS):
                if l > 0:
                    pool.wait_ge(sem("qk_ready"), 2 + before("qk_ready", l - 1))
                    pool.wait_ge(sem("sgu_done"), 1 + before("sgu_done", l - 1))
                    pool.wait_ge(sem("moe_added"), KT + before("moe_added", l - 1))
                pool.dma_start(rows[:, :], dram["rows"][l]).then_inc(sem("rows_loaded"), 16)
                pool.dma_start(sgu_t, dram["sgu_t"][l]).then_inc(sem("rows_loaded"), 16)
                pool.wait_ge(sem("proj_done"), len(proj_jobs(l)) + before("proj_done", l))
                pool.dma_start(att, dram["att"]).then_inc(sem("att_loaded"), 16)
                pool.dma_start(rel_bias, dram["rel_bias"][l]).then_inc(sem("att_loaded"), 16)
                pool.wait_ge(sem("mix_added"), KT + before("mix_added", l))
                pool.dma_start(expand[0:48, :], dram["expand"]).then_inc(sem("expand_loaded"), 16)
            pool.wait_ge(sem("ple_added"), KT)
            pool.dma_start(pool_inv, dram["pool_inv"]).then_inc(sem("pool_inv_loaded"), 16)

        def norm_pe(pe, release, i):
            width = norms[i][0]
            for k in range(KT):
                pe.wait_ge(sem("norm_squares"), KT * i + k + 1)
                mm = pe.matmul(ps[:, 0, 0:width], mean_w[:, :], h_buf[:, k, 0:width], start=k == 0, stop=k == KT - 1)
                if k == 0:
                    release(mm)
            mm.then_inc(sem("norm_mean"), 1)

        def norm_act(act, i, rs, shift):
            width, streams, shifted = norms[i]
            for k in range(KT):
                act.activation(h_buf[:, k, 0:width], x_res[:, k, 0:width], ACT.Square).then_inc(sem("norm_squares"), 1)
            act.wait_ge(sem("norm_mean"), i + 1)
            act.activation(rs[:, 0:width], ps[:, 0, 0:width], ACT.Sqrt, bias=eps_col[:, 0:1]).then_inc(sem("norm_std"), 1)
            if shifted:
                for k in range(KT):
                    for s in range(streams):
                        act.wait_ge(sem("norm_scaled"), scaled_before[i] + k * streams + s + 1)
                        part_ = h_buf[:, k, s * N:s * N + N]
                        act.activation(part_, part_, ACT.Identity, bias=shift[:, k, s:s + 1]).then_inc(sem("norm_shifted"), 1)

        def norm_dve(dve, link, i, rs, gain):
            width, streams, _ = norms[i]
            dve.wait_ge(sem("norm_std"), i + 1)
            link(dve.reciprocal(rs[:, 0:width], rs[:, 0:width]))
            for k in range(KT):
                for s in range(streams):
                    lo = s * N
                    dve.scalar_tensor_tensor(h_buf[:, k, lo:lo + N], x_res[:, k, lo:lo + N], gain(k, s),
                                             rs[:, lo:lo + N], ALU.mult, ALU.mult).then_inc(sem("norm_scaled"), 1)

        def norm_ready(eng, i):
            if norms[i][2]:
                eng.wait_ge(sem("norm_shifted"), shifted_before[i + 1])
            else:
                eng.wait_ge(sem("norm_scaled"), scaled_before[i + 1])

        def units(l):
            return [(q, h) for q in (range(4) if l == 0 else range(2)) for h in range(HEADS)]

        def keys(q):
            return (0, 512) if q < 2 else (256, 256)

        SC = GROUP // P

        @block.tensor
        def _(pe):
            owed = [0]

            def release(mm):
                if owed[0]:
                    mm.then_inc(weights_used, owed[0])
                    owed[0] = 0

            def chunk(n):
                pe.wait_ge(slot_loaded[n % SLOTS], loaded_value(n))

            def ada_group(l, i):
                step = 3 * l + i
                n = chunk_at["ada", l] + 4 * i
                for j in range(4):
                    chunk(n + j)
                pe.wait_ge(sem("cond_ready"), 2)
                if step:
                    pe.wait_ge(sem("ada_mod"), step)
                for k in range(KT):
                    for j in range(4):
                        mm = pe.matmul(ps[32 * j:32 * j + 32, 7, :], cond[:, k, :], slot(n + j)[:, 512 * k:512 * k + 512],
                                       start=k == 0, stop=k == KT - 1)
                        if k == 0 and j == 0:
                            release(mm)
                        if k == KT - 1:
                            mm.then_inc(weights_used, 1)
                pe.wait_ge(sem("ada_rows"), step + 1)
                for b in range(4):
                    mm = pe.transpose(ps[:, 7, P * b:P * b + P], ada_rows[:, P * b:P * b + P], ident)
                mm.then_inc(sem("ada_turned"), 1)

            def projection(l):
                base = chunk_at["w_in", l]
                jobs = proj_jobs(l)
                seen, ordinal = {"act": 0, "dve": 0}, []
                for j, (c, t, lo, width, engine) in enumerate(jobs):
                    seen[engine] += 1
                    ordinal.append(seen[engine])
                    if j == 0 or jobs[j - 1][0] != c:
                        chunk(base + c)
                    if j >= 6:
                        pe.wait_ge(sem(f"proj_read_{jobs[j - 6][4]}"), ordinal[j - 6] + before(f"proj_read_{jobs[j - 6][4]}", l))
                    w = slot(base + c)
                    tokens = 2 * N if l == 0 else N
                    for k in range(KT):
                        start, stop = k == 0, k == KT - 1
                        if c == 4:
                            mm = pe.matmul(ps[:, j % 6, 0:tokens], w[:, GROUP * k + P * t:GROUP * k + P * t + P],
                                           h_buf[:, k, 0:tokens], start=start, stop=stop)
                        elif c == 3:
                            both = w.rearrange("p (h k n) -> p k h n", h=2, k=KT)[:, k, :, :]
                            mm = pe.matmul(ps[:, j % 6, :].rearrange("p (h n) -> p h n", h=2),
                                           h_buf[:, k, P * t:P * t + P], both, start=start, stop=stop)
                        else:
                            mm = pe.matmul(ps[:, j % 6, 0:width], h_buf[:, k, P * t:P * t + P],
                                           w[:, 512 * k + lo:512 * k + lo + width], start=start, stop=stop)
                        if k == 0:
                            release(mm)
                    mm.then_inc(sem("proj_done"), 1)
                    if j == len(jobs) - 1 or jobs[j + 1][0] != c:
                        owed[0] += 1

            def fourier_channels(l):
                pe.wait_ge(sem("att_loaded"), 16 * 2 + before("att_loaded", l))
                tiles = 4 if l == 0 else 2
                pe.wait_ge(sem("qk_t_act"), 2 + before("qk_t_act", l))
                pe.wait_ge(sem("qk_t_dve"), 2 + before("qk_t_dve", l))
                cs = att[:, columns(ATT, "cs_d")]
                for t in range(tiles):
                    for c in range(SC):
                        mm = pe.matmul(ps[:, t, 2 * P * c:2 * P * c + 2 * P], fourier_in[:, c, P * t:P * t + P], cs,
                                       start=True, stop=True)
                    mm.then_inc(sem("fourier_uv"), 1)

            def fourier_tokens(l):
                cos_n = att[:, columns(ATT, "cos_n")].rearrange("p (a n) -> p a n", a=2)
                sin_n = att[:, columns(ATT, "sin_n")].rearrange("p (a n) -> p a n", a=2)
                for s in range(2 if l == 0 else 1):
                    if s == 0:
                        pe.wait_ge(sem("sgu_done"), 1 + before("sgu_done", l))
                    for nt in range(2):
                        pe.wait_ge(sem("uv_ready"), 2 * s + 2 + before("uv_ready", l))
                        step = 0
                        for a in range(2):
                            for w, table in enumerate((cos_n, sin_n)):
                                mm = pe.matmul(ps[:, 4 + s, N * nt:N * nt + N], table[:, a, P * nt:P * nt + P],
                                               uv[:, 2 * s + a, :, w, :], start=step == 0, stop=step == 3)
                                step += 1
                        mm.then_inc(sem("fourier_done"), 1)

            def spatial_gating(l):
                tiles = 4 if l == 0 else 2
                pe.wait_ge(sem("v_normed"), 1 + before("v_normed", l))
                pe.wait_ge(sem("rows_loaded"), 32 + before("rows_loaded", l))
                for h in range(HEADS):
                    v = gated[:, 0:tiles, GROUP + HEAD * h:GROUP + HEAD * h + HEAD]
                    out = ps[:, 4 + h // 2, N * (h % 2):N * (h % 2) + HEAD * tiles]
                    mm = pe.matmul(out.rearrange("p (t c) -> p t c", t=tiles), sgu_t[:, h, :], v, start=True, stop=True)
                mm.then_inc(sem("sgu_mixed"), 1)

            def turn_qk(l, which):
                src = (qk_c, qk_d)[which]
                if which == 0:
                    for engine in ("act", "dve"):
                        pe.wait_ge(sem(f"proj_read_{engine}"), sum(j[4] == engine for j in proj_jobs(l)) + before(f"proj_read_{engine}", l))
                pe.wait_ge(sem("qk_ready"), which + 1 + before("qk_ready", l))
                for b in range(4):
                    for t in range(4 if l == 0 or b >= 2 else 2):
                        mm = pe.transpose(ps[:, b, P * t:P * t + P], src[:, t, P * b:P * b + P], ident)
                        if t == 0:
                            release(mm)
                    mm.then_inc(sem("qk_turned"), 1)

            def attention_c(l):
                todo = units(l)
                pe.wait_ge(sem("qk_t_act"), 2 + before("qk_t_act", l))
                pe.wait_ge(sem("qk_t_dve"), 2 + before("qk_t_dve", l))

                def scores(u):
                    q, h = todo[u]
                    lo, width = keys(q)
                    if u >= 2:
                        pe.wait_ge(sem("c_exp"), 2 * (u - 1) + before("c_exp", l))
                    for m in range(2):
                        g = 2 * h + m
                        rows_ = slice(32 * (g % 4), 32 * (g % 4) + 32)
                        pe.matmul(ps[:, 2 * (u % 2) + m, 0:width], qk_t[rows_, g // 4, P * q:P * q + P],
                                  qk_t[rows_, 2 + g // 4, lo:lo + width], start=True, stop=True)\
                            .then_inc(sem("c_scores"), 1)

                scores(0)
                for u, (q, h) in enumerate(todo):
                    if u + 1 < len(todo):
                        scores(u + 1)
                    lo, width = keys(q)
                    tiles = width // P
                    pe.wait_ge(sem("c_weights"), u + 1 + before("c_weights", l))
                    if u >= 2:
                        pe.wait_ge(sem("c_wt"), u - 1 + before("c_wt", l))
                    for j in range(tiles):
                        mm = pe.transpose(ps[:, 4 + u % 2, P * j:P * j + P], expo[:, 2 * (u % 2), P * j:P * j + P], ident)
                    mm.then_inc(sem("c_turned"), 1)
                    pe.wait_ge(sem("c_wt"), u + 1 + before("c_wt", l))
                    if h == 0 and q >= 1:
                        pe.wait_ge(sem("c_out"), q + before("c_out", l))
                    at = HEAD * h
                    for j in range(tiles):
                        mm = pe.matmul(ps[:, 6, at:at + HEAD], w_t[:, u % 2, j, :],
                                       vals[:, lo // P + j, HEAD * h:HEAD * h + HEAD], start=j == 0, stop=j == tiles - 1)
                    mm.then_inc(sem("c_pv"), 1)

            def attention_d(l):
                todo = units(l)
                pe.wait_ge(sem("qk_t_act"), 4 + before("qk_t_act", l))
                pe.wait_ge(sem("qk_t_dve"), 4 + before("qk_t_dve", l))
                mask = att[:, columns(ATT, "mask")]

                def scores(u):
                    q, h = todo[u]
                    lo, width = keys(q)
                    if u >= 3:
                        pe.wait_ge(sem("d_exp"), u - 2 + before("d_exp", l))
                    rows_ = slice(64 * (h % 2), 64 * (h % 2) + 64)
                    mm = pe.matmul(ps[:, u % 3, 0:width], qk_t[rows_, h // 2, P * q:P * q + P],
                                   qk_t[rows_, 2 + h // 2, lo:lo + width], start=True, stop=q >= 2)
                    if q < 2:
                        pe.matmul(ps[:, u % 3, 0:N], ident, rel_bias[:, q, h, :], start=False, stop=False)
                        mm = pe.matmul(ps[:, u % 3, 0:N], ident, mask, start=False, stop=True)
                    mm.then_inc(sem("d_scores"), 1)

                scores(0)
                scores(1)
                for u, (q, h) in enumerate(todo):
                    if u + 2 < len(todo):
                        scores(u + 2)
                    lo, width = keys(q)
                    tiles = width // P
                    pe.wait_ge(sem("d_exp"), u + 1 + before("d_exp", l))
                    if u >= 2:
                        pe.wait_ge(sem("d_wt"), u - 1 + before("d_wt", l))
                    for j in range(tiles):
                        mm = pe.transpose(ps[:, 4 + u % 2, P * j:P * j + P], expo[:, u % 4, P * j:P * j + P], ident)
                    mm.then_inc(sem("d_turned"), 1)
                    pe.wait_ge(sem("d_wt"), u + 1 + before("d_wt", l))
                    if u >= 2:
                        pe.wait_ge(sem("d_out"), u - 1 + before("d_out", l))
                    for j in range(tiles):
                        mm = pe.matmul(ps[:, (6, 3)[u % 2], 0:HEAD], w_t[:, u % 2, j, :],
                                       vals[:, lo // P + j, GROUP + HEAD * h:GROUP + HEAD * h + HEAD],
                                       start=j == 0, stop=j == tiles - 1)
                    mm.then_inc(sem("d_pv"), 1)

            def merge(l):
                tiles = 4 if l == 0 else 2
                width = P * tiles
                pe.wait_ge(sem("y_normed"), 1 + before("y_normed", l))
                for k in range(KT):
                    if k >= 6:
                        pe.wait_ge(sem("y_t"), k - 5 + before("y_t", l))
                    for t in range(tiles):
                        mm = pe.transpose(ps[:, k % 6, P * t:P * t + P], ycat[:, t, P * k:P * k + P], ident)
                    mm.then_inc(sem("y_turned"), 1)
                pe.wait_ge(sem("y_t"), KT + before("y_t", l))
                for d in range(KT):
                    n = chunk_at["w_out", l] + d // 4
                    if d % 4 == 0:
                        chunk(n)
                    if d >= 6:
                        pe.wait_ge(sem("mix_added"), d - 5 + before("mix_added", l))
                    for k in range(KT):
                        at = 512 * k + P * (d % 4)
                        mm = pe.matmul(ps[:, d % 6, 0:width], slot(n)[:, at:at + P], h_buf[:, k, 0:width],
                                       start=k == 0, stop=k == KT - 1)
                        if k == 0:
                            release(mm)
                    mm.then_inc(sem("mix_out"), 1)
                    if d % 4 == 3:
                        owed[0] += 1

            def route(l):
                tiles = 4 if l == 0 else 2
                streams = tiles // 2
                rows_ = 48 if l == 0 else 16
                for t in range(tiles):
                    for k in range(KT):
                        mm = pe.matmul(ps[:, 0, EXPERTS * t:EXPERTS * t + EXPERTS], h_buf[:, k, P * t:P * t + P],
                                       router_sb[:, l, k, :], start=k == 0, stop=k == KT - 1)
                mm.then_inc(sem("logits"), 1)
                for j in range(2 * tiles):
                    t, half = divmod(j, 2)
                    if j >= 4:
                        pe.wait_ge(sem(f"h_tok_{('act', 'dve')[j % 2]}"), (j - 4) // 2 + 1 + before(f"h_tok_{('act', 'dve')[j % 2]}", l))
                    for k in range(4):
                        mm = pe.transpose(ps[:, 1 + j % 4, P * k:P * k + P], h_buf[:, 4 * half + k, P * t:P * t + P], ident)
                    mm.then_inc(sem("h_turned"), 1)
                pe.wait_ge(sem("aff"), 1 + before("aff", l))
                for t in range(tiles):
                    mm = pe.transpose(ps[0:EXPERTS, 0, P * t:P * t + P], logit[:, EXPERTS * t:EXPERTS * t + EXPERTS], ident)
                mm.then_inc(sem("aff_turned"), 1)
                pe.wait_ge(sem("slots"), 1 + before("slots", l))
                for a in range(2):
                    mm = pe.transpose(ps[:, 0, 48 * a:48 * a + rows_], slot_id[0:rows_, P * a:P * a + P],
                                      ident[0:rows_, 0:rows_])
                mm.then_inc(sem("slots_turned"), 1)
                pe.wait_ge(sem("expand_loaded"), 16 + before("expand_loaded", l))
                pe.wait_ge(sem("h_tok_act"), tiles + before("h_tok_act", l))
                pe.wait_ge(sem("h_tok_dve"), tiles + before("h_tok_dve", l))
                for s in range(streams):
                    if s:
                        pe.wait_ge(sem("scatter_ready"), 2 * s + before("scatter_ready", l))
                    experts = slice(32 * s, 32 * s + EXPERTS)
                    for src, bank, spread in ((aff_t, 1, "aff_spread"), (slot_id, 3, "slots_spread")):
                        for g in range(4):
                            mm = pe.matmul(ps[:, bank + g // 2, N * (g % 2):N * (g % 2) + N],
                                           expand[experts, P * g:P * g + P], src[experts, :], start=True, stop=True)
                        mm.then_inc(sem(spread), 1)
                pe.wait_ge(sem("gather_ready"), 1 + before("gather_ready", l))
                pe.wait_ge(sem("scatter_ready"), 2 * streams + before("scatter_ready", l))
                for j in range(KT * streams):
                    s, k = divmod(j, KT)
                    if j >= 6:
                        pe.wait_ge(sem(f"picked_{('act', 'dve')[j % 2]}"), (j - 6) // 2 + 1 + before(f"picked_{('act', 'dve')[j % 2]}", l))
                    for a in range(2):
                        mm = pe.matmul(ps[:, j % 6, :], h_tok[:, 2 * s + a, P * k:P * k + P],
                                       gather[:, 2 * s + a, :, :].rearrange("p e s -> p (e s)"),
                                       start=a == 0, stop=a == 1)
                    mm.then_inc(sem("gathered"), 1)

            def experts(l):
                m = 2 * CAP if l == 0 else CAP
                n = chunk_at["experts", l]
                pe.wait_ge(sem("picked_act"), KT // 2 * (m // CAP) + before("picked_act", l))
                pe.wait_ge(sem("picked_dve"), KT // 2 * (m // CAP) + before("picked_dve", l))
                hid_t = hid_exp_t[:, 0:8 * m].rearrange("p (j h m) -> p j h m", j=4, h=2)
                with pe.Fori(0, EXPERTS // 4) as it:
                    for j in range(4):
                        xe = x_exp[:, 512 * (j % 2):512 * (j % 2) + KT * m].rearrange("p (k m) -> p k m", k=KT)
                        pe.wait_ge(sem("x_exp"), it * 4 + (j + 1) + before("x_exp", l))
                        for which in range(2):
                            for k in range(KT):
                                c = 6 * j + 2 * which + k // 4
                                if k % 4 == 0:
                                    pe.wait_ge(slot_loaded[(n + c) % SLOTS], it * 64 + (loaded_value(n + c)))
                                for half in range(2):
                                    mm = pe.matmul(ps[half * m:half * m + m, which, :], xe[:, k, :],
                                                   slot(n + c)[:, D * (k % 4) + 512 * half:D * (k % 4) + 512 * half + 512],
                                                   start=k == 0, stop=k == KT - 1)
                                if k % 4 == 3:
                                    mm.then_inc(weights_used, 1)
                        pe.wait_ge(sem("exp_hid"), it * 4 + (j + 1) + before("exp_hid", l))
                        for b in range(4):
                            mm = pe.transpose(ps[:, 2, P * b:P * b + P], hid_exp[:, P * b:P * b + P], ident)
                        mm.then_inc(sem("exp_turned"), 1)
                        pe.wait_ge(sem("exp_hid_t"), it * 4 + (j + 1) + before("exp_hid_t", l))
                        for k in range(KT):
                            c = 6 * j + 4 + k // 4
                            if k % 4 == 0:
                                pe.wait_ge(slot_loaded[(n + c) % SLOTS], it * 64 + (loaded_value(n + c)))
                            for half in range(2):
                                mm = pe.matmul(ps[half * m:half * m + m, 3, :], hid_t[:, k % 4, k // 4, :],
                                               slot(n + c)[:, D * (k % 4) + 512 * half:D * (k % 4) + 512 * half + 512],
                                               start=k == 0, stop=k == KT - 1)
                            if k % 4 == 3:
                                mm.then_inc(weights_used, 1)

            def scatter_back(l):
                streams = 2 if l == 0 else 1
                pe.wait_ge(sem("o_act"), EXPERTS + before("o_act", l))
                pe.wait_ge(sem("o_dve"), EXPERTS + before("o_dve", l))
                for d in range(KT):
                    if d >= 4:
                        pe.wait_ge(sem("moe_added"), d - 3 + before("moe_added", l))
                    for s in range(streams):
                        for g in range(4):
                            o = (o_lat, o_ctx)[s]
                            mm = pe.matmul(ps[:, 4 + d % 4, N * s:N * s + N], o[:, g, P * d:P * d + P],
                                           scatter[:, s, g, :], start=g == 0, stop=g == 3)
                    mm.then_inc(sem("moe_out"), 1)

            def ffn_group(i, first, it, step, tiles):
                n = first
                per = 8 * it if it is not None else 0

                def landed(c):
                    v = loaded_value(c)
                    pe.wait_ge(slot_loaded[c % SLOTS], it * 16 + v if it is not None else v)

                width = P * tiles
                for f in range(tiles):
                    if f == 0:
                        landed(n)
                        landed(n + 1)
                    for which in range(2):
                        for k in range(KT):
                            mm = pe.matmul(ps[:, f, N * which:N * which + N],
                                           slot(n + which)[:, width * k + P * f:width * k + P * f + P],
                                           h_buf[:, k, 0:N], start=k == 0, stop=k == KT - 1)
                        if f == tiles - 1 and which == 0:
                            mm.then_inc(weights_used, 1)
                    mm.then_inc(sem("ffn_gate_up"), 1)
                landed(n + 2)
                for f in range(tiles):
                    pe.wait_ge(sem("ffn_hid"), per + (FT * i + step + f + 1))
                    for d in range(KT):
                        mm = pe.matmul(ps[:, 4 + d // 2, N * (d % 2):N * (d % 2) + N],
                                       slot(n + 2)[:, D * f + P * d:D * f + P * d + P], hid_f[:, f, :],
                                       start=False, stop=False, skip_group_check=True)
                        if f == 0 and d == 0:
                            mm.then_inc(weights_used, 1)
                mm.then_inc(weights_used, 1)

            def open_sums():
                for b in range(4, 8):
                    release(pe.matmul(ps[:, b, :], zeros[:, 0:P], zeros[:, :], start=True, stop=False, skip_group_check=True))

            def ffn(i):
                n = chunk_at["ffn", i]
                open_sums()
                with pe.Fori(0, FT // 8) as it:
                    ffn_group(i, n, it, 0, 4)
                    ffn_group(i, n + 3, it, 4, 4)
                at = FT // 8 * 8
                ffn_group(i, n + 3 * at // 4, None, at, 4)
                ffn_group(i, n + 3 * at // 4 + 3, None, at + 4, 2)

            def lru():
                n = chunk_at["lru", 0]
                for o in range(2 * RT):
                    c = n + o // 4
                    if o % 4 == 0:
                        chunk(c)
                    if o >= 8:
                        pe.wait_ge(sem("lru_read_act" if o - 8 < RT else "lru_read_dve"), (o - 8) % RT + 1)
                    for k in range(KT):
                        at = 512 * k + P * (o % 4)
                        mm = pe.matmul(ps[:, o % 8, 0:N], slot(c)[:, at:at + P], h_buf[:, k, 0:N],
                                       start=k == 0, stop=k == KT - 1)
                        if k == 0:
                            release(mm)
                    mm.then_inc(sem("lru_in"), 1)
                    if o % 4 == 3:
                        owed[0] += 1
                chunk(n + 5)
                chunk(n + 6)
                pe.wait_ge(sem("lru_read_dve"), RT)
                pe.wait_ge(sem("lru_conv"), RT)
                for o in range(RT):
                    if o >= 4:
                        pe.wait_ge(sem("lru_gates"), 2 * (o - 3))
                    for which in range(2):
                        mine = [i for i, (a, _) in enumerate(PAIRS) if a == o]
                        for i in mine:
                            mm = pe.matmul(ps[:, o % 4, N * which:N * which + N], slot(n + 5 + which)[:, P * i:P * i + P],
                                           l_x[:, PAIRS[i][1], :], start=i == mine[0], stop=i == mine[-1])
                            if i == mine[0]:
                                release(mm)
                    mm.then_inc(sem("lru_gate_in"), 1)
                owed[0] += 2
                open_sums()
                for k in range(RT):
                    c = n + 7 + k // 4
                    if k % 4 == 0:
                        chunk(c)
                    pe.wait_ge(sem("lru_y"), 1)
                    for d in range(KT):
                        at = D * (k % 4) + P * d
                        mm = pe.matmul(ps[:, 4 + d // 2, N * (d % 2):N * (d % 2) + N], slot(c)[:, at:at + P],
                                       l_gate[:, k, :], start=False, stop=False, skip_group_check=True)
                    if k % 4 == 3 or k == RT - 1:
                        mm.then_inc(weights_used, 1)

            def pooling():
                n = chunk_at["pool", 0]
                chunk(n)
                pe.wait_ge(sem("pool_ready"), 1)
                for d in range(KT):
                    g, half = divmod(d, 2)
                    for k in range(2):
                        at = GROUP * (2 * g + k) + P * half
                        mm = pe.matmul(ps[:, 4 + d // 2, N * half:N * half + N], slot(n)[:, at:at + P],
                                       pool_u[:, 2 * g + k, :], start=k == 0, stop=k == 1)
                    if half:
                        mm.then_inc(sem("pool_mapped"), 1)
                owed[0] += 1

            def ple(l):
                n = chunk_at["ple", l]
                chunk(n)
                for d in range(KT):
                    c = n + 1 + d // 4
                    if d % 4 == 0:
                        chunk(c)
                    if d >= 6:
                        pe.wait_ge(sem("ple_added"), KT * l + d - 5)
                    for k in range(KT):
                        at = 512 * k + P * (d % 4)
                        pe.matmul(ps[:, 1 + d % 6, 0:N], slot(c)[:, at:at + P], h_buf[:, k, 0:N],
                                  start=k == 0, stop=k == KT - 1)
                    for k in range(2):
                        mm = pe.matmul(ps[:, 1 + d % 6, N:2 * N], slot(n)[:, D * k + P * d:D * k + P * d + P],
                                       slot(n)[:, 2 * D + N * k:2 * D + N * k + N], start=k == 0, stop=k == 1)
                    mm.then_inc(sem("ple_products"), 1)
                owed[0] += 3

            pe.wait_ge(sem("setup_loaded"), 16 * 5)
            pe.wait_ge(sem("memsets"), 1)
            for i in range(3):
                ada_group(0, i)
            for l in range(LAYERS):
                norm_pe(pe, release, 2 * l)
                norm_ready(pe, 2 * l)
                projection(l)
                if l == 0:
                    ada_group(1, 0)
                turn_qk(l, 0)
                spatial_gating(l)
                fourier_channels(l)
                fourier_tokens(l)
                if l == 0:
                    ada_group(1, 1)
                pe.wait_ge(sem("fourier_read"), (2 if l == 0 else 1) + before("fourier_read", l))
                attention_c(l)
                pe.wait_ge(sem("c_exp"), 2 * len(units(l)) + before("c_exp", l))
                turn_qk(l, 1)
                if l == 0:
                    ada_group(1, 2)
                pe.wait_ge(sem("c_out"), (4 if l == 0 else 2) + before("c_out", l))
                attention_d(l)
                merge(l)
                norm_pe(pe, release, 2 * l + 1)
                norm_ready(pe, 2 * l + 1)
                route(l)
                experts(l)
                scatter_back(l)
            for l in range(LAYERS):
                i = 4 + 4 * l
                norm_pe(pe, release, i)
                norm_ready(pe, i)
                ffn(2 * l)
                norm_pe(pe, release, i + 1)
                norm_ready(pe, i + 1)
                if l == 0:
                    lru()
                else:
                    pooling()
                norm_pe(pe, release, i + 2)
                norm_ready(pe, i + 2)
                ffn(2 * l + 1)
                norm_pe(pe, release, i + 3)
                norm_ready(pe, i + 3)
                ple(l)
            norm_pe(pe, release, 12)

        @block.scalar
        def _(act):
            count = [0]

            def link(ins):
                count[0] += 1
                ins.then_inc(sem("act_chain"), 1)
                act.wait_ge(sem("act_chain"), count[0])

            def ada_group(step):
                act.wait_ge(weights_used, ADA_USED(step))
                act.activation(ada_rows, ps[:, 7, :], ACT.Copy).then_inc(sem("ada_rows"), 1)

            def ADA_USED(step):
                l, i = divmod(step, 3)
                return chunk_at["ada", l] + 4 * i + 4

            def projection(l):
                for j, (c, t, lo, width, engine) in enumerate(proj_jobs(l)):
                    if engine != "act":
                        continue
                    act.wait_ge(sem("proj_done"), j + 1 + before("proj_done", l))
                    if c == 0:
                        ins = act.activation(gated[:, t, :], ps[:, j % 6, :], ACT.Gelu_apprx_tanh)
                    elif c == 2:
                        ins = act.activation(qk_d[:, t, lo:lo + width], ps[:, j % 6, 0:width], ACT.Copy)
                    else:
                        tokens = 2 * N if l == 0 else N
                        ins = act.activation(fourier_in[:, t, 0:tokens], ps[:, j % 6, 0:tokens], ACT.Copy)
                    ins.then_inc(sem("proj_read_act"), 1)

            def qk_stats(l):
                tiles = 4 if l == 0 else 2
                acts = sum(j[4] == "act" for j in proj_jobs(l))
                act.wait_ge(sem("proj_read_act"), acts + before("proj_read_act", l))
                act.activation(sq_v[:, 0:GROUP * tiles].rearrange("p (t f) -> p t f", t=tiles),
                               gated[:, 0:tiles, GROUP:2 * GROUP], ACT.Square).then_inc(sem("mix_squares"), 1)
                act.activation(sq_d, qk_d.rearrange("p t f -> p (t f)"), ACT.Square).then_inc(sem("mix_squares"), 1)
                act.wait_ge(sem("proj_read_dve"), 4 + before("proj_read_dve", l))
                act.activation(sq_c, qk_c.rearrange("p t f -> p (t f)"), ACT.Square).then_inc(sem("mix_squares"), 1)
                act.wait_ge(sem("mix_sums"), 3 + before("mix_sums", l))
                act.activation(mix_ss[:, 0:64], mix_ss[:, 0:64], ACT.Sqrt, bias=eps_col[:, 0:1], scale=1.0 / DIFF)\
                    .then_inc(sem("mix_std"), 1)
                act.activation(mix_ss[:, 64:112], mix_ss[:, 64:112], ACT.Sqrt, bias=eps_col[:, 0:1], scale=1.0 / HEAD)\
                    .then_inc(sem("mix_std"), 1)

            def swap_partners(l):
                act.wait_ge(sem("c_normed"), 1 + before("c_normed", l))
                src = qk_c.rearrange("p t f -> p (t f)").rearrange("p (g w e) -> p g w e", w=2, e=8)
                dst = swapped.rearrange("p (g w e) -> p g w e", w=2, e=8)
                for w in range(2):
                    act.activation(dst[:, :, w, :], src[:, :, 1 - w, :], ACT.Copy).then_inc(sem("c_swapped"), 1)

            def read_fourier_uv(l):
                for t in range(4 if l == 0 else 2):
                    act.wait_ge(sem("fourier_uv"), t + 1 + before("fourier_uv", l))
                    if t == 0:
                        act.wait_ge(sem("sgu_done"), 1 + before("sgu_done", l))
                    act.activation(uv_flat[:, t, :], ps[:, t, :], ACT.Copy).then_inc(sem("uv_ready"), 1)

            uv_flat = part(4096, 6144).rearrange("p (t f) -> p t f", t=4)

            def read_qk_t(l, which):
                for b in (0, 2):
                    act.wait_ge(sem("qk_turned"), 4 * which + b + 1 + before("qk_turned", l))
                    width = 512 if l == 0 or b >= 2 else N
                    act.activation(qk_t[:, b, 0:width], ps[:, b, 0:width], ACT.Copy).then_inc(sem("qk_t_act"), 1)

            def attention_c(l):
                for u, (q, h) in enumerate(units(l)):
                    width = keys(q)[1]
                    for m in range(2):
                        i = 2 * u + m
                        act.wait_ge(sem("c_max"), i + 1 + before("c_max", l))
                        if u >= 2 and m == 0:
                            act.wait_ge(sem("c_turned"), u - 1 + before("c_turned", l))
                        if u == 0 and m == 0:
                            act.wait_ge(sem("qk_turned"), 4 + before("qk_turned", l))
                        act.activation(expo[:, 2 * (u % 2) + m, 0:width], ps[:, 2 * (u % 2) + m, 0:width], ACT.Exp,
                                       bias=c_max[:, i:i + 1], accum_out=c_den[:, i:i + 1]).then_inc(sem("c_exp"), 1)
                    act.wait_ge(sem("c_turned"), u + 1 + before("c_turned", l))
                    if u >= 2:
                        act.wait_ge(sem("c_pv"), u - 1 + before("c_pv", l))
                    act.activation(w_t[:, u % 2, 0:width // P, :].rearrange("p k f -> p (k f)"), ps[:, 4 + u % 2, 0:width],
                                   ACT.Copy).then_inc(sem("c_wt"), 1)

            def attention_d(l):
                todo = units(l)

                def softmax(u):
                    width = keys(todo[u][0])[1]
                    act.wait_ge(sem("d_max"), u + 1 + before("d_max", l))
                    if u >= 4:
                        act.wait_ge(sem("d_turned"), u - 3 + before("d_turned", l))
                    act.activation(expo[:, u % 4, 0:width], ps[:, u % 3, 0:width], ACT.Exp, bias=d_max[:, u:u + 1],
                                   accum_out=d_den[:, u:u + 1]).then_inc(sem("d_exp"), 1)

                softmax(0)
                for u in range(len(todo)):
                    if u + 1 < len(todo):
                        softmax(u + 1)
                    width = keys(todo[u][0])[1]
                    act.wait_ge(sem("d_turned"), u + 1 + before("d_turned", l))
                    if u >= 2:
                        act.wait_ge(sem("d_pv"), u - 1 + before("d_pv", l))
                    act.activation(w_t[:, u % 2, 0:width // P, :].rearrange("p k f -> p (k f)"), ps[:, 4 + u % 2, 0:width],
                                   ACT.Copy).then_inc(sem("d_wt"), 1)

            def merge(l):
                tiles = 4 if l == 0 else 2
                act.wait_ge(sem("sgu_done"), 1 + before("sgu_done", l))
                act.wait_ge(sem("fourier_read"), (2 if l == 0 else 1) + before("fourier_read", l))
                act.wait_ge(sem("c_out"), (4 if l == 0 else 2) + before("c_out", l))
                act.wait_ge(sem("d_out"), len(units(l)) + before("d_out", l))
                act.wait_ge(sem("d_pv"), len(units(l)) + before("d_pv", l))
                act.activation(y_sq[:, 0:D * tiles], ycat[:, 0:tiles, :].rearrange("p t f -> p (t f)"), ACT.Square)\
                    .then_inc(sem("y_squares"), 1)
                act.wait_ge(sem("y_sums"), 1 + before("y_sums", l))
                act.activation(y_ss[:, 0:16 * tiles], y_ss[:, 0:16 * tiles], ACT.Sqrt, bias=eps_col[:, 0:1],
                               scale=1.0 / HEAD).then_inc(sem("y_std"), 1)
                for k in range(KT):
                    act.wait_ge(sem("y_turned"), k + 1 + before("y_turned", l))
                    act.activation(h_buf[:, k, 0:P * tiles], ps[:, k % 6, 0:P * tiles], ACT.Copy,
                                   scale=head_gain(l)[:, k:k + 1]).then_inc(sem("y_t"), 1)

            def head_gain(l):
                return vec1[:, l, columns(VEC1, "head_out_g")]

            def route(l):
                tiles = 4 if l == 0 else 2
                for j in range(0, 2 * tiles, 2):
                    act.wait_ge(sem("h_turned"), j + 1 + before("h_turned", l))
                    act.activation(h_tok[:, j // 2, 0:512], ps[:, 1 + j % 4, :], ACT.Copy).then_inc(sem("h_tok_act"), 1)
                act.wait_ge(sem("logits_shifted"), 1 + before("logits_shifted", l))
                act.activation(logit[:, 0:EXPERTS * tiles], logit[:, 0:EXPERTS * tiles], ACT.Exp)\
                    .then_inc(sem("logits_exp"), 1)
                for s in range(tiles // 2):
                    act.wait_ge(sem("aff_spread"), s + 1 + before("aff_spread", l))
                    if s:
                        act.wait_ge(sem("scatter_ready"), 2 * s + before("scatter_ready", l))
                    act.activation(aff_bc.rearrange("p (b f) -> p b f", b=2), ps[:, 1:3, :], ACT.Copy)\
                        .then_inc(sem("aff_bc"), 1)
                for j in range(0, KT * tiles // 2, 2):
                    s, k = divmod(j, KT)
                    act.wait_ge(sem("gathered"), j + 1 + before("gathered", l))
                    act.activation(picked_of(l)[:, k, :, CAP * s:CAP * s + CAP],
                                   ps[:, j % 6, :].rearrange("p (e s) -> p e s", e=EXPERTS), ACT.Copy)\
                        .then_inc(sem("picked_act"), 1)

            def experts(l):
                m = 2 * CAP if l == 0 else CAP
                first = chunk_at["experts", l]
                with act.Fori(0, EXPERTS // 4) as it:
                    for j in range(4):
                        act.wait_ge(weights_used, it * 24 + (first + 6 * j + 2))
                        act.activation(hid_exp[0:2 * m, :], ps[0:2 * m, 0, :], ACT.Silu).then_inc(sem("exp_silu"), 1)
                        act.wait_ge(sem("exp_turned"), it * 4 + (j + 1) + before("exp_turned", l))
                        turned = ps[:, 2, :].rearrange("p (b m) -> p b m", b=4)[:, :, 0:2 * m]
                        act.activation(hid_exp_t[:, 0:8 * m].rearrange("p (b m) -> p b m", b=4), turned, ACT.Copy).then_inc(sem("exp_hid_t"), 1)
                        act.wait_ge(weights_used, it * 24 + (first + 6 * j + 6))
                        for s in range(m // CAP):
                            o = (o_lat, o_ctx)[s]
                            ins = act.activation(o[32 * j:32 * j + 32, it, 0:512], ps[32 * s:32 * s + 32, 3, :], ACT.Copy)
                        ins.then_inc(sem("o_act"), 1)

            def ffn(i):
                def one(f, n, it):
                    act.wait_ge(sem("ffn_gate_up"), it * 8 + (n + 1) if it is not None else n + 1)
                    act.activation(silu_f[:, f, :], ps[:, f, 0:N], ACT.Silu).then_inc(sem("ffn_silu"), 1)

                with act.Fori(0, FT // 8) as it:
                    for f in range(8):
                        one(f % 4, FT * i + f, it)
                for f in range(FT // 8 * 8, FT):
                    one(f % 4, FT * i + f, None)

            def lru():
                v = lambda name: vec2[:, columns(VEC2, name)]
                for o in range(RT):
                    act.wait_ge(sem("lru_in"), o + 1)
                    act.activation(l_gate[:, o, :], ps[:, o % 8, 0:N], ACT.Gelu_apprx_tanh).then_inc(sem("lru_read_act"), 1)
                for o in range(RT):
                    act.wait_ge(sem("lru_gate_in"), o + 1)
                    act.activation(l_r[:, o, :], ps[:, o % 4, 0:N], ACT.Sigmoid, bias=v("b_a")[:, o:o + 1])\
                        .then_inc(sem("lru_gates"), 1)
                    act.activation(l_i[:, o, :], ps[:, o % 4, N:2 * N], ACT.Sigmoid, bias=v("b_x")[:, o:o + 1])\
                        .then_inc(sem("lru_gates"), 1)
                act.wait_ge(sem("lru_abs"), 1)
                act.activation(lru_s[1][:, :], lru_s[0][:, :], ACT.Exp, scale=-1.0).then_inc(sem("lru_exp"), 1)
                act.wait_ge(sem("lru_gates"), 2 * RT)
                act.wait_ge(sem("lru_rate"), 1)
                for o in range(RT):
                    act.activation(l_a[:, o, :], l_r[:, o, :], ACT.Exp, scale=lru_s[5][:, o:o + 1])
                    act.activation(l_r[:, o, :], l_r[:, o, :], ACT.Tanh, scale=lru_s[4][:, o:o + 1])\
                        .then_inc(sem("lru_decay"), 1)
                act.wait_ge(sem("lru_square"), 1)
                act.activation(l_r.rearrange("p o t -> p (o t)"), l_r.rearrange("p o t -> p (o t)"), ACT.Sqrt, scale=2.0)\
                    .then_inc(sem("lru_mult"), 1)

            def ple(l):
                for d in range(KT):
                    act.wait_ge(sem("ple_products"), KT * l + d + 1)
                    if d >= 4:
                        act.wait_ge(sem("ple_added"), KT * l + d - 3)
                    act.activation(silu_f[:, d % 4, :], ps[:, 1 + d % 6, 0:N], ACT.Sigmoid).then_inc(sem("ple_gate"), 1)

            act.wait_ge(sem("setup_loaded"), 16 * 5)
            act.wait_ge(sem("cond_ready"), 1)
            act.activation(cond[:, :, 0:2], cond_in[:, :, :], ACT.Silu).then_inc(sem("cond_ready"), 1)
            act.wait_ge(sem("memsets"), 1)
            for i in range(3):
                ada_group(i)
            act.wait_ge(sem("x_loaded"), 32)
            for l in range(LAYERS):
                if l:
                    act.wait_ge(sem("moe_added"), KT + before("moe_added", l - 1))
                norm_act(act, 2 * l, rstd, mod[:, l, 0:KT, :])
                projection(l)
                act.wait_ge(sem("lam_sum"), l + 1)
                act.activation(lam_sum, lam_sum, ACT.Exp).then_inc(sem("lam_exp"), 1)
                qk_stats(l)
                if l == 0:
                    ada_group(3)
                swap_partners(l)
                read_qk_t(l, 0)
                read_fourier_uv(l)
                if l == 0:
                    ada_group(4)
                attention_c(l)
                read_qk_t(l, 1)
                if l == 0:
                    ada_group(5)
                attention_d(l)
                merge(l)
                act.wait_ge(sem("mix_added"), KT + before("mix_added", l))
                norm_act(act, 2 * l + 1, rstd, mod[:, l, 3 * KT:4 * KT, :])
                route(l)
                experts(l)
            act.wait_ge(sem("moe_added"), KT + before("moe_added", 1))
            for l in range(LAYERS):
                i = 4 + 4 * l
                if l:
                    act.wait_ge(sem("ple_added"), KT * l)
                norm_act(act, i, rstd2, None)
                ffn(2 * l)
                act.wait_ge(sem("ffn_added"), 4 * (2 * l + 1))
                norm_act(act, i + 1, rstd2, None)
                if l == 0:
                    lru()
                    act.wait_ge(sem("lru_added"), 4)
                else:
                    act.wait_ge(sem("pool_added"), KT)
                norm_act(act, i + 2, rstd2, None)
                ffn(2 * l + 1)
                act.wait_ge(sem("ffn_added"), 4 * (2 * l + 2))
                norm_act(act, i + 3, rstd2, None)
                ple(l)
            act.wait_ge(sem("ple_added"), KT * LAYERS)
            norm_act(act, 12, rstd2, None)

        @block.vector
        def _(dve):
            count = [0]

            def link(ins):
                count[0] += 1
                ins.then_inc(sem("dve_chain"), 1)
                dve.wait_ge(sem("dve_chain"), count[0])

            def bc(ap, n):
                return bass.AP(ap.tensor, ap.offset, [list(x) for x in ap.ap] + [[0, n]])

            def bc_mid(ap, n):
                a = [list(x) for x in ap.ap]
                return bass.AP(ap.tensor, ap.offset, a[:-1] + [[0, n]] + a[-1:])

            def ada_group(l, i):
                step = 3 * l + i
                dve.wait_ge(sem("ada_turned"), step + 1)
                turned = ps[:, 7, :].rearrange("p (b j s) -> p j b s", b=4, j=4)[:, :, :, 0:2]
                bias = vec1[:, l, 16 * i:16 * i + 16].rearrange("p (j b) -> p j b", b=4)
                dst = mod[:, l, 16 * i:16 * i + 16, :].rearrange("p (j b) s -> p j b s", b=4)
                for s in range(2):
                    ins = dve.tensor_tensor(dst[:, :, :, s], turned[:, :, :, s], bias, ALU.add)
                    if s == 0:
                        link(ins)
                ins.then_inc(sem("ada_mod"), 1)
                dve.wait_ge(sem("ada_mod"), step + 1)

            def gains(l):
                for dst, at, name in ((gain1, KT, "norm1_g"), (gain2, 4 * KT, "norm2_g")):
                    g = vec1[:, l, columns(VEC1, name)]
                    link(dve.scalar_tensor_tensor(dst[:, :, :], mod[:, l, at:at + KT, :], 1.0, bc(g, 2), ALU.add, ALU.mult))
                lam_init = 0.8 - 0.6 * math.exp(-0.3 * l)
                hg = vec1[:, l, columns(VEC1, "head_out_g")][:, 4:6]
                dve.tensor_scalar(hg, hg, 1.0 - lam_init, None, ALU.mult).then_inc(sem("head_gain"), 1)
                dve.wait_ge(sem("head_gain"), l + 1)

            def row_constants(l):
                lam_init = 0.8 - 0.6 * math.exp(-0.3 * l)
                dve.wait_ge(sem("rows_loaded"), 32 + before("rows_loaded", l))
                for dst, table, name in ((rope_cos, "cos", "c_gain"), (rope_sin, "sin", "c_gain_swapped")):
                    t = const[:, columns(CONST, table)].rearrange("p (t d) -> p t d", t=4)
                    g = rows[:, columns(ROWS, name)].rearrange("p (w d) -> p w d", w=2)
                    for w in range(2):
                        gain = bc_mid(g[:, w, :], 4)
                        link(dve.tensor_tensor(dst[:, :, w, :], t, gain, ALU.mult))
                lam = rows[:, columns(ROWS, "lambda")].rearrange("p (a b d) -> p a b d", a=2, b=2)
                link(dve.tensor_tensor(lam_tmp.rearrange("p (a d) -> p a d", a=2), lam[:, :, 0, :], lam[:, :, 1, :], ALU.mult))
                dve.tensor_reduce(lam_sum, lam_tmp.rearrange("p (a d) -> p a d", a=2), AX, ALU.add).then_inc(sem("lam_sum"), 1)

            def lam_value(l):
                lam_init = 0.8 - 0.6 * math.exp(-0.3 * l)
                dve.wait_ge(sem("lam_exp"), l + 1)
                link(dve.tensor_tensor(neg_lam, lam_sum[:, 1:2], lam_sum[:, 0:1], ALU.subtract))
                link(dve.tensor_scalar(neg_lam, neg_lam, -lam_init, None, ALU.add))

            def projection(l):
                for j, (c, t, lo, width, engine) in enumerate(proj_jobs(l)):
                    if engine != "dve":
                        continue
                    dve.wait_ge(sem("proj_done"), j + 1 + before("proj_done", l))
                    dst = qk_c[:, t, lo:lo + width] if c == 1 else vals[:, t, :]
                    dve.tensor_copy(dst, ps[:, j % 6, 0:width]).then_inc(sem("proj_read_dve"), 1)

            def qk_norms(l):
                tiles = 4 if l == 0 else 2
                for i, (src, lo, n, width) in enumerate(((sq_v[:, 0:GROUP * tiles], 96, 4 * tiles, HEAD),
                                                         (sq_d, 64, 32, HEAD), (sq_c, 0, 64, DIFF))):
                    dve.wait_ge(sem("mix_squares"), i + 1 + before("mix_squares", l))
                    dve.tensor_reduce(mix_ss[:, lo:lo + n], src.rearrange("p (g d) -> p g d", d=width), AX, ALU.add)\
                        .then_inc(sem("mix_sums"), 1)
                dve.wait_ge(sem("mix_std"), 2 + before("mix_std", l))
                last = 96 + 4 * tiles
                link(dve.reciprocal(mix_ss[:, 0:last], mix_ss[:, 0:last]))
                for lo, groups, scale in ((0, 8, DIFF ** -0.5), (64, 4, HEAD ** -0.5)):
                    q = mix_ss[:, lo:lo + 8 * groups].rearrange("p (t w g) -> p t w g", t=4, w=2)[:, :, 0, :]
                    link(dve.tensor_scalar(q, q, scale, None, ALU.mult))
                c = qk_c.rearrange("p t f -> p (t f)").rearrange("p (g d) -> p g d", d=DIFF)
                dve.wait_ge(sem("proj_read_dve"), 8 + before("proj_read_dve", l))
                dve.tensor_tensor(c, c, bc(mix_ss[:, 0:64], DIFF), ALU.mult).then_inc(sem("c_normed"), 1)
                for t in range(tiles):
                    v = gated[:, t, GROUP:2 * GROUP].rearrange("p (g d) -> p g d", d=HEAD)
                    ins = dve.tensor_tensor(v, v, bc(mix_ss[:, 96 + 4 * t:100 + 4 * t], HEAD), ALU.mult)
                ins.then_inc(sem("v_normed"), 1)
                dve.wait_ge(sem("c_normed"), 1 + before("c_normed", l))
                dve.wait_ge(sem("c_swapped"), 2 + before("c_swapped", l))
                sw = swapped.rearrange("p (t f) -> p t f", t=4)
                for t in range(4):
                    for src, table in ((qk_c[:, t, :], rope_cos), (sw[:, t, :], rope_sin)):
                        v = src.rearrange("p (w g d) -> p w g d", w=2, d=DIFF)
                        ins = dve.tensor_tensor(v, v, bc_mid(table[:, t, :, :], 8), ALU.mult)
                link(ins)
                c = qk_c.rearrange("p t f -> p (t f)")
                dve.tensor_tensor(c, c, swapped, ALU.add).then_inc(sem("qk_ready"), 1)
                d = qk_d.rearrange("p t f -> p (t f)").rearrange("p (g d) -> p g d", d=HEAD)
                link(dve.tensor_tensor(d, d, bc(mix_ss[:, 64:96], HEAD), ALU.mult))
                g = rows[:, columns(ROWS, "d_gain")].rearrange("p (w d) -> p w d", w=2)
                for t in range(4):
                    v = qk_d[:, t, :].rearrange("p (w h d) -> p w h d", w=2, d=HEAD)
                    ins = dve.tensor_tensor(v, v, bc_mid(g, HEADS), ALU.mult)
                ins.then_inc(sem("qk_ready"), 1)

            def spatial_gating(l):
                tiles = 4 if l == 0 else 2
                dve.wait_ge(sem("sgu_mixed"), 1 + before("sgu_mixed", l))
                dve.wait_ge(sem("qk_ready"), 2 + before("qk_ready", l))
                b = vec1[:, l, columns(VEC1, "sgu_b")]
                for h in range(HEADS):
                    cols = slice(HEAD * h, HEAD * h + HEAD)
                    mixed = ps[:, 4 + h // 2, N * (h % 2):N * (h % 2) + HEAD * tiles].rearrange("p (t c) -> p t c", t=tiles)
                    ins = dve.scalar_tensor_tensor(ycat[:, 0:tiles, cols], mixed, b[:, h:h + 1], gated[:, 0:tiles, cols],
                                                   ALU.add, ALU.mult)
                ins.then_inc(sem("sgu_done"), 1)

            def read_fourier(l):
                for s in range(2 if l == 0 else 1):
                    dve.wait_ge(sem("fourier_done"), 2 * s + 2 + before("fourier_done", l))
                    dve.tensor_copy(ycat[:, 2 * s:2 * s + 2, GROUP:2 * GROUP],
                                    ps[:, 4 + s, :].rearrange("p (t f) -> p t f", t=2)).then_inc(sem("fourier_read"), 1)

            def read_qk_t(l, which):
                for b in (1, 3):
                    dve.wait_ge(sem("qk_turned"), 4 * which + b + 1 + before("qk_turned", l))
                    width = 512 if l == 0 or b >= 2 else N
                    dve.tensor_copy(qk_t[:, b, 0:width], ps[:, b, 0:width]).then_inc(sem("qk_t_dve"), 1)

            def attention_c(l):
                todo = units(l)

                def maxima(u):
                    width = keys(todo[u][0])[1]
                    for m in range(2):
                        i = 2 * u + m
                        dve.wait_ge(sem("c_scores"), i + 1 + before("c_scores", l))
                        dve.tensor_reduce(c_max[:, i:i + 1], ps[:, 2 * (u % 2) + m, 0:width], AX, ALU.max, negate=True)\
                            .then_inc(sem("c_max"), 1)

                maxima(0)
                for u, (q, h) in enumerate(todo):
                    if u + 1 < len(todo):
                        maxima(u + 1)
                    width = keys(q)[1]
                    den = c_den[:, 2 * u:2 * u + 2]
                    dve.wait_ge(sem("c_exp"), 2 * u + 2 + before("c_exp", l))
                    link(dve.reciprocal(den, den))
                    link(dve.tensor_tensor(den[:, 1:2], den[:, 1:2], neg_lam, ALU.mult))
                    e0, e1 = (expo[:, 2 * (u % 2) + m, 0:width] for m in range(2))
                    link(dve.tensor_scalar(e1, e1, den[:, 1:2], None, ALU.mult))
                    dve.scalar_tensor_tensor(e0, e0, den[:, 0:1], e1, ALU.mult, ALU.add).then_inc(sem("c_weights"), 1)
                    if h == HEADS - 1:
                        dve.wait_ge(sem("c_pv"), u + 1 + before("c_pv", l))
                        dve.tensor_copy(ycat[:, q, 2 * GROUP:3 * GROUP], ps[:, 6, 0:GROUP])\
                            .then_inc(sem("c_out"), 1)

            def attention_d(l):
                todo = units(l)

                def maximum(u):
                    width = keys(todo[u][0])[1]
                    dve.wait_ge(sem("d_scores"), u + 1 + before("d_scores", l))
                    dve.tensor_reduce(d_max[:, u:u + 1], ps[:, u % 3, 0:width], AX, ALU.max, negate=True)\
                        .then_inc(sem("d_max"), 1)

                maximum(0)
                maximum(1)
                for u, (q, h) in enumerate(todo):
                    if u + 2 < len(todo):
                        maximum(u + 2)
                    dve.wait_ge(sem("d_exp"), u + 1 + before("d_exp", l))
                    link(dve.reciprocal(d_den[:, u:u + 1], d_den[:, u:u + 1]))
                    dve.wait_ge(sem("d_pv"), u + 1 + before("d_pv", l))
                    dve.tensor_scalar(ycat[:, q, 3 * GROUP + HEAD * h:3 * GROUP + HEAD * h + HEAD],
                                      ps[:, (6, 3)[u % 2], 0:HEAD], d_den[:, u:u + 1], None, ALU.mult).then_inc(sem("d_out"), 1)

            def merge(l):
                tiles = 4 if l == 0 else 2
                dve.wait_ge(sem("y_squares"), 1 + before("y_squares", l))
                y = ycat[:, 0:tiles, :].rearrange("p t f -> p (t f)").rearrange("p (g d) -> p g d", d=HEAD)
                dve.tensor_reduce(y_ss[:, 0:16 * tiles], y_sq[:, 0:D * tiles].rearrange("p (g d) -> p g d", d=HEAD), AX,
                                  ALU.add).then_inc(sem("y_sums"), 1)
                dve.wait_ge(sem("y_std"), 1 + before("y_std", l))
                link(dve.reciprocal(y_ss[:, 0:16 * tiles], y_ss[:, 0:16 * tiles]))
                dve.tensor_tensor(y, y, bc(y_ss[:, 0:16 * tiles], HEAD), ALU.mult).then_inc(sem("y_normed"), 1)
                add_gated(l, "mix_out", "mix_added", 2 * KT, 6, 0, tiles // 2)

            def add_gated(l, produced, added, at, banks, first, streams):
                for d in range(KT):
                    dve.wait_ge(sem(produced), d + 1 + before(produced, l))
                    for s in range(streams):
                        x = x_res[:, d, N * s:N * s + N]
                        ins = dve.scalar_tensor_tensor(x, ps[:, first + d % banks, N * s:N * s + N],
                                                       mod[:, l, at + d, s:s + 1], x, ALU.mult, ALU.add)
                    ins.then_inc(sem(added), 1)

            def route(l):
                tiles = 4 if l == 0 else 2
                streams = tiles // 2
                rows_ = 48 if l == 0 else 16
                for j in range(1, 2 * tiles, 2):
                    dve.wait_ge(sem("h_turned"), j + 1 + before("h_turned", l))
                    dve.tensor_copy(h_tok[:, j // 2, 512:1024], ps[:, 1 + j % 4, :]).then_inc(sem("h_tok_dve"), 1)
                dve.wait_ge(sem("logits"), 1 + before("logits", l))
                raw = ps[:, 0, 0:EXPERTS * tiles].rearrange("p (t e) -> p t e", t=tiles)
                lg = logit[:, 0:EXPERTS * tiles].rearrange("p (t e) -> p t e", t=tiles)
                link(dve.tensor_reduce(r_max[:, 0:tiles], raw, AX, ALU.max))
                dve.tensor_tensor(lg, raw, bc(r_max[:, 0:tiles], EXPERTS), ALU.subtract).then_inc(sem("logits_shifted"), 1)
                dve.wait_ge(sem("logits_exp"), 1 + before("logits_exp", l))
                link(dve.tensor_reduce(r_sum[:, 0:tiles], lg, AX, ALU.add))
                link(dve.reciprocal(r_sum[:, 0:tiles], r_sum[:, 0:tiles]))
                dve.tensor_tensor(lg, lg, bc(r_sum[:, 0:tiles], EXPERTS), ALU.mult).then_inc(sem("aff"), 1)
                if l == 0:
                    link(dve.memset(aff_t[0:48, :], 0.0))
                dve.wait_ge(sem("aff_turned"), 1 + before("aff_turned", l))
                for s in range(streams):
                    link(dve.tensor_copy(aff_t[32 * s:32 * s + EXPERTS, :], ps[0:EXPERTS, 0, N * s:N * s + N]))
                src = aff_t
                for r in range(CAP // 8):
                    link(dve.max(top8[0:rows_, :], src[0:rows_, :]))
                    link(dve.match_replace(work[0:rows_, :], top8[0:rows_, :], src[0:rows_, :], -1.0))
                    src = work
                link(dve.tensor_scalar(sel[0:rows_, :], work[0:rows_, :], -1.0, None, ALU.is_equal))
                link(dve.tensor_scalar(work[0:rows_, :], work[0:rows_, :], 0.0, 1.0, ALU.mult, ALU.add))
                link(dve.tensor_tensor_scan(cum[0:rows_, :], work[0:rows_, :], sel[0:rows_, :], 0.0, ALU.mult, ALU.add))
                dve.tensor_tensor(slot_id[0:rows_, :], cum[0:rows_, :], sel[0:rows_, :], ALU.mult).then_inc(sem("slots"), 1)
                dve.wait_ge(sem("slots_turned"), 1 + before("slots_turned", l))
                turned = ps[:, 0, 0:96].rearrange("p (a r) -> p a r", a=2)
                for s in range(streams):
                    ins = dve.tensor_copy(slot_tokens[:, 2 * s:2 * s + 2, :], turned[:, :, 32 * s:32 * s + EXPERTS])
                    link(ins)
                for t in range(tiles):
                    ins = dve.tensor_tensor(gather[:, t, :, :], bc(slot_tokens[:, t, :], CAP), bc_mid(slot_row, EXPERTS),
                                            ALU.is_equal)
                ins.then_inc(sem("gather_ready"), 1)
                for s in range(streams):
                    dve.wait_ge(sem("slots_spread"), s + 1 + before("slots_spread", l))
                    dve.wait_ge(sem("aff_bc"), s + 1 + before("aff_bc", l))
                    for half in range(2):
                        dve.scalar_tensor_tensor(scatter[:, s, 2 * half:2 * half + 2, :].rearrange("p g t -> p (g t)"),
                                                 ps[:, 3 + half, :], slot_col, aff_bc[:, 512 * half:512 * half + 512],
                                                 ALU.is_equal, ALU.mult).then_inc(sem("scatter_ready"), 1)
                for j in range(1, KT * streams, 2):
                    s, k = divmod(j, KT)
                    dve.wait_ge(sem("gathered"), j + 1 + before("gathered", l))
                    dve.tensor_copy(picked_of(l)[:, k, :, CAP * s:CAP * s + CAP],
                                    ps[:, j % 6, :].rearrange("p (e s) -> p e s", e=EXPERTS)).then_inc(sem("picked_dve"), 1)

            def experts(l):
                m = 2 * CAP if l == 0 else CAP
                dve.wait_ge(sem("picked_act"), KT // 2 * (m // CAP) + before("picked_act", l))
                dve.wait_ge(sem("picked_dve"), KT // 2 * (m // CAP) + before("picked_dve", l))
                dve.wait_ge(sem("gathered"), KT * (m // CAP) + before("gathered", l))

                def tokens(e, j):
                    dst = x_exp[:, 512 * (j % 2):512 * (j % 2) + KT * m].rearrange("p (k m) -> p k m", k=KT)
                    dve.tensor_copy(dst, picked_of(l)[:, :, e, :]).then_inc(sem("x_exp"), 1)

                first = chunk_at["experts", l]
                with dve.Fori(0, EXPERTS // 4) as it:
                    tokens(it * 4, 0)
                    for j in range(4):
                        dve.wait_ge(sem("exp_silu"), it * 4 + (j + 1) + before("exp_silu", l))
                        dve.wait_ge(weights_used, it * 24 + (first + 6 * j + 4))
                        hid = hid_exp[0:2 * m, :]
                        dve.tensor_tensor(hid, hid, ps[0:2 * m, 1, :], ALU.mult).then_inc(sem("exp_hid"), 1)
                        if j < 3:
                            tokens(it * 4 + (j + 1), j + 1)
                        dve.wait_ge(weights_used, it * 24 + (first + 6 * j + 6))
                        for s in range(m // CAP):
                            o = (o_lat, o_ctx)[s]
                            ins = dve.tensor_copy(o[32 * j:32 * j + 32, it, 512:1024], ps[m + 32 * s:m + 32 * s + 32, 3, :])
                        ins.then_inc(sem("o_dve"), 1)

            def ffn(i):
                def one(f, n, it):
                    dve.wait_ge(sem("ffn_silu"), it * 8 + (n + 1) if it is not None else n + 1)
                    dve.tensor_tensor(hid_f[:, f, :], silu_f[:, f, :], ps[:, f, N:2 * N], ALU.mult).then_inc(sem("ffn_hid"), 1)

                with dve.Fori(0, FT // 8) as it:
                    for f in range(8):
                        one(f % 4, FT * i + f, it)
                for f in range(FT // 8 * 8, FT):
                    one(f % 4, FT * i + f, None)
                dve.wait_ge(weights_used, chunk_at["ffn", i] + FFN_CHUNKS)
                add_sums(0.5, "ffn_added")

            def add_sums(scale, added):
                for b in range(4):
                    x = x_res[:, 2 * b:2 * b + 2, 0:N]
                    dve.scalar_tensor_tensor(x, ps[:, 4 + b, :].rearrange("p (d t) -> p d t", d=2), scale, x,
                                             ALU.mult, ALU.add).then_inc(sem(added), 1)

            def softplus_rate():
                a = vec2[:, columns(VEC2, "a_param")]
                s = [t[:, :] for t in lru_s]
                link(dve.tensor_scalar(s[2], a, -1.0, None, ALU.mult))
                dve.tensor_tensor(s[0], a, s[2], ALU.max).then_inc(sem("lru_abs"), 1)
                link(dve.tensor_scalar(s[2], s[2], 0.0, None, ALU.max))
                dve.wait_ge(sem("lru_exp"), 1)
                link(dve.tensor_scalar(s[3], s[1], 2.0, None, ALU.add))
                link(dve.reciprocal(s[3], s[3]))
                link(dve.tensor_tensor(s[1], s[1], s[3], ALU.mult))
                link(dve.tensor_tensor(s[3], s[1], s[1], ALU.mult))
                link(dve.tensor_scalar(s[4], s[3], 1.0 / 17, None, ALU.mult))
                for c in range(15, 2, -2):
                    link(dve.scalar_tensor_tensor(s[4], s[4], 1.0 / c, s[3], ALU.add, ALU.mult))
                link(dve.scalar_tensor_tensor(s[4], s[4], 1.0, s[1], ALU.add, ALU.mult))
                link(dve.scalar_tensor_tensor(s[4], s[4], 2.0, s[2], ALU.mult, ALU.add))
                link(dve.tensor_scalar(s[4], s[4], 8.0, None, ALU.mult))
                dve.tensor_scalar(s[5], s[4], -1.0, None, ALU.mult).then_inc(sem("lru_rate"), 1)

            def lru():
                v = lambda name: vec2[:, columns(VEC2, name)]
                link(dve.memset(l_pad[:, :, 0:CONV - 1], 0.0))
                for o in range(RT):
                    dve.wait_ge(sem("lru_in"), RT + o + 1)
                    dve.tensor_copy(l_pad[:, o, CONV - 1:CONV - 1 + N], ps[:, (RT + o) % 8, 0:N]).then_inc(sem("lru_read_dve"), 1)
                dve.wait_ge(sem("lru_read_dve"), RT)
                w = v("conv_w")
                for tap in range(CONV):
                    for o in range(RT):
                        src = l_pad[:, o, tap:tap + N]
                        if tap == 0:
                            ins = dve.tensor_scalar(l_x[:, o, :], src, w[:, o:o + 1], v("conv_b")[:, o:o + 1], ALU.mult, ALU.add)
                        else:
                            ins = dve.scalar_tensor_tensor(l_x[:, o, :], src, w[:, RT * tap + o:RT * tap + o + 1], l_x[:, o, :],
                                                           ALU.mult, ALU.add)
                        if tap == CONV - 1:
                            ins.then_inc(sem("lru_conv"), 1)
                        elif o == RT - 1:
                            link(ins)
                softplus_rate()
                flat = lambda ap: ap.rearrange("p o t -> p (o t)")
                dve.wait_ge(sem("lru_gates"), 2 * RT)
                dve.wait_ge(sem("lru_gate_in"), RT)
                link(dve.tensor_tensor(flat(l_i), flat(l_i), flat(l_x), ALU.mult))
                dve.wait_ge(sem("lru_decay"), RT)
                link(dve.tensor_scalar(flat(l_x), flat(l_r), 1.0, None, ALU.add))
                link(dve.reciprocal(flat(l_x), flat(l_x)))
                dve.tensor_tensor(flat(l_r), flat(l_r), flat(l_x), ALU.mult).then_inc(sem("lru_square"), 1)
                dve.wait_ge(sem("lru_mult"), 1)
                link(dve.tensor_tensor(flat(l_i), flat(l_i), flat(l_r), ALU.mult))
                for o in range(RT):
                    ins = dve.tensor_tensor_scan(l_x[:, o, :], l_a[:, o, :], l_i[:, o, :], 0.0, ALU.mult, ALU.add)
                link(ins)
                dve.wait_ge(sem("lru_read_act"), RT)
                dve.tensor_tensor(flat(l_gate), flat(l_gate), flat(l_x), ALU.mult).then_inc(sem("lru_y"), 1)
                dve.wait_ge(weights_used, chunk_at["lru", 0] + 10)
                add_sums(1.0, "lru_added")

            def pooling():
                norm = h_buf
                norm_ready(dve, 9)
                dve.wait_ge(sem("pool_inv_loaded"), 16)
                src = norm[:, :, 0:N]
                for g, win in enumerate(POOLS):
                    lo = 2 * g
                    back = win // 2
                    dst = (pool_a, pool_b)[g % 2]
                    link(dve.tensor_copy(dst[:, lo:KT, 0:back], src[:, lo:KT, 0:back]))
                    link(dve.tensor_tensor(dst[:, lo:KT, back:N], src[:, lo:KT, back:N], src[:, lo:KT, 0:N - back], ALU.add))
                    inv = bc_mid(pool_inv[:, g, :], 2)
                    link(dve.tensor_tensor(pool_u[:, lo:lo + 2, :], dst[:, lo:lo + 2, :], inv, ALU.mult))
                    src = dst
                dve.tensor_tensor(pool_u, pool_u, norm[:, :, 0:N], ALU.subtract).then_inc(sem("pool_ready"), 1)
                b, s = (vec2[:, columns(VEC2, n)] for n in ("pool_b", "pool_scale"))
                for d in range(KT):
                    dve.wait_ge(sem("pool_mapped"), d // 2 + 1)
                    y = pool_a[:, d, :]
                    link(dve.tensor_scalar(y, ps[:, 4 + d // 2, N * (d % 2):N * (d % 2) + N], b[:, d:d + 1], s[:, d:d + 1],
                                           ALU.add, ALU.mult))
                    x = x_res[:, d, 0:N]
                    dve.tensor_tensor(x, x, y, ALU.add).then_inc(sem("pool_added"), 1)

            def ple(l):
                for d in range(KT):
                    dve.wait_ge(sem("ple_gate"), KT * l + d + 1)
                    y = hid_f[:, d % 4, :]
                    link(dve.tensor_tensor(y, silu_f[:, d % 4, :], ps[:, 1 + d % 6, N:2 * N], ALU.mult))
                    x = x_res[:, d, 0:N]
                    dve.tensor_tensor(x, x, y, ALU.add).then_inc(sem("ple_added"), 1)

            link(dve.memset(mean_w[:, :], 1.0 / D))
            link(dve.memset(eps_col[:, :], EPS))
            dve.memset(cond[:, :, :], 0.0).then_inc(sem("cond_ready"), 1)
            dve.memset(zeros[:, :], 0.0).then_inc(sem("memsets"), 1)
            dve.wait_ge(sem("setup_loaded"), 16 * 5)
            for i in range(3):
                ada_group(0, i)
            for l in range(LAYERS):
                gains(l)
                norm_dve(dve, link, 2 * l, rstd, lambda k, s: gain1[:, k, s:s + 1])
                row_constants(l)
                projection(l)
                qk_norms(l)
                if l == 0:
                    ada_group(1, 0)
                read_qk_t(l, 0)
                spatial_gating(l)
                read_fourier(l)
                if l == 0:
                    ada_group(1, 1)
                lam_value(l)
                attention_c(l)
                read_qk_t(l, 1)
                if l == 0:
                    ada_group(1, 2)
                attention_d(l)
                merge(l)
                norm_dve(dve, link, 2 * l + 1, rstd, lambda k, s: gain2[:, k, s:s + 1])
                route(l)
                experts(l)
                add_gated(l, "moe_out", "moe_added", 5 * KT, 4, 4, 2 if l == 0 else 1)
            for l in range(LAYERS):
                i = 4 + 4 * l

                def gain(name, l=l):
                    g = vec2[:, columns(VEC2, name)]
                    return lambda k, s: g[:, KT * l + k:KT * l + k + 1]

                norm_dve(dve, link, i, rstd2, gain("ffn1_norm"))
                ffn(2 * l)
                norm_dve(dve, link, i + 1, rstd2, gain("mix_norm"))
                if l == 0:
                    lru()
                else:
                    pooling()
                norm_dve(dve, link, i + 2, rstd2, gain("ffn2_norm"))
                ffn(2 * l + 1)
                norm_dve(dve, link, i + 3, rstd2, gain("ple_norm"))
                ple(l)
            final = vec2[:, columns(VEC2, "final_norm")]
            norm_dve(dve, link, 12, rstd2, lambda k, s: final[:, k:k + 1])


def host_constants():
    f = np.float32
    tok = np.arange(N)
    const = {
        "ident": np.eye(P, dtype=f),
        "slot_row": np.broadcast_to(np.arange(1, CAP + 1, dtype=f), (P, CAP)),
        "slot_col": (np.arange(P) % CAP + 1).astype(f)[:, None],
    }
    half = DIFF // 2
    inv = (1.0 / (10000.0 ** (np.arange(0, half, 2, dtype=f) / f(half)))).astype(f)
    row, col = ((a.astype(f)[:, None] * inv).astype(f) for a in (tok // GRID_W, tok % GRID_W))
    cos = np.concatenate([np.cos(row), np.cos(row), np.cos(col), np.cos(col)], 1).astype(f)
    sin = np.concatenate([-np.sin(row), np.sin(row), -np.sin(col), np.sin(col)], 1).astype(f)
    cos = np.concatenate([cos, np.ones_like(cos)]).reshape(4, P, DIFF)
    sin = np.concatenate([sin, np.zeros_like(sin)]).reshape(4, P, DIFF)
    const["cos"] = cos.transpose(1, 0, 2).reshape(P, 4 * DIFF)
    const["sin"] = sin.transpose(1, 0, 2).reshape(P, 4 * DIFF)
    q, k = np.arange(P) % GRID_W, tok % GRID_W
    start = np.clip(q - NA_COLS // 2, 0, GRID_W - NA_COLS)
    inside = (k[None] >= start[:, None]) & (k[None] < start[:, None] + NA_COLS)
    turn = 2 * np.pi * np.outer(tok, tok) / N
    scale = 1.0 / math.sqrt(N * HEAD)
    turn_d = 2 * np.pi * np.outer(np.arange(HEAD), np.arange(HEAD)) / HEAD
    two = np.eye(P // HEAD)

    def on_partitions(a):
        return a.reshape(2, P, N).transpose(1, 0, 2).reshape(P, 2 * N)

    att = {
        "mask": np.where(inside, 0.0, NEG),
        "cos_n": on_partitions(np.cos(turn) * scale),
        "sin_n": on_partitions(-np.sin(turn) * scale),
        "cs_d": np.concatenate([np.kron(two, np.cos(turn_d)), np.kron(two, np.sin(turn_d))], 1),
    }
    expand = np.zeros((48, 4, 4, CAP), f)
    for e in range(EXPERTS):
        expand[e, e // 4, e % 4] = expand[32 + e, e // 4, e % 4] = 1
    count = np.stack([1.0 / np.minimum(tok + 1, w).astype(f) for w in POOLS]).astype(f)

    def packed(parts, widths):
        return np.ascontiguousarray(np.concatenate([parts[n] for n in widths], 1).astype(f))

    return {
        "const": packed(const, CONST), "att": packed(att, ATT),
        "expand": np.ascontiguousarray(expand.reshape(48, 512)),
        "pool_inv": np.ascontiguousarray(np.broadcast_to(count.reshape(1, -1), (P, 4 * N))),
    }


def host_layout(a):
    def feat(v):
        return v.reshape(-1, P).T

    vec1 = np.stack([np.concatenate([feat(a["ada_b"][l]), feat(a["norm1_g"][l]), feat(a["norm2_g"][l]),
                                     feat(a["head_out_g"][l]), a["sgu_b"][l].T], 1) for l in range(LAYERS)], 1)
    both = [np.concatenate([feat(a[n + "_2"][l]) for l in range(LAYERS)], 1)
            for n in ("ffn1_norm", "mix_norm", "ffn2_norm", "ple_norm")]
    vec2 = np.concatenate(both + [
        feat(a["lru_conv_w_2"][0].reshape(-1)), feat(a["lru_conv_b_2"][0]), feat(a["lru_b_a_2"][0]), feat(a["lru_b_x_2"][0]),
        feat(a["lru_a_param_2"][0]), feat(a["pool_b_2"][0]), feat(a["pool_scale_2"][0]), feat(a["final_norm_2"])], 1)
    partner = np.arange(DIFF).reshape(2, 2, 8)[:, ::-1].reshape(-1)
    qg, kg = a["diff_qn_g"], a["diff_kn_g"]
    rows = np.concatenate([qg, kg, qg[:, partner], kg[:, partner], a["na_qn_g"], a["na_kn_g"],
                           a["diff_lambda"].reshape(LAYERS, -1)], 1)

    def blocks(w):
        full = np.zeros((D_RNN, D_RNN), w.dtype)
        for h in range(D_RNN // LRU_HEAD):
            at = slice(h * LRU_HEAD, (h + 1) * LRU_HEAD)
            full[at, at] = w[h]
        return np.concatenate([full[k * P:k * P + P, o * P:o * P + P] for o, k in PAIRS], 1)

    row, col = np.divmod(np.arange(N), GRID_W)
    row_off = row[None] - row[:, None] + NA_ROWS - 1
    col_off = np.clip(col[None] - col[:, None], 1 - NA_COLS, NA_COLS - 1) + NA_COLS - 1
    rel_bias = a["na_rpb"][:, :, row_off, col_off].reshape(LAYERS, HEADS, 2, P, N).transpose(0, 3, 2, 1, 4)
    cond = np.stack([a["c"][0], a["c_ctx"]]).reshape(2, KT, P).transpose(2, 1, 0)
    router = a["router_w"].reshape(LAYERS, KT, P, EXPERTS).transpose(2, 0, 1, 3).reshape(P, -1)
    return {
        "x_t": a["x"][0].T, "ctx_t": a["ctx"][0].T, "cond_t": cond, "vec1": vec1, "vec2": vec2,
        "rows": np.broadcast_to(rows[:, None, :], (LAYERS, P, ROWS_W)), "router": router,
        "sgu_t": a["sgu_w"].transpose(0, 3, 1, 2), "rel_bias": rel_bias,
        "ada_w": a["ada_w"], "w_in": a["w_in"], "w_out": a["w_out"],
        "exp_gate": a["exp_w_gate"], "exp_up": a["exp_w_up"], "exp_down": a["exp_w_down"],
        "ffn1_gate": a["ffn1_w_gate_2"], "ffn1_up": a["ffn1_w_up_2"], "ffn1_down": a["ffn1_w_down_2"],
        "ffn2_gate": a["ffn2_w_gate_2"], "ffn2_up": a["ffn2_w_up_2"], "ffn2_down": a["ffn2_w_down_2"],
        "lru_in": a["lru_w_in_2"][0], "lru_a": blocks(a["lru_w_a_2"][0]), "lru_x": blocks(a["lru_w_x_2"][0]),
        "lru_out": a["lru_w_out_2"][0], "pool_w": a["pool_w_2"][0].reshape(D, GROUP),
        "ple_gate": a["ple_w_gate_2"], "ple_proj": a["ple_w_proj_2"], "p_t": a["p_2"][:, 0].transpose(0, 2, 1),
    }


def kernel(**inputs):
    import concourse.bacc as bacc
    from concourse.bass_utils import run_bass_kernel_spmd

    nc = bacc.Bacc("TRN2", target_bir_lowering=False, num_devices=1)
    arrays = {**host_layout({k: np.asarray(v) for k, v in inputs.items()}), **host_constants()}
    arrays = {f"in_{k}": np.ascontiguousarray(v) for k, v in arrays.items()}
    dram = {k[3:]: nc.dram_tensor(k, v.shape, F32, kind="ExternalInput").ap() for k, v in arrays.items()}
    out_t = nc.dram_tensor("out_t", (D, N), F32, kind="ExternalOutput").ap()
    build(nc, dram, out_t)
    r = run_bass_kernel_spmd(nc, [arrays], core_ids=[0])
    return np.ascontiguousarray(r.results[0]["out_t"].T)[None]
```

```python
from contextlib import ExitStack
import math

import numpy as np

import concourse.bass as bass
from concourse import mybir

F32 = mybir.dt.float32
BF16 = mybir.dt.bfloat16
ALU = mybir.AluOpType
ACT = mybir.ActivationFunctionType
AX = mybir.AxisListType.X

P = 128
D = 1024
KT = D // P
N = 256
LAYERS = 2
EPS = 1e-6
HEADS, HEAD = 4, 64
GROUP = HEADS * HEAD
DIFF = HEAD // 2
GRID_W = 64
NA_ROWS, NA_COLS = 8, 16
IN_W = 9 * GROUP
EXPERTS = 16
CAP = 2 * N // EXPERTS
D_FF = 11 * D // 4
FT = D_FF // P
D_RNN = 5 * D // 4
RT = D_RNN // P
LRU_HEAD = D_RNN // 16
CONV = 4
POOLS = (2, 4, 8, 16)
PLE = 256
NEG = -1e30

SLOTS = 6
SLOT = 4096

VEC1 = {"ada_b": 48, "norm1_g": 8, "norm2_g": 8, "head_out_g": 8, "sgu_b": 4}
VEC1_W = sum(VEC1.values())
VEC2 = {"ffn1_norm": 16, "mix_norm": 16, "ffn2_norm": 16, "ple_norm": 16, "conv_w": 40, "conv_b": 10,
        "b_a": 10, "b_x": 10, "a_param": 10, "pool_b": 8, "pool_scale": 8, "final_norm": 8}
VEC2_W = sum(VEC2.values())
ROWS = {"c_gain": 2 * DIFF, "c_gain_swapped": 2 * DIFF, "d_gain": 2 * HEAD, "lambda": 4 * DIFF}
ROWS_W = sum(ROWS.values())
CONST = {"ident": P, "slot_row": CAP, "slot_col": 1, "band_c": P // DIFF, "band_d": P // HEAD, "cos": 4 * DIFF, "sin": 4 * DIFF}
CONST_W = sum(CONST.values())
ATT = {"mask": N, "cos_n": 2 * N, "sin_n": 2 * N, "cs_d": 2 * P}
ATT_W = sum(ATT.values())


def columns(parts, name):
    at = 0
    for key, width in parts.items():
        if key == name:
            return slice(at, at + width)
        at += width
    raise KeyError(name)


def lru_pairs():
    out = []
    for o in range(RT):
        first = o * P // LRU_HEAD * LRU_HEAD
        last = (o * P + P - 1) // LRU_HEAD * LRU_HEAD + LRU_HEAD - 1
        out += [(o, k) for k in range(first // P, last // P + 1)]
    return out


PAIRS = lru_pairs()

COUNTS = {
    "rows_loaded": 32, "att_loaded": 32,
    "proj_done": 18, "proj_read_act": 14, "proj_read_dve": 4, "bias_ready": 1,
    "mix_squares": 3, "mix_sums": 3, "mix_std": 3, "c_normed": 1, "c_swapped": 2, "v_normed": 1, "qk_ready": 2,
    "qk_turned": 8, "qk_t_act": 4, "qk_t_dve": 4, "sgu_mixed": 1, "sgu_done": 1,
    "fourier_uv": 4, "uv_ready": 4, "fourier_done": 4, "fourier_read": 2,
    "c_bands": 16, "d_bands": 16, "c_scores": 32, "c_max": 32, "c_exp": 32, "c_weights": 16, "c_turned": 16, "c_wt": 16, "c_pv": 16, "c_out": 4,
    "d_scores": 16, "d_max": 16, "d_exp": 16, "d_turned": 16, "d_wt": 16, "d_pv": 16, "d_out": 16,
    "y_squares": 3, "y_sums": 3, "y_std": 3, "y_normed": 3, "y_turned": 8, "y_t": 8, "mix_out": 8, "mix_added": 8,
    "logits": 1, "logits_shifted": 1, "logits_exp": 1, "h_turned": 8, "h_tok_act": 4, "h_tok_dve": 4,
    "aff": 1, "aff_turned": 1, "slots": 1, "slots_turned": 1, "aff_spread": 2, "slots_spread": 2, "aff_bc": 2,
    "gather_ready": 1, "scatter_ready": 4, "gathered": 16, "picked_act": 8, "picked_dve": 8,
    "x_exp": 16, "exp_silu": 16, "exp_hid": 16, "exp_turned": 16, "exp_hid_t": 16, "o_act": 16, "o_dve": 16,
    "moe_out": 8, "moe_added": 8,
}


def before(name, layer):
    return COUNTS[name] * layer


def proj_jobs(layer):
    tiles = range(4)
    own = range(4) if layer == 0 else range(2)
    jobs = [(0, t, 0, 512, "act") if t in own else (0, t, 256, 256, "act") for t in tiles]
    jobs += [(1, t, 0, 512, "act") if t in own else (1, t, 256, 256, "act") for t in tiles]
    jobs += [(2, t, 0, 512, "act") for t in own]
    jobs += [(3, t, 0, 512, "dve") for t in tiles]
    jobs += [(4, c, 0, P, "act") for c in range(2)]
    return jobs


def build(nc, dram, out_t):
    ctx = ExitStack()
    with ctx:
        def sb(name, shape, dt=F32):
            return ctx.enter_context(nc.sbuf_tensor(name, shape, dt))

        sems = {}

        def sem(name):
            if name not in sems:
                sems[name] = ctx.enter_context(nc.semaphore(name))
            return sems[name]

        ring = sb("ring", [P, SLOTS, SLOT])
        x_res = sb("x_res", [P, KT, 2 * N])
        h_buf = sb("h_buf", [P, KT, 2 * N])
        arena = sb("arena", [P, 16384])
        const = sb("const", [P, CONST_W])
        vec1 = sb("vec1", [P, LAYERS, VEC1_W])
        vec2 = sb("vec2", [P, VEC2_W])
        rows = sb("rows", [P, ROWS_W])
        router_sb = sb("router_sb", [P, LAYERS, KT, EXPERTS])
        cond_in = sb("cond_in", [P, KT, 2])
        cond = sb("cond", [P, KT, 32])
        mod = sb("mod", [P, LAYERS, 48, 2])
        gain1 = sb("gain1", [P, KT, 2])
        gain2 = sb("gain2", [P, KT, 2])
        rope_cos = sb("rope_cos", [P, 4, 2, DIFF])
        rope_sin = sb("rope_sin", [P, 4, 2, DIFF])
        mean_w = sb("mean_w", [P, P])
        zeros = sb("zeros", [P, 512], BF16)
        eps_col = sb("eps_col", [P, 1])
        small = sb("small", [P, 512])
        expand = sb("expand", [48, 4 * P])
        ps = ctx.enter_context(nc.psum_tensor("ps", [P, 8, 512], F32))

        def part(lo, hi):
            return arena[:, lo:hi]

        ycat = part(0, 4096).rearrange("p (t f) -> p t f", t=4)
        gated = part(4096, 6144).rearrange("p (t f) -> p t f", t=4)
        uv = part(4096, 6144).rearrange("p (t c w f) -> p t c w f", t=4, c=2, w=2)
        qk_c = part(6144, 8192).rearrange("p (t f) -> p t f", t=4)
        expo = part(4096, 7168).rearrange("p (b f) -> p b f", b=6)
        q_band = part(7168, 8192).rearrange("p (b f) -> p b f", b=8)
        qk_d = part(8192, 10240).rearrange("p (t f) -> p t f", t=4)
        vals = part(10240, 12288).rearrange("p (t f) -> p t f", t=4)
        y_sq = part(4096, 6144)
        fourier_in = part(12288, 13312).rearrange("p (c f) -> p c f", c=2)
        w_t = part(12288, 13312).rearrange("p (b k f) -> p b k f", b=2, k=4)
        qk_t = part(13312, 15360).rearrange("p (b f) -> p b f", b=4)
        sgu_t = part(15360, 15872).rearrange("p (h f) -> p h f", h=HEADS)
        ada_rows = part(15872, 16384)
        sq_c, sq_v, sq_d = part(0, 2048), part(2048, 3072), part(13312, 15360)
        swapped = part(0, 2048)
        rstd = part(4096, 4608)
        h_flat = h_buf[:, :, :].rearrange("p k t -> p (k t)")
        rel_bias = h_flat[:, 0:2048].rearrange("p (q h f) -> p q h f", q=2, h=HEADS)
        att = h_flat[:, 2048:2048 + ATT_W]
        picked = part(0, 8192).rearrange("p (k e m) -> p k e m", k=KT, e=EXPERTS)
        aff_bc = part(0, 1024)
        aff_t, work, sel, cum, slot_id = (part(a, a + N) for a in (3072, 3328, 3584, 3840, 4608))
        h_tok = part(8192, 12288).rearrange("p (t f) -> p t f", t=4)
        o_lat = part(8192, 12288).rearrange("p (g f) -> p g f", g=4)
        o_ctx = h_flat.rearrange("p (g f) -> p g f", g=4)
        scatter = part(12288, 14336).rearrange("p (s g t) -> p s g t", s=2, g=4)
        gather = part(14336, 16384).rearrange("p (t e s) -> p t e s", t=4, e=EXPERTS)
        x_exp = part(14336, 15360)
        hid_exp = part(15360, 15872)
        hid_exp_t = part(15872, 16384)
        rstd2 = part(0, 256)
        silu_f = part(512, 1536).rearrange("p (f t) -> p f t", f=4)
        hid_f = part(1536, 2560).rearrange("p (f t) -> p f t", f=4)
        l_gate = part(2560, 5120).rearrange("p (o t) -> p o t", o=RT)
        l_pad = part(5120, 5120 + RT * 260).rearrange("p (o t) -> p o t", o=RT)
        l_a = part(5120, 7680).rearrange("p (o t) -> p o t", o=RT)
        l_x = part(7760, 10320).rearrange("p (o t) -> p o t", o=RT)
        l_r = part(10320, 12880).rearrange("p (o t) -> p o t", o=RT)
        l_i = part(12880, 15440).rearrange("p (o t) -> p o t", o=RT)
        pool_a = part(2560, 4608).rearrange("p (k t) -> p k t", k=KT)
        pool_b = part(4608, 6656).rearrange("p (k t) -> p k t", k=KT)
        pool_u = part(6656, 8704).rearrange("p (k t) -> p k t", k=KT)
        pool_inv = part(8704, 9728).rearrange("p (g t) -> p g t", g=4)

        ident = const[:, columns(CONST, "ident")]
        slot_row = const[:, columns(CONST, "slot_row")]
        slot_col = const[:, columns(CONST, "slot_col")]

        mix_ss = small[:, 0:112]
        c_max, c_den = small[:, 112:144], small[:, 144:176]
        d_max, d_den = small[:, 176:192], small[:, 192:208]
        y_ss = small[:, 208:272]
        logit = small[:, 320:384]
        Y_PIECES = ((0, 2 * HEADS, 0), (2 * GROUP, HEADS, 8 * HEADS), (3 * GROUP, HEADS, 12 * HEADS))
        r_max, r_sum = small[:, 384:388], small[:, 388:392]
        lam_tmp = small[:, 392:456]
        lam_sum, neg_lam = small[:, 456:458], small[:, 458:459]
        lru_s = [sb(f"lru_s{i}", [P, RT]) for i in range(6)]
        slot_tokens = sb("slot_tokens", [P, 4, EXPERTS])
        top8 = sb("top8", [P, 8])

        def picked_of(l):
            m = 2 * CAP if l == 0 else CAP
            return part(0, KT * EXPERTS * m).rearrange("p (k e m) -> p k e m", k=KT, e=EXPERTS)

        norms = []
        for l in range(LAYERS):
            norms += [(2 * N, 2, True), (2 * N, 2, True) if l == 0 else (N, 1, True)]
        norms += [(N, 1, False)] * (4 * LAYERS + 1)
        scaled_before = [sum(KT * s for _, s, _ in norms[:i]) for i in range(len(norms) + 1)]
        shifted_before = [sum(KT * s for _, s, sh in norms[:i] if sh) for i in range(len(norms) + 1)]
        NORM_END = scaled_before[-1]

        weights_used = sem("weights_used")
        slot_loaded = [sem(f"slot_loaded{i}") for i in range(SLOTS)]

        def slot(n):
            return ring[:, n % SLOTS, :]

        chunk_at = {}
        loads = []
        for l in range(LAYERS):
            if l == 0:
                chunk_at["ada", 0] = len(loads)
                loads += [1] * 4
            chunk_at["w_in", l] = len(loads)
            loads += [1, 1, 1, 2, 1]
            if l == 0:
                for step in range(1, 5):
                    chunk_at["ada", step] = len(loads)
                    loads += [1] * 4
            chunk_at["w_out", l] = len(loads)
            loads += [1] * 2
            if l == 0:
                for step in range(5, 6):
                    chunk_at["ada", step] = len(loads)
                    loads += [1] * 4
            chunk_at["experts", l] = len(loads)
            loads += [1] * 6 * EXPERTS
        FFN_CHUNKS = 3 * ((FT + 3) // 4)
        for l in range(LAYERS):
            chunk_at["ffn", 2 * l] = len(loads)
            loads += [1] * FFN_CHUNKS
            if l == 0:
                chunk_at["lru", 0] = len(loads)
                loads += [1] * (3 + 2 + 3 + 3)
            else:
                chunk_at["pool", 0] = len(loads)
                loads += [1]
            chunk_at["ffn", 2 * l + 1] = len(loads)
            loads += [1] * FFN_CHUNKS
            chunk_at["ple", l] = len(loads)
            loads += [2, 1, 1]

        def loaded_value(n):
            return 16 * sum(loads[n % SLOTS:n + 1:SLOTS])

        def units(l):
            return [(q, h) for q in (range(4) if l == 0 else range(2)) for h in range(HEADS)]

        def keys(q):
            return (0, 512) if q < 2 else (256, 256)

        block = ctx.enter_context(nc.Block())

        @block.sync
        def _(sp):
            loaded = sem("setup_loaded")
            sp.dma_start(cond_in[:, :, :], dram["cond_t"]).then_inc(loaded, 16)
            sp.dma_start(const[:, :], dram["const"]).then_inc(loaded, 16)
            sp.dma_start(vec1[:, :, :], dram["vec1"]).then_inc(loaded, 16)
            sp.dma_start(vec2[:, :], dram["vec2"]).then_inc(loaded, 16)
            sp.dma_start(expand[:, :], dram["expand"]).then_inc(loaded, 16)
            sp.dma_start(router_sb[:, :, :, :].rearrange("p l k e -> p l (k e)"), dram["router"]).then_inc(loaded, 16)
            sp.dma_start(x_res[:, :, 0:N], dram["x_t"].rearrange("(k p) t -> p k t", p=P)).then_inc(sem("x_loaded"), 16)
            sp.dma_start(x_res[:, :, N:2 * N], dram["ctx_t"].rearrange("(k p) t -> p k t", p=P)).then_inc(sem("x_loaded"), 16)

            def load(n, src, lo=0, first=True):
                width = 1
                for d in src.shape[1:]:
                    width *= d
                if first and n >= SLOTS:
                    sp.wait_ge(weights_used, n - SLOTS + 1)
                dst = slot(n)[:, lo:lo + width]
                if len(src.shape) == 3:
                    dst = dst.rearrange("p (a b) -> p a b", a=src.shape[1])
                sp.dma_start(dst, src).then_inc(slot_loaded[n % SLOTS], 16)

            def cols(w, lo, hi):
                return w[:, lo:hi].rearrange("(k p) n -> p k n", p=P)

            def krows(w, lo, hi):
                return w[lo * P:hi * P, :].rearrange("(k p) n -> p k n", p=P)

            def ada(step):
                l, i = divmod(step, 3)
                for j in range(4):
                    at = 512 * (4 * i + j)
                    load(chunk_at["ada", step] + j, cols(dram["ada_w"][l], at, at + 512))

            def ffn(i):
                l, which = divmod(i, 2)
                n = chunk_at["ffn", i]
                gate, up, down = (dram[f"ffn{which + 1}_{w}"][l] for w in ("gate", "up", "down"))

                for g in range((FT + 3) // 4):
                    lo, hi = 4 * g, min(4 * g + 4, FT)
                    load(n + 3 * g, cols(gate, lo * P, hi * P))
                    load(n + 3 * g + 1, cols(up, lo * P, hi * P))
                    load(n + 3 * g + 2, krows(down, lo, hi))

            for l in range(LAYERS):
                if l == 0:
                    ada(0)
                n, w = chunk_at["w_in", l], dram["w_in"][l]
                load(n, cols(w, 3 * GROUP, 5 * GROUP))
                load(n + 1, cols(w, 6 * GROUP, 8 * GROUP))
                load(n + 2, cols(w, 0, 2 * GROUP))
                load(n + 3, cols(w, 5 * GROUP, 6 * GROUP))
                load(n + 3, cols(w, 8 * GROUP, 9 * GROUP), lo=KT * GROUP, first=False)
                load(n + 4, cols(w, 2 * GROUP, 3 * GROUP))
                if l == 0:
                    for step in range(1, 5):
                        ada(step)
                for i in range(2):
                    load(chunk_at["w_out", l] + i, cols(dram["w_out"][l], 512 * i, 512 * i + 512))
                if l == 0:
                    for step in range(5, 6):
                        ada(step)
                n = chunk_at["experts", l]
                with sp.Fori(0, EXPERTS // 4) as it:
                    for c in range(24):
                        w = dram[("exp_gate", "exp_up", "exp_down")[c % 6 // 2]]
                        sp.wait_ge(weights_used, it * 24 + (n + c - SLOTS + 1))
                        half = c % 2
                        src = w[l, it * 4 + c // 6, half * 512:half * 512 + 512, :].rearrange("(k p) n -> p k n", p=P)
                        sp.dma_start(slot(n + c).rearrange("p (k n) -> p k n", k=4), src)\
                            .then_inc(slot_loaded[(n + c) % SLOTS], 16)
            for l in range(LAYERS):
                ffn(2 * l)
                if l == 0:
                    n = chunk_at["lru", 0]
                    for first, branch in ((n, D_RNN), (n + 5, 0)):
                        for i in range(0, RT, 4):
                            at, end = branch + P * i, branch + P * min(i + 4, RT)
                            load(first + i // 4, cols(dram["lru_in"], at, end))
                        if branch:
                            load(n + 3, dram["lru_a"])
                            load(n + 4, dram["lru_x"])
                    for i in range(3):
                        load(n + 8 + i, krows(dram["lru_out"], 4 * i, min(4 * i + 4, RT)))
                else:
                    load(chunk_at["pool", 0], dram["pool_w"].rearrange("(j p) n -> p j n", p=P))
                ffn(2 * l + 1)
                n = chunk_at["ple", l]
                load(n, krows(dram["ple_proj"][l], 0, 2))
                load(n, krows(dram["p_t"][l], 0, 2), lo=2 * D, first=False)
                for i in range(2):
                    load(n + 1 + i, cols(dram["ple_gate"][l], 512 * i, 512 * i + 512))
            sp.wait_ge(sem("norm_scaled"), NORM_END)
            sp.dma_start(out_t.rearrange("(k p) t -> p k t", p=P), h_buf[:, :, 0:N]).then_inc(sem("out_stored"), 16)
            sp.wait_ge(sem("out_stored"), 16)

        @block.gpsimd
        def _(pool):
            for l in range(LAYERS):
                if l > 0:
                    pool.wait_ge(sem("qk_ready"), 2 + before("qk_ready", l - 1))
                    pool.wait_ge(sem("sgu_done"), 1 + before("sgu_done", l - 1))
                    pool.wait_ge(sem("moe_added"), KT + before("moe_added", l - 1))
                pool.dma_start(rows[:, :], dram["rows"][l]).then_inc(sem("rows_loaded"), 16)
                pool.dma_start(sgu_t, dram["sgu_t"][l]).then_inc(sem("rows_loaded"), 16)
                pool.wait_ge(sem("proj_done"), len(proj_jobs(l)) + before("proj_done", l))
                pool.dma_start(att, dram["att"]).then_inc(sem("att_loaded"), 16)
                pool.dma_start(rel_bias, dram["rel_bias"][l]).then_inc(sem("att_loaded"), 16)
                pool.wait_ge(sem("att_loaded"), 32 + before("att_loaded", l))
                biases = rel_bias.rearrange("p q h f -> p (q h) f")
                mask = att[:, columns(ATT, "mask")]
                masks = bass.AP(mask.tensor, mask.offset, [list(mask.ap[0]), [0, 2 * HEADS], list(mask.ap[1])])
                pool.tensor_tensor(biases, biases, masks, ALU.add).then_inc(sem("bias_ready"), 1)
                pool.wait_ge(sem("qk_t_act"), 1 + before("qk_t_act", l))
                pool.wait_ge(sem("qk_t_dve"), 1 + before("qk_t_dve", l))
                band = const[:, columns(CONST, "band_c")]
                for u, (q, h) in enumerate(units(l)):
                    if u == 0:
                        pool.wait_ge(sem("qk_turned"), 4 + before("qk_turned", l))
                    if u >= 4:
                        pool.wait_ge(sem("c_scores"), 2 * (u - 3) + before("c_scores", l))
                    for m in range(2):
                        g = 2 * h + m
                        ins = pool.tensor_scalar(q_band[:, 2 * (u % 4) + m, :], qk_t[:, g // 4, P * q:P * q + P],
                                                 band[:, g % 4:g % 4 + 1], None, ALU.mult)
                    ins.then_inc(sem("c_bands"), 1)
                pool.wait_ge(sem("qk_t_act"), 3 + before("qk_t_act", l))
                pool.wait_ge(sem("qk_t_dve"), 3 + before("qk_t_dve", l))
                pool.wait_ge(sem("c_scores"), 2 * len(units(l)) + before("c_scores", l))
                band = const[:, columns(CONST, "band_d")]
                for u, (q, h) in enumerate(units(l)):
                    if u >= 8:
                        pool.wait_ge(sem("d_scores"), u - 7 + before("d_scores", l))
                    pool.tensor_scalar(q_band[:, u % 8, :], qk_t[:, h // 2, P * q:P * q + P],
                                       band[:, h % 2:h % 2 + 1], None, ALU.mult).then_inc(sem("d_bands"), 1)
            pool.wait_ge(sem("ple_added"), KT)
            pool.dma_start(pool_inv, dram["pool_inv"]).then_inc(sem("pool_inv_loaded"), 16)

        def squares(i):
            return part(0, 4096).rearrange("p (k t) -> p k t", k=KT) if i < 4 else \
                part(2560, 4608).rearrange("p (k t) -> p k t", k=KT)

        def norm_pe(pe, release, i):
            width = norms[i][0]
            for k in range(KT):
                pe.wait_ge(sem("norm_squares"), KT * i + k + 1)
                mm = pe.matmul(ps[:, 0, 0:width], mean_w[:, :], squares(i)[:, k, 0:width], start=k == 0, stop=k == KT - 1)
                if k == 0:
                    release(mm)
            mm.then_inc(sem("norm_mean"), 1)

        def norm_squares(act, i, added):
            width = norms[i][0]
            name, start, tiles = added
            for k in range(KT):
                if k % tiles == 0:
                    act.wait_ge(sem(name), start + k // tiles + 1)
                act.activation(squares(i)[:, k, 0:width], x_res[:, k, 0:width], ACT.Square).then_inc(sem("norm_squares"), 1)

        def norm_act(act, i, rs):
            width = norms[i][0]
            act.wait_ge(sem("norm_mean"), i + 1)
            act.activation(rs[:, 0:width], ps[:, 0, 0:width], ACT.Sqrt, bias=eps_col[:, 0:1]).then_inc(sem("norm_std"), 1)

        def norm_shift(act, i, shift):
            for k in range(KT):
                for s in range(norms[i][1]):
                    act.wait_ge(sem("norm_scaled"), scaled_before[i] + k * norms[i][1] + s + 1)
                    part_ = h_buf[:, k, s * N:s * N + N]
                    act.activation(part_, part_, ACT.Identity, bias=shift[:, k, s:s + 1]).then_inc(sem("norm_shifted"), 1)

        def norm_dve(dve, link, i, rs, gain):
            width, streams, _ = norms[i]
            dve.wait_ge(sem("norm_std"), i + 1)
            link(dve.reciprocal(rs[:, 0:width], rs[:, 0:width]))
            for k in range(KT):
                for s in range(streams):
                    lo = s * N
                    dve.scalar_tensor_tensor(h_buf[:, k, lo:lo + N], x_res[:, k, lo:lo + N], gain(k, s),
                                             rs[:, lo:lo + N], ALU.mult, ALU.mult).then_inc(sem("norm_scaled"), 1)

        def norm_tile(eng, i, k):
            _, streams, shifted = norms[i]
            name, done = ("norm_shifted", shifted_before) if shifted else ("norm_scaled", scaled_before)
            eng.wait_ge(sem(name), done[i] + (k + 1) * streams)

        def norm_ready(eng, i):
            if norms[i][2]:
                eng.wait_ge(sem("norm_shifted"), shifted_before[i + 1])
            else:
                eng.wait_ge(sem("norm_scaled"), scaled_before[i + 1])

        SC = GROUP // P

        @block.tensor
        def _(pe):
            owed = [0]

            def release(mm):
                if owed[0]:
                    mm.then_inc(weights_used, owed[0])
                    owed[0] = 0

            def chunk(n):
                pe.wait_ge(slot_loaded[n % SLOTS], loaded_value(n))

            def ada_group(step):
                n = chunk_at["ada", step]
                for j in range(4):
                    chunk(n + j)
                pe.wait_ge(sem("cond_ready"), 2)
                if step:
                    pe.wait_ge(sem("ada_mod"), step)
                for k in range(KT):
                    for j in range(4):
                        mm = pe.matmul(ps[32 * j:32 * j + 32, 7, :], cond[:, k, :], slot(n + j)[:, 512 * k:512 * k + 512],
                                       start=k == 0, stop=k == KT - 1)
                        if k == 0 and j == 0:
                            release(mm)
                        if k == KT - 1:
                            mm.then_inc(weights_used, 1)
                pe.wait_ge(sem("ada_rows"), step + 1)
                for b in range(4):
                    mm = pe.transpose(ps[:, 7, P * b:P * b + P], ada_rows[:, P * b:P * b + P], ident)
                mm.then_inc(sem("ada_turned"), 1)

            def projection(l):
                base = chunk_at["w_in", l]
                jobs = proj_jobs(l)
                seen, ordinal = {"act": 0, "dve": 0}, []
                for j, (c, t, lo, width, engine) in enumerate(jobs):
                    seen[engine] += 1
                    ordinal.append(seen[engine])
                    if j == 0 or jobs[j - 1][0] != c:
                        chunk(base + c)
                    if j >= 6:
                        pe.wait_ge(sem(f"proj_read_{jobs[j - 6][4]}"), ordinal[j - 6] + before(f"proj_read_{jobs[j - 6][4]}", l))
                    w = slot(base + c)
                    tokens = 2 * N if l == 0 else N
                    for k in range(KT):
                        start, stop = k == 0, k == KT - 1
                        if j == 0:
                            norm_tile(pe, 2 * l, k)
                        if c == 4:
                            mm = pe.matmul(ps[:, j % 6, 0:tokens], w[:, GROUP * k + P * t:GROUP * k + P * t + P],
                                           h_buf[:, k, 0:tokens], start=start, stop=stop)
                        elif c == 3:
                            both = w.rearrange("p (h k n) -> p k h n", h=2, k=KT)[:, k, :, :]
                            mm = pe.matmul(ps[:, j % 6, :].rearrange("p (h n) -> p h n", h=2),
                                           h_buf[:, k, P * t:P * t + P], both, start=start, stop=stop)
                        else:
                            mm = pe.matmul(ps[:, j % 6, 0:width], h_buf[:, k, P * t:P * t + P],
                                           w[:, 512 * k + lo:512 * k + lo + width], start=start, stop=stop)
                        if k == 0:
                            release(mm)
                    mm.then_inc(sem("proj_done"), 1)
                    if j == len(jobs) - 1 or jobs[j + 1][0] != c:
                        owed[0] += 1

            def fourier_channels(l):
                pe.wait_ge(sem("att_loaded"), 16 * 2 + before("att_loaded", l))
                tiles = 4 if l == 0 else 2
                pe.wait_ge(sem("qk_t_act"), 2 + before("qk_t_act", l))
                pe.wait_ge(sem("qk_t_dve"), 2 + before("qk_t_dve", l))
                cs = att[:, columns(ATT, "cs_d")]
                for t in range(tiles):
                    for c in range(SC):
                        mm = pe.matmul(ps[:, t, 2 * P * c:2 * P * c + 2 * P], fourier_in[:, c, P * t:P * t + P], cs,
                                       start=True, stop=True)
                    mm.then_inc(sem("fourier_uv"), 1)

            def fourier_tokens(l):
                cos_n = att[:, columns(ATT, "cos_n")].rearrange("p (a n) -> p a n", a=2)
                sin_n = att[:, columns(ATT, "sin_n")].rearrange("p (a n) -> p a n", a=2)
                for s in range(2 if l == 0 else 1):
                    if s == 0:
                        pe.wait_ge(sem("sgu_done"), 1 + before("sgu_done", l))
                    for nt in range(2):
                        pe.wait_ge(sem("uv_ready"), 2 * s + 2 + before("uv_ready", l))
                        step = 0
                        for a in range(2):
                            for w, table in enumerate((cos_n, sin_n)):
                                mm = pe.matmul(ps[:, 4 + s, N * nt:N * nt + N], table[:, a, P * nt:P * nt + P],
                                               uv[:, 2 * s + a, :, w, :], start=step == 0, stop=step == 3)
                                step += 1
                        mm.then_inc(sem("fourier_done"), 1)

            def spatial_gating(l):
                tiles = 4 if l == 0 else 2
                pe.wait_ge(sem("v_normed"), 1 + before("v_normed", l))
                pe.wait_ge(sem("rows_loaded"), 32 + before("rows_loaded", l))
                for h in range(HEADS):
                    v = gated[:, 0:tiles, GROUP + HEAD * h:GROUP + HEAD * h + HEAD]
                    out = ps[:, 4 + h // 2, N * (h % 2):N * (h % 2) + HEAD * tiles]
                    mm = pe.matmul(out.rearrange("p (t c) -> p t c", t=tiles), sgu_t[:, h, :], v, start=True, stop=True)
                mm.then_inc(sem("sgu_mixed"), 1)

            def turn_qk(l, which):
                src = (qk_c, qk_d)[which]
                if which == 0:
                    for engine in ("act", "dve"):
                        pe.wait_ge(sem(f"proj_read_{engine}"), sum(j[4] == engine for j in proj_jobs(l)) + before(f"proj_read_{engine}", l))
                pe.wait_ge(sem("qk_ready"), which + 1 + before("qk_ready", l))
                for b in range(4):
                    for t in range(4 if l == 0 or b >= 2 else 2):
                        mm = pe.transpose(ps[:, b, P * t:P * t + P], src[:, t, P * b:P * b + P], ident)
                        if t == 0:
                            release(mm)
                    mm.then_inc(sem("qk_turned"), 1)

            def attention_c(l):
                todo = units(l)
                pe.wait_ge(sem("qk_t_act"), 2 + before("qk_t_act", l))
                pe.wait_ge(sem("qk_t_dve"), 2 + before("qk_t_dve", l))

                def scores(u):
                    q, h = todo[u]
                    lo, width = keys(q)
                    if u >= 3:
                        pe.wait_ge(sem("c_exp"), 2 * (u - 2) + before("c_exp", l))
                    pe.wait_ge(sem("c_bands"), u + 1 + before("c_bands", l))
                    for m in range(2):
                        pe.matmul(ps[:, 2 * (u % 3) + m, 0:width], q_band[:, 2 * (u % 4) + m, :],
                                  qk_t[:, 2 + (2 * h + m) // 4, lo:lo + width], start=True, stop=True)\
                            .then_inc(sem("c_scores"), 1)

                for u in range(3):
                    scores(u)
                for u, (q, h) in enumerate(todo):
                    lo, width = keys(q)
                    tiles = width // P
                    pe.wait_ge(sem("c_weights"), u + 1 + before("c_weights", l))
                    if u >= 1:
                        pe.wait_ge(sem("c_wt"), u + before("c_wt", l))
                    for j in range(tiles):
                        mm = pe.transpose(ps[:, 6, P * j:P * j + P], expo[:, 2 * (u % 3), P * j:P * j + P], ident)
                    mm.then_inc(sem("c_turned"), 1)
                    if u + 3 < len(todo):
                        scores(u + 3)
                    pe.wait_ge(sem("c_wt"), u + 1 + before("c_wt", l))
                    if h == 0 and q >= 1:
                        pe.wait_ge(sem("c_out"), q + before("c_out", l))
                    at = HEAD * h
                    for j in range(tiles):
                        mm = pe.matmul(ps[:, 7, at:at + HEAD], w_t[:, u % 2, j, :],
                                       vals[:, lo // P + j, HEAD * h:HEAD * h + HEAD], start=j == 0, stop=j == tiles - 1)
                    mm.then_inc(sem("c_pv"), 1)

            def attention_d(l):
                todo = units(l)
                pe.wait_ge(sem("qk_t_act"), 4 + before("qk_t_act", l))
                pe.wait_ge(sem("qk_t_dve"), 4 + before("qk_t_dve", l))
                pe.wait_ge(sem("bias_ready"), 1 + before("bias_ready", l))

                def scores(u):
                    q, h = todo[u]
                    lo, width = keys(q)
                    if u >= 3:
                        pe.wait_ge(sem("d_exp"), u - 2 + before("d_exp", l))
                    pe.wait_ge(sem("d_bands"), u + 1 + before("d_bands", l))
                    mm = pe.matmul(ps[:, u % 3, 0:width], q_band[:, u % 8, :], qk_t[:, 2 + h // 2, lo:lo + width],
                                   start=True, stop=q >= 2)
                    if q < 2:
                        mm = pe.matmul(ps[:, u % 3, 0:N], ident, rel_bias[:, q, h, :], start=False, stop=True)
                    mm.then_inc(sem("d_scores"), 1)

                scores(0)
                scores(1)
                for u, (q, h) in enumerate(todo):
                    if u + 2 < len(todo):
                        scores(u + 2)
                    lo, width = keys(q)
                    tiles = width // P
                    pe.wait_ge(sem("d_exp"), u + 1 + before("d_exp", l))
                    if u >= 2:
                        pe.wait_ge(sem("d_wt"), u - 1 + before("d_wt", l))
                    for j in range(tiles):
                        mm = pe.transpose(ps[:, 4 + u % 2, P * j:P * j + P], expo[:, u % 4, P * j:P * j + P], ident)
                    mm.then_inc(sem("d_turned"), 1)
                    pe.wait_ge(sem("d_wt"), u + 1 + before("d_wt", l))
                    if u >= 2:
                        pe.wait_ge(sem("d_out"), u - 1 + before("d_out", l))
                    for j in range(tiles):
                        mm = pe.matmul(ps[:, (6, 3)[u % 2], 0:HEAD], w_t[:, u % 2, j, :],
                                       vals[:, lo // P + j, GROUP + HEAD * h:GROUP + HEAD * h + HEAD],
                                       start=j == 0, stop=j == tiles - 1)
                    mm.then_inc(sem("d_pv"), 1)

            def merge(l):
                tiles = 4 if l == 0 else 2
                width = P * tiles
                pe.wait_ge(sem("y_normed"), 3 + before("y_normed", l))
                for k in range(KT):
                    if k >= 6:
                        pe.wait_ge(sem("y_t"), k - 5 + before("y_t", l))
                    for t in range(tiles):
                        mm = pe.transpose(ps[:, k % 6, P * t:P * t + P], ycat[:, t, P * k:P * k + P], ident)
                    mm.then_inc(sem("y_turned"), 1)
                pe.wait_ge(sem("y_t"), KT + before("y_t", l))
                for d in range(KT):
                    n = chunk_at["w_out", l] + d // 4
                    if d % 4 == 0:
                        chunk(n)
                    if d >= 6:
                        pe.wait_ge(sem("mix_added"), d - 5 + before("mix_added", l))
                    for k in range(KT):
                        at = 512 * k + P * (d % 4)
                        mm = pe.matmul(ps[:, 1 + d % 6, 0:width], slot(n)[:, at:at + P], h_buf[:, k, 0:width],
                                       start=k == 0, stop=k == KT - 1)
                        if k == 0:
                            release(mm)
                    mm.then_inc(sem("mix_out"), 1)
                    if d % 4 == 3:
                        owed[0] += 1

            def route(l):
                tiles = 4 if l == 0 else 2
                streams = tiles // 2
                rows_ = 48 if l == 0 else 16
                for t in range(tiles):
                    for k in range(KT):
                        mm = pe.matmul(ps[:, 0, EXPERTS * t:EXPERTS * t + EXPERTS], h_buf[:, k, P * t:P * t + P],
                                       router_sb[:, l, k, :], start=k == 0, stop=k == KT - 1)
                mm.then_inc(sem("logits"), 1)
                for j in range(2 * tiles):
                    t, half = divmod(j, 2)
                    if j >= 4:
                        pe.wait_ge(sem(f"h_tok_{('act', 'dve')[j % 2]}"), (j - 4) // 2 + 1 + before(f"h_tok_{('act', 'dve')[j % 2]}", l))
                    for k in range(4):
                        mm = pe.transpose(ps[:, 1 + j % 4, P * k:P * k + P], h_buf[:, 4 * half + k, P * t:P * t + P], ident)
                    mm.then_inc(sem("h_turned"), 1)
                pe.wait_ge(sem("aff"), 1 + before("aff", l))
                for t in range(tiles):
                    mm = pe.transpose(ps[0:EXPERTS, 0, P * t:P * t + P], logit[:, EXPERTS * t:EXPERTS * t + EXPERTS], ident)
                mm.then_inc(sem("aff_turned"), 1)
                pe.wait_ge(sem("slots"), 1 + before("slots", l))
                for a in range(2):
                    mm = pe.transpose(ps[:, 0, 48 * a:48 * a + rows_], slot_id[0:rows_, P * a:P * a + P],
                                      ident[0:rows_, 0:rows_])
                mm.then_inc(sem("slots_turned"), 1)
                pe.wait_ge(sem("h_tok_act"), tiles + before("h_tok_act", l))
                pe.wait_ge(sem("h_tok_dve"), tiles + before("h_tok_dve", l))
                for s in range(streams):
                    if s:
                        pe.wait_ge(sem("scatter_ready"), 2 * s + before("scatter_ready", l))
                    experts = slice(32 * s, 32 * s + EXPERTS)
                    for src, bank, spread in ((aff_t, 1, "aff_spread"), (slot_id, 3, "slots_spread")):
                        for g in range(4):
                            mm = pe.matmul(ps[:, bank + g // 2, N * (g % 2):N * (g % 2) + N],
                                           expand[experts, P * g:P * g + P], src[experts, :], start=True, stop=True)
                        mm.then_inc(sem(spread), 1)
                pe.wait_ge(sem("gather_ready"), 1 + before("gather_ready", l))
                pe.wait_ge(sem("scatter_ready"), 2 * streams + before("scatter_ready", l))
                for j in range(KT * streams):
                    s, k = divmod(j, KT)
                    if j >= 6:
                        pe.wait_ge(sem(f"picked_{('act', 'dve')[j % 2]}"), (j - 6) // 2 + 1 + before(f"picked_{('act', 'dve')[j % 2]}", l))
                    for a in range(2):
                        mm = pe.matmul(ps[:, j % 6, :], h_tok[:, 2 * s + a, P * k:P * k + P],
                                       gather[:, 2 * s + a, :, :].rearrange("p e s -> p (e s)"),
                                       start=a == 0, stop=a == 1)
                    mm.then_inc(sem("gathered"), 1)

            def experts(l):
                m = 2 * CAP if l == 0 else CAP
                n = chunk_at["experts", l]
                pe.wait_ge(sem("picked_act"), KT // 2 * (m // CAP) + before("picked_act", l))
                pe.wait_ge(sem("picked_dve"), KT // 2 * (m // CAP) + before("picked_dve", l))
                hid_t = hid_exp_t[:, 0:8 * m].rearrange("p (j h m) -> p j h m", j=4, h=2)
                with pe.Fori(0, EXPERTS // 4) as it:
                    for j in range(4):
                        xe = x_exp[:, 512 * (j % 2):512 * (j % 2) + KT * m].rearrange("p (k m) -> p k m", k=KT)
                        pe.wait_ge(sem("x_exp"), it * 4 + (j + 1) + before("x_exp", l))
                        for which in range(2):
                            for k in range(KT):
                                c = 6 * j + 2 * which + k // 4
                                if k % 4 == 0:
                                    pe.wait_ge(slot_loaded[(n + c) % SLOTS], it * 64 + (loaded_value(n + c)))
                                for half in range(2):
                                    mm = pe.matmul(ps[half * m:half * m + m, which, :], xe[:, k, :],
                                                   slot(n + c)[:, D * (k % 4) + 512 * half:D * (k % 4) + 512 * half + 512],
                                                   start=k == 0, stop=k == KT - 1)
                                if k % 4 == 3:
                                    mm.then_inc(weights_used, 1)
                        pe.wait_ge(sem("exp_hid"), it * 4 + (j + 1) + before("exp_hid", l))
                        for b in range(4):
                            mm = pe.transpose(ps[:, 2, P * b:P * b + P], hid_exp[:, P * b:P * b + P], ident)
                        mm.then_inc(sem("exp_turned"), 1)
                        pe.wait_ge(sem("exp_hid_t"), it * 4 + (j + 1) + before("exp_hid_t", l))
                        for k in range(KT):
                            c = 6 * j + 4 + k // 4
                            if k % 4 == 0:
                                pe.wait_ge(slot_loaded[(n + c) % SLOTS], it * 64 + (loaded_value(n + c)))
                            for half in range(2):
                                mm = pe.matmul(ps[half * m:half * m + m, 3, :], hid_t[:, k % 4, k // 4, :],
                                               slot(n + c)[:, D * (k % 4) + 512 * half:D * (k % 4) + 512 * half + 512],
                                               start=k == 0, stop=k == KT - 1)
                            if k % 4 == 3:
                                mm.then_inc(weights_used, 1)

            def scatter_back(l):
                streams = 2 if l == 0 else 1
                pe.wait_ge(sem("o_act"), EXPERTS + before("o_act", l))
                pe.wait_ge(sem("o_dve"), EXPERTS + before("o_dve", l))
                for d in range(KT):
                    if d >= 4:
                        pe.wait_ge(sem("moe_added"), d - 3 + before("moe_added", l))
                    for s in range(streams):
                        for g in range(4):
                            o = (o_lat, o_ctx)[s]
                            mm = pe.matmul(ps[:, 4 + d % 4, N * s:N * s + N], o[:, g, P * d:P * d + P],
                                           scatter[:, s, g, :], start=g == 0, stop=g == 3)
                    mm.then_inc(sem("moe_out"), 1)

            def ffn_group(i, norm, first, it, step, tiles):
                n = first
                per = 8 * it if it is not None else 0

                def landed(c):
                    v = loaded_value(c)
                    pe.wait_ge(slot_loaded[c % SLOTS], it * 16 + v if it is not None else v)

                width = P * tiles
                for f in range(tiles):
                    if f == 0:
                        landed(n)
                        landed(n + 1)
                    for which in range(2):
                        for k in range(KT):
                            if step == 0 and f == 0 and which == 0:
                                norm_tile(pe, norm, k)
                            mm = pe.matmul(ps[:, f, N * which:N * which + N],
                                           slot(n + which)[:, width * k + P * f:width * k + P * f + P],
                                           h_buf[:, k, 0:N], start=k == 0, stop=k == KT - 1)
                        if f == tiles - 1 and which == 0:
                            mm.then_inc(weights_used, 1)
                    mm.then_inc(sem("ffn_gate_up"), 1)
                landed(n + 2)
                for f in range(tiles):
                    pe.wait_ge(sem("ffn_hid"), per + (FT * i + step + f + 1))
                    for d in range(KT):
                        mm = pe.matmul(ps[:, 4 + d // 2, N * (d % 2):N * (d % 2) + N],
                                       slot(n + 2)[:, D * f + P * d:D * f + P * d + P], hid_f[:, f, :],
                                       start=False, stop=False, skip_group_check=True)
                        if f == 0 and d == 0:
                            mm.then_inc(weights_used, 1)
                mm.then_inc(weights_used, 1)

            def open_sums():
                for b in range(4, 8):
                    release(pe.matmul(ps[:, b, :], zeros[:, 0:P], zeros[:, :], start=True, stop=False, skip_group_check=True))

            def ffn(i, norm):
                n = chunk_at["ffn", i]
                open_sums()
                with pe.Fori(0, FT // 8) as it:
                    ffn_group(i, norm, n, it, 0, 4)
                    ffn_group(i, norm, n + 3, it, 4, 4)
                at = FT // 8 * 8
                ffn_group(i, norm, n + 3 * at // 4, None, at, 4)
                ffn_group(i, norm, n + 3 * at // 4 + 3, None, at + 4, 2)

            def lru(norm):
                n = chunk_at["lru", 0]
                for o in range(RT):
                    c, wide = n + o // 4, P * min(4, RT - o // 4 * 4)
                    if o % 4 == 0:
                        chunk(c)
                    if o >= 8:
                        pe.wait_ge(sem("lru_read_dve"), o - 7)
                    for k in range(KT):
                        if o == 0:
                            norm_tile(pe, norm, k)
                        at = wide * k + P * (o % 4)
                        mm = pe.matmul(ps[:, o % 8, 0:N], slot(c)[:, at:at + P], h_buf[:, k, 0:N],
                                       start=k == 0, stop=k == KT - 1)
                        if k == 0:
                            release(mm)
                    mm.then_inc(sem("lru_in"), 1)
                    if o % 4 == 3 or o == RT - 1:
                        owed[0] += 1
                chunk(n + 3)
                chunk(n + 4)
                pe.wait_ge(sem("lru_read_dve"), 6)
                for o in range(RT):
                    mine = [i for i, (a, _) in enumerate(PAIRS) if a == o]
                    pe.wait_ge(sem("lru_conv"), PAIRS[mine[-1]][1] + 1)
                    if o >= 4:
                        pe.wait_ge(sem("lru_gates"), 2 * (o - 3))
                    for which in range(2):
                        for i in mine:
                            mm = pe.matmul(ps[:, 2 + o % 4, N * which:N * which + N],
                                           slot(n + 3 + which)[:, P * i:P * i + P],
                                           l_x[:, PAIRS[i][1], :], start=i == mine[0], stop=i == mine[-1])
                            if i == mine[0]:
                                release(mm)
                    mm.then_inc(sem("lru_gate_in"), 1)
                owed[0] += 2
                for o in range(RT):
                    c, wide = n + 5 + o // 4, P * min(4, RT - o // 4 * 4)
                    if o % 4 == 0:
                        chunk(c)
                    if o == 0:
                        pe.wait_ge(sem("lru_read_dve"), RT)
                    if o == 4:
                        pe.wait_ge(sem("lru_gates"), 2 * RT)
                    if o >= 8:
                        pe.wait_ge(sem("lru_read_act"), o - 7)
                    for k in range(KT):
                        at = wide * k + P * (o % 4)
                        mm = pe.matmul(ps[:, (6 + o) % 8, 0:N], slot(c)[:, at:at + P], h_buf[:, k, 0:N],
                                       start=k == 0, stop=k == KT - 1)
                        if k == 0:
                            release(mm)
                    mm.then_inc(sem("lru_branch"), 1)
                    if o % 4 == 3 or o == RT - 1:
                        owed[0] += 1
                pe.wait_ge(sem("lru_read_act"), RT)
                open_sums()
                for k in range(RT):
                    c = n + 8 + k // 4
                    if k % 4 == 0:
                        chunk(c)
                    pe.wait_ge(sem("lru_y"), k + 1)
                    for d in range(KT):
                        at = D * (k % 4) + P * d
                        mm = pe.matmul(ps[:, 4 + d // 2, N * (d % 2):N * (d % 2) + N], slot(c)[:, at:at + P],
                                       l_gate[:, k, :], start=False, stop=False, skip_group_check=True)
                    if k % 4 == 3 or k == RT - 1:
                        mm.then_inc(weights_used, 1)

            def pooling():
                n = chunk_at["pool", 0]
                chunk(n)
                pe.wait_ge(sem("pool_ready"), 1)
                for d in range(KT):
                    g, half = divmod(d, 2)
                    for k in range(2):
                        at = GROUP * (2 * g + k) + P * half
                        mm = pe.matmul(ps[:, 4 + d // 2, N * half:N * half + N], slot(n)[:, at:at + P],
                                       pool_u[:, 2 * g + k, :], start=k == 0, stop=k == 1)
                    if half:
                        mm.then_inc(sem("pool_mapped"), 1)
                owed[0] += 1

            def ple(l, norm):
                n = chunk_at["ple", l]
                chunk(n)
                for d in range(KT):
                    c = n + 1 + d // 4
                    if d % 4 == 0:
                        chunk(c)
                    if d >= 6:
                        pe.wait_ge(sem("ple_added"), KT * l + d - 5)
                    for k in range(KT):
                        if d == 0:
                            norm_tile(pe, norm, k)
                        at = 512 * k + P * (d % 4)
                        pe.matmul(ps[:, 1 + d % 6, 0:N], slot(c)[:, at:at + P], h_buf[:, k, 0:N],
                                  start=k == 0, stop=k == KT - 1)
                    for k in range(2):
                        mm = pe.matmul(ps[:, 1 + d % 6, N:2 * N], slot(n)[:, D * k + P * d:D * k + P * d + P],
                                       slot(n)[:, 2 * D + N * k:2 * D + N * k + N], start=k == 0, stop=k == 1)
                    mm.then_inc(sem("ple_products"), 1)
                owed[0] += 3

            pe.wait_ge(sem("setup_loaded"), 16 * 6)
            pe.wait_ge(sem("memsets"), 1)
            for l in range(LAYERS):
                norm_pe(pe, release, 2 * l)
                if l == 0:
                    ada_group(0)
                projection(l)
                turn_qk(l, 0)
                spatial_gating(l)
                if l == 0:
                    ada_group(1)
                fourier_channels(l)
                fourier_tokens(l)
                if l == 0:
                    ada_group(2)
                pe.wait_ge(sem("fourier_read"), (2 if l == 0 else 1) + before("fourier_read", l))
                attention_c(l)
                pe.wait_ge(sem("c_exp"), 2 * len(units(l)) + before("c_exp", l))
                turn_qk(l, 1)
                pe.wait_ge(sem("c_out"), (4 if l == 0 else 2) + before("c_out", l))
                if l == 0:
                    ada_group(3)
                attention_d(l)
                if l == 0:
                    ada_group(4)
                merge(l)
                if l == 0:
                    ada_group(5)
                norm_pe(pe, release, 2 * l + 1)
                norm_ready(pe, 2 * l + 1)
                route(l)
                experts(l)
                scatter_back(l)
            for l in range(LAYERS):
                i = 4 + 4 * l
                norm_pe(pe, release, i)
                ffn(2 * l, i)
                norm_pe(pe, release, i + 1)
                if l == 0:
                    lru(i + 1)
                else:
                    pooling()
                norm_pe(pe, release, i + 2)
                ffn(2 * l + 1, i + 2)
                norm_pe(pe, release, i + 3)
                ple(l, i + 3)
            norm_pe(pe, release, 12)

        @block.scalar
        def _(act):
            count = [0]

            def link(ins):
                count[0] += 1
                ins.then_inc(sem("act_chain"), 1)
                act.wait_ge(sem("act_chain"), count[0])

            def ada_group(step):
                act.wait_ge(weights_used, chunk_at["ada", step] + 4)
                act.activation(ada_rows, ps[:, 7, :], ACT.Copy).then_inc(sem("ada_rows"), 1)

            def projection(l, chunks):
                for j, (c, t, lo, width, engine) in enumerate(proj_jobs(l)):
                    if engine != "act" or c not in chunks:
                        continue
                    act.wait_ge(sem("proj_done"), j + 1 + before("proj_done", l))
                    if c == 2:
                        ins = act.activation(gated[:, t, :], ps[:, j % 6, :], ACT.Gelu_apprx_tanh)
                    elif c < 2:
                        ins = act.activation((qk_c, qk_d)[c][:, t, lo:lo + width], ps[:, j % 6, 0:width], ACT.Copy)
                    else:
                        tokens = 2 * N if l == 0 else N
                        ins = act.activation(fourier_in[:, t, 0:tokens], ps[:, j % 6, 0:tokens], ACT.Copy)
                    ins.then_inc(sem("proj_read_act"), 1)

            def mix_std(lo, hi, width):
                act.activation(mix_ss[:, lo:hi], mix_ss[:, lo:hi], ACT.Sqrt, bias=eps_col[:, 0:1], scale=1.0 / width)\
                    .then_inc(sem("mix_std"), 1)

            def qk_stats(l):
                act.wait_ge(sem("proj_read_act"), 8 + before("proj_read_act", l))
                act.activation(sq_c, qk_c.rearrange("p t f -> p (t f)"), ACT.Square).then_inc(sem("mix_squares"), 1)
                act.activation(sq_d, qk_d.rearrange("p t f -> p (t f)"), ACT.Square).then_inc(sem("mix_squares"), 1)
                act.wait_ge(sem("mix_sums"), 2 + before("mix_sums", l))
                mix_std(0, 64, DIFF)
                mix_std(64, 96, HEAD)
                act.wait_ge(sem("c_normed"), 1 + before("c_normed", l))
                src = qk_c.rearrange("p t f -> p (t f)").rearrange("p (g w e) -> p g w e", w=2, e=8)
                dst = swapped.rearrange("p (g w e) -> p g w e", w=2, e=8)
                for w in range(2):
                    act.activation(dst[:, :, w, :], src[:, :, 1 - w, :], ACT.Copy).then_inc(sem("c_swapped"), 1)

            def gate_stats(l):
                tiles = 4 if l == 0 else 2
                act.wait_ge(sem("proj_read_act"), 8 + tiles + before("proj_read_act", l))
                act.activation(sq_v[:, 0:GROUP * tiles].rearrange("p (t f) -> p t f", t=tiles),
                               gated[:, 0:tiles, GROUP:2 * GROUP], ACT.Square).then_inc(sem("mix_squares"), 1)
                act.wait_ge(sem("mix_sums"), 3 + before("mix_sums", l))
                mix_std(96, 96 + 4 * tiles, HEAD)

            def read_fourier_uv(l):
                for t in range(4 if l == 0 else 2):
                    act.wait_ge(sem("fourier_uv"), t + 1 + before("fourier_uv", l))
                    if t == 0:
                        act.wait_ge(sem("sgu_done"), 1 + before("sgu_done", l))
                    act.activation(uv_flat[:, t, :], ps[:, t, :], ACT.Copy).then_inc(sem("uv_ready"), 1)

            uv_flat = part(4096, 6144).rearrange("p (t f) -> p t f", t=4)

            def read_qk_t(l, which):
                for b in (0, 2):
                    act.wait_ge(sem("qk_turned"), 4 * which + b + 1 + before("qk_turned", l))
                    width = 512 if l == 0 or b >= 2 else N
                    act.activation(qk_t[:, b, 0:width], ps[:, b, 0:width], ACT.Copy).then_inc(sem("qk_t_act"), 1)

            def attention_c(l):
                todo = units(l)

                def softmax(u):
                    width = keys(todo[u][0])[1]
                    if u >= 3:
                        act.wait_ge(sem("c_turned"), u - 2 + before("c_turned", l))
                    for m in range(2):
                        i = 2 * u + m
                        act.wait_ge(sem("c_max"), i + 1 + before("c_max", l))
                        act.activation(expo[:, 2 * (u % 3) + m, 0:width], ps[:, 2 * (u % 3) + m, 0:width], ACT.Exp,
                                       bias=c_max[:, i:i + 1], accum_out=c_den[:, i:i + 1]).then_inc(sem("c_exp"), 1)

                act.wait_ge(sem("qk_turned"), 4 + before("qk_turned", l))
                for u in range(3):
                    softmax(u)
                for u, (q, h) in enumerate(todo):
                    width = keys(q)[1]
                    act.wait_ge(sem("c_turned"), u + 1 + before("c_turned", l))
                    if u >= 2:
                        act.wait_ge(sem("c_pv"), u - 1 + before("c_pv", l))
                    act.activation(w_t[:, u % 2, 0:width // P, :].rearrange("p k f -> p (k f)"), ps[:, 6, 0:width],
                                   ACT.Copy).then_inc(sem("c_wt"), 1)
                    if u + 3 < len(todo):
                        softmax(u + 3)

            def attention_d(l):
                todo = units(l)

                def softmax(u):
                    width = keys(todo[u][0])[1]
                    act.wait_ge(sem("d_max"), u + 1 + before("d_max", l))
                    if u >= 4:
                        act.wait_ge(sem("d_turned"), u - 3 + before("d_turned", l))
                    act.activation(expo[:, u % 4, 0:width], ps[:, u % 3, 0:width], ACT.Exp, bias=d_max[:, u:u + 1],
                                   accum_out=d_den[:, u:u + 1]).then_inc(sem("d_exp"), 1)

                softmax(0)
                for u in range(len(todo)):
                    if u + 1 < len(todo):
                        softmax(u + 1)
                    width = keys(todo[u][0])[1]
                    act.wait_ge(sem("d_turned"), u + 1 + before("d_turned", l))
                    if u >= 2:
                        act.wait_ge(sem("d_pv"), u - 1 + before("d_pv", l))
                    act.activation(w_t[:, u % 2, 0:width // P, :].rearrange("p k f -> p (k f)"), ps[:, 4 + u % 2, 0:width],
                                   ACT.Copy).then_inc(sem("d_wt"), 1)

            def y_stats(l, piece):
                tiles = 4 if l == 0 else 2
                lo, heads, at = Y_PIECES[piece]
                if piece == 0:
                    act.wait_ge(sem("sgu_done"), 1 + before("sgu_done", l))
                    act.wait_ge(sem("fourier_read"), tiles // 2 + before("fourier_read", l))
                    act.wait_ge(sem("qk_turned"), 4 + before("qk_turned", l))
                elif piece == 1:
                    act.wait_ge(sem("c_out"), tiles + before("c_out", l))
                    act.wait_ge(sem("c_turned"), len(units(l)) + before("c_turned", l))
                else:
                    act.wait_ge(sem("d_out"), len(units(l)) + before("d_out", l))
                    act.wait_ge(sem("d_turned"), len(units(l)) + before("d_turned", l))
                act.activation(y_sq[:, 0:tiles * heads * HEAD].rearrange("p (t f) -> p t f", t=tiles),
                               ycat[:, 0:tiles, lo:lo + heads * HEAD], ACT.Square).then_inc(sem("y_squares"), 1)
                act.wait_ge(sem("y_sums"), piece + 1 + before("y_sums", l))
                ss = y_ss[:, at:at + heads * tiles]
                act.activation(ss, ss, ACT.Sqrt, bias=eps_col[:, 0:1], scale=1.0 / HEAD).then_inc(sem("y_std"), 1)

            def merge(l):
                tiles = 4 if l == 0 else 2
                for k in range(KT):
                    act.wait_ge(sem("y_turned"), k + 1 + before("y_turned", l))
                    act.activation(h_buf[:, k, 0:P * tiles], ps[:, k % 6, 0:P * tiles], ACT.Copy,
                                   scale=head_gain(l)[:, k:k + 1]).then_inc(sem("y_t"), 1)

            def head_gain(l):
                return vec1[:, l, columns(VEC1, "head_out_g")]

            def route(l):
                tiles = 4 if l == 0 else 2
                for j in range(0, 2 * tiles, 2):
                    act.wait_ge(sem("h_turned"), j + 1 + before("h_turned", l))
                    act.activation(h_tok[:, j // 2, 0:512], ps[:, 1 + j % 4, :], ACT.Copy).then_inc(sem("h_tok_act"), 1)
                act.wait_ge(sem("logits_shifted"), 1 + before("logits_shifted", l))
                act.activation(logit[:, 0:EXPERTS * tiles], logit[:, 0:EXPERTS * tiles], ACT.Exp)\
                    .then_inc(sem("logits_exp"), 1)
                for s in range(tiles // 2):
                    act.wait_ge(sem("aff_spread"), s + 1 + before("aff_spread", l))
                    if s:
                        act.wait_ge(sem("scatter_ready"), 2 * s + before("scatter_ready", l))
                    act.activation(aff_bc.rearrange("p (b f) -> p b f", b=2), ps[:, 1:3, :], ACT.Copy)\
                        .then_inc(sem("aff_bc"), 1)
                for j in range(0, KT * tiles // 2, 2):
                    s, k = divmod(j, KT)
                    act.wait_ge(sem("gathered"), j + 1 + before("gathered", l))
                    act.activation(picked_of(l)[:, k, :, CAP * s:CAP * s + CAP],
                                   ps[:, j % 6, :].rearrange("p (e s) -> p e s", e=EXPERTS), ACT.Copy)\
                        .then_inc(sem("picked_act"), 1)

            def experts(l):
                m = 2 * CAP if l == 0 else CAP
                first = chunk_at["experts", l]
                with act.Fori(0, EXPERTS // 4) as it:
                    for j in range(4):
                        act.wait_ge(weights_used, it * 24 + (first + 6 * j + 2))
                        act.activation(hid_exp[0:2 * m, :], ps[0:2 * m, 0, :], ACT.Silu).then_inc(sem("exp_silu"), 1)
                        act.wait_ge(sem("exp_turned"), it * 4 + (j + 1) + before("exp_turned", l))
                        turned = ps[:, 2, :].rearrange("p (b m) -> p b m", b=4)[:, :, 0:2 * m]
                        act.activation(hid_exp_t[:, 0:8 * m].rearrange("p (b m) -> p b m", b=4), turned, ACT.Copy).then_inc(sem("exp_hid_t"), 1)
                        act.wait_ge(weights_used, it * 24 + (first + 6 * j + 6))
                        for s in range(m // CAP):
                            o = (o_lat, o_ctx)[s]
                            ins = act.activation(o[32 * j:32 * j + 32, it, 0:512], ps[32 * s:32 * s + 32, 3, :], ACT.Copy)
                        ins.then_inc(sem("o_act"), 1)

            def ffn(i):
                def one(f, n, it):
                    act.wait_ge(sem("ffn_gate_up"), it * 8 + (n + 1) if it is not None else n + 1)
                    act.activation(silu_f[:, f, :], ps[:, f, 0:N], ACT.Silu).then_inc(sem("ffn_silu"), 1)

                with act.Fori(0, FT // 8) as it:
                    for f in range(8):
                        one(f % 4, FT * i + f, it)
                for f in range(FT // 8 * 8, FT):
                    one(f % 4, FT * i + f, None)

            def lru():
                v = lambda name: vec2[:, columns(VEC2, name)]
                for o in range(RT):
                    act.wait_ge(sem("lru_gate_in"), o + 1)
                    act.activation(l_r[:, o, :], ps[:, 2 + o % 4, 0:N], ACT.Sigmoid, bias=v("b_a")[:, o:o + 1])\
                        .then_inc(sem("lru_gates"), 1)
                    act.activation(l_i[:, o, :], ps[:, 2 + o % 4, N:2 * N], ACT.Sigmoid, bias=v("b_x")[:, o:o + 1])\
                        .then_inc(sem("lru_gates"), 1)
                act.wait_ge(sem("lru_gates"), 2 * RT)
                act.wait_ge(sem("lru_rate"), 1)
                act.wait_ge(sem("lru_conv"), RT)
                for o in range(RT):
                    act.activation(l_a[:, o, :], l_r[:, o, :], ACT.Exp, scale=lru_s[5][:, o:o + 1])
                    act.activation(l_r[:, o, :], l_r[:, o, :], ACT.Tanh, scale=lru_s[4][:, o:o + 1])\
                        .then_inc(sem("lru_decay"), 1)
                for o in range(RT):
                    act.wait_ge(sem("lru_square"), o + 1)
                    act.activation(l_r[:, o, :], l_r[:, o, :], ACT.Sqrt, scale=2.0).then_inc(sem("lru_mult"), 1)
                for o in range(RT):
                    act.wait_ge(sem("lru_branch"), o + 1)
                    act.activation(l_gate[:, o, :], ps[:, (6 + o) % 8, 0:N], ACT.Gelu_apprx_tanh).then_inc(sem("lru_read_act"), 1)

            def ple(l):
                for d in range(KT):
                    act.wait_ge(sem("ple_products"), KT * l + d + 1)
                    if d >= 4:
                        act.wait_ge(sem("ple_added"), KT * l + d - 3)
                    act.activation(silu_f[:, d % 4, :], ps[:, 1 + d % 6, 0:N], ACT.Sigmoid).then_inc(sem("ple_gate"), 1)

            act.wait_ge(sem("setup_loaded"), 16 * 6)
            act.wait_ge(sem("cond_ready"), 1)
            act.activation(cond[:, :, 0:2], cond_in[:, :, :], ACT.Silu).then_inc(sem("cond_ready"), 1)
            act.wait_ge(sem("lru_abs"), 1)
            act.activation(lru_s[1][:, :], lru_s[0][:, :], ACT.Exp, scale=-1.0).then_inc(sem("lru_exp"), 1)
            act.wait_ge(sem("memsets"), 1)
            for l in range(LAYERS):
                norm_squares(act, 2 * l, ("moe_added", before("moe_added", l - 1), 1) if l else ("x_loaded", 31, KT))
                norm_act(act, 2 * l, rstd)
                if l == 0:
                    ada_group(0)
                norm_shift(act, 2 * l, mod[:, l, 0:KT, :])
                projection(l, (0, 1))
                act.wait_ge(sem("lam_sum"), l + 1)
                act.activation(lam_sum, lam_sum, ACT.Exp).then_inc(sem("lam_exp"), 1)
                qk_stats(l)
                projection(l, (2,))
                gate_stats(l)
                projection(l, (4,))
                read_qk_t(l, 0)
                if l == 0:
                    ada_group(1)
                read_fourier_uv(l)
                if l == 0:
                    ada_group(2)
                y_stats(l, 0)
                attention_c(l)
                read_qk_t(l, 1)
                if l == 0:
                    ada_group(3)
                y_stats(l, 1)
                attention_d(l)
                if l == 0:
                    ada_group(4)
                y_stats(l, 2)
                merge(l)
                if l == 0:
                    ada_group(5)
                norm_squares(act, 2 * l + 1, ("mix_added", before("mix_added", l), 1))
                norm_act(act, 2 * l + 1, rstd)
                norm_shift(act, 2 * l + 1, mod[:, l, 3 * KT:4 * KT, :])
                route(l)
                experts(l)
            for l in range(LAYERS):
                i = 4 + 4 * l
                norm_squares(act, i, ("ple_added", KT * (l - 1), 1) if l else ("moe_added", before("moe_added", 1), 1))
                norm_act(act, i, rstd2)
                ffn(2 * l)
                norm_squares(act, i + 1, ("ffn_added", 4 * 2 * l, 2))
                norm_act(act, i + 1, rstd2)
                if l == 0:
                    lru()
                norm_squares(act, i + 2, ("lru_added", 0, 2) if l == 0 else ("pool_added", 0, 1))
                norm_act(act, i + 2, rstd2)
                ffn(2 * l + 1)
                norm_squares(act, i + 3, ("ffn_added", 4 * (2 * l + 1), 2))
                norm_act(act, i + 3, rstd2)
                ple(l)
            norm_squares(act, 12, ("ple_added", KT * (LAYERS - 1), 1))
            norm_act(act, 12, rstd2)

        @block.vector
        def _(dve):
            count = [0]

            def link(ins):
                count[0] += 1
                ins.then_inc(sem("dve_chain"), 1)
                dve.wait_ge(sem("dve_chain"), count[0])

            def bc(ap, n):
                return bass.AP(ap.tensor, ap.offset, [list(x) for x in ap.ap] + [[0, n]])

            def bc_mid(ap, n):
                a = [list(x) for x in ap.ap]
                return bass.AP(ap.tensor, ap.offset, a[:-1] + [[0, n]] + a[-1:])

            def ada_group(step):
                l, i = divmod(step, 3)
                dve.wait_ge(sem("ada_turned"), step + 1)
                turned = ps[:, 7, :].rearrange("p (b j s) -> p j b s", b=4, j=4)[:, :, :, 0:2]
                bias = vec1[:, l, 16 * i:16 * i + 16].rearrange("p (j b) -> p j b", b=4)
                dst = mod[:, l, 16 * i:16 * i + 16, :].rearrange("p (j b) s -> p j b s", b=4)
                for s in range(2):
                    ins = dve.tensor_tensor(dst[:, :, :, s], turned[:, :, :, s], bias, ALU.add)
                    if s == 0:
                        link(ins)
                ins.then_inc(sem("ada_mod"), 1)
                dve.wait_ge(sem("ada_mod"), step + 1)

            def gains(l, which):
                dst, at, name = ((gain1, KT, "norm1_g"), (gain2, 4 * KT, "norm2_g"))[which]
                g = vec1[:, l, columns(VEC1, name)]
                link(dve.scalar_tensor_tensor(dst[:, :, :], mod[:, l, at:at + KT, :], 1.0, bc(g, 2), ALU.add, ALU.mult))

            def head_gains(l):
                lam_init = 0.8 - 0.6 * math.exp(-0.3 * l)
                hg = vec1[:, l, columns(VEC1, "head_out_g")][:, 4:6]
                dve.tensor_scalar(hg, hg, 1.0 - lam_init, None, ALU.mult).then_inc(sem("head_gain"), 1)
                dve.wait_ge(sem("head_gain"), l + 1)

            def row_constants(l):
                lam_init = 0.8 - 0.6 * math.exp(-0.3 * l)
                dve.wait_ge(sem("rows_loaded"), 32 + before("rows_loaded", l))
                for dst, table, name in ((rope_cos, "cos", "c_gain"), (rope_sin, "sin", "c_gain_swapped")):
                    t = const[:, columns(CONST, table)].rearrange("p (t d) -> p t d", t=4)
                    g = rows[:, columns(ROWS, name)].rearrange("p (w d) -> p w d", w=2)
                    for w in range(2):
                        gain = bc_mid(g[:, w, :], 4)
                        link(dve.tensor_tensor(dst[:, :, w, :], t, gain, ALU.mult))
                lam = rows[:, columns(ROWS, "lambda")].rearrange("p (a b d) -> p a b d", a=2, b=2)
                link(dve.tensor_tensor(lam_tmp.rearrange("p (a d) -> p a d", a=2), lam[:, :, 0, :], lam[:, :, 1, :], ALU.mult))
                dve.tensor_reduce(lam_sum, lam_tmp.rearrange("p (a d) -> p a d", a=2), AX, ALU.add).then_inc(sem("lam_sum"), 1)

            def lam_value(l):
                lam_init = 0.8 - 0.6 * math.exp(-0.3 * l)
                dve.wait_ge(sem("lam_exp"), l + 1)
                link(dve.tensor_tensor(neg_lam, lam_sum[:, 1:2], lam_sum[:, 0:1], ALU.subtract))
                link(dve.tensor_scalar(neg_lam, neg_lam, -lam_init, None, ALU.add))

            def projection(l):
                for j, (c, t, lo, width, engine) in enumerate(proj_jobs(l)):
                    if engine != "dve":
                        continue
                    dve.wait_ge(sem("proj_done"), j + 1 + before("proj_done", l))
                    dve.tensor_copy(vals[:, t, :], ps[:, j % 6, 0:width]).then_inc(sem("proj_read_dve"), 1)

            def group_sums(l, i, src, lo, n, width):
                dve.wait_ge(sem("mix_squares"), i + 1 + before("mix_squares", l))
                dve.tensor_reduce(mix_ss[:, lo:lo + n], src.rearrange("p (g d) -> p g d", d=width), AX, ALU.add)\
                    .then_inc(sem("mix_sums"), 1)

            def qk_norms(l):
                group_sums(l, 0, sq_c, 0, 64, DIFF)
                group_sums(l, 1, sq_d, 64, 32, HEAD)
                dve.wait_ge(sem("mix_std"), 2 + before("mix_std", l))
                link(dve.reciprocal(mix_ss[:, 0:96], mix_ss[:, 0:96]))
                for lo, groups, scale in ((0, 8, DIFF ** -0.5), (64, 4, HEAD ** -0.5)):
                    q = mix_ss[:, lo:lo + 8 * groups].rearrange("p (t w g) -> p t w g", t=4, w=2)[:, :, 0, :]
                    link(dve.tensor_scalar(q, q, scale, None, ALU.mult))
                c = qk_c.rearrange("p t f -> p (t f)").rearrange("p (g d) -> p g d", d=DIFF)
                dve.tensor_tensor(c, c, bc(mix_ss[:, 0:64], DIFF), ALU.mult).then_inc(sem("c_normed"), 1)
                dve.wait_ge(sem("c_normed"), 1 + before("c_normed", l))
                dve.wait_ge(sem("c_swapped"), 2 + before("c_swapped", l))
                sw = swapped.rearrange("p (t f) -> p t f", t=4)
                for t in range(4):
                    for src, table in ((qk_c[:, t, :], rope_cos), (sw[:, t, :], rope_sin)):
                        v = src.rearrange("p (w g d) -> p w g d", w=2, d=DIFF)
                        ins = dve.tensor_tensor(v, v, bc_mid(table[:, t, :, :], 8), ALU.mult)
                link(ins)
                c = qk_c.rearrange("p t f -> p (t f)")
                dve.tensor_tensor(c, c, swapped, ALU.add).then_inc(sem("qk_ready"), 1)
                d = qk_d.rearrange("p t f -> p (t f)").rearrange("p (g d) -> p g d", d=HEAD)
                link(dve.tensor_tensor(d, d, bc(mix_ss[:, 64:96], HEAD), ALU.mult))
                g = rows[:, columns(ROWS, "d_gain")].rearrange("p (w d) -> p w d", w=2)
                for t in range(4):
                    v = qk_d[:, t, :].rearrange("p (w h d) -> p w h d", w=2, d=HEAD)
                    ins = dve.tensor_tensor(v, v, bc_mid(g, HEADS), ALU.mult)
                ins.then_inc(sem("qk_ready"), 1)

            def gate_norm(l):
                tiles = 4 if l == 0 else 2
                group_sums(l, 2, sq_v[:, 0:GROUP * tiles], 96, 4 * tiles, HEAD)
                dve.wait_ge(sem("mix_std"), 3 + before("mix_std", l))
                link(dve.reciprocal(mix_ss[:, 96:96 + 4 * tiles], mix_ss[:, 96:96 + 4 * tiles]))
                for t in range(tiles):
                    v = gated[:, t, GROUP:2 * GROUP].rearrange("p (g d) -> p g d", d=HEAD)
                    ins = dve.tensor_tensor(v, v, bc(mix_ss[:, 96 + 4 * t:100 + 4 * t], HEAD), ALU.mult)
                ins.then_inc(sem("v_normed"), 1)

            def spatial_gating(l):
                tiles = 4 if l == 0 else 2
                dve.wait_ge(sem("sgu_mixed"), 1 + before("sgu_mixed", l))
                dve.wait_ge(sem("qk_ready"), 2 + before("qk_ready", l))
                b = vec1[:, l, columns(VEC1, "sgu_b")]
                for h in range(HEADS):
                    cols = slice(HEAD * h, HEAD * h + HEAD)
                    mixed = ps[:, 4 + h // 2, N * (h % 2):N * (h % 2) + HEAD * tiles].rearrange("p (t c) -> p t c", t=tiles)
                    ins = dve.scalar_tensor_tensor(ycat[:, 0:tiles, cols], mixed, b[:, h:h + 1], gated[:, 0:tiles, cols],
                                                   ALU.add, ALU.mult)
                ins.then_inc(sem("sgu_done"), 1)

            def read_fourier(l):
                for s in range(2 if l == 0 else 1):
                    dve.wait_ge(sem("fourier_done"), 2 * s + 2 + before("fourier_done", l))
                    dve.tensor_copy(ycat[:, 2 * s:2 * s + 2, GROUP:2 * GROUP],
                                    ps[:, 4 + s, :].rearrange("p (t f) -> p t f", t=2)).then_inc(sem("fourier_read"), 1)

            def read_qk_t(l, which):
                for b in (1, 3):
                    dve.wait_ge(sem("qk_turned"), 4 * which + b + 1 + before("qk_turned", l))
                    width = 512 if l == 0 or b >= 2 else N
                    dve.tensor_copy(qk_t[:, b, 0:width], ps[:, b, 0:width]).then_inc(sem("qk_t_dve"), 1)

            def attention_c(l):
                todo = units(l)

                def maxima(u):
                    width = keys(todo[u][0])[1]
                    for m in range(2):
                        i = 2 * u + m
                        dve.wait_ge(sem("c_scores"), i + 1 + before("c_scores", l))
                        dve.tensor_reduce(c_max[:, i:i + 1], ps[:, 2 * (u % 3) + m, 0:width], AX, ALU.max, negate=True)\
                            .then_inc(sem("c_max"), 1)

                def read_out(q):
                    dve.wait_ge(sem("c_pv"), HEADS * (q + 1) + before("c_pv", l))
                    dve.tensor_copy(ycat[:, q, 2 * GROUP:3 * GROUP], ps[:, 7, 0:GROUP]).then_inc(sem("c_out"), 1)

                for u in range(3):
                    maxima(u)
                for u, (q, h) in enumerate(todo):
                    width = keys(q)[1]
                    den = c_den[:, 2 * u:2 * u + 2]
                    dve.wait_ge(sem("c_exp"), 2 * u + 2 + before("c_exp", l))
                    link(dve.reciprocal(den, den))
                    link(dve.tensor_tensor(den[:, 1:2], den[:, 1:2], neg_lam, ALU.mult))
                    e0, e1 = (expo[:, 2 * (u % 3) + m, 0:width] for m in range(2))
                    link(dve.tensor_scalar(e1, e1, den[:, 1:2], None, ALU.mult))
                    dve.scalar_tensor_tensor(e0, e0, den[:, 0:1], e1, ALU.mult, ALU.add).then_inc(sem("c_weights"), 1)
                    if u + 3 < len(todo):
                        maxima(u + 3)
                    if h == 0 and q > 0:
                        read_out(q - 1)
                read_out(todo[-1][0])

            def attention_d(l):
                todo = units(l)

                def maximum(u):
                    width = keys(todo[u][0])[1]
                    dve.wait_ge(sem("d_scores"), u + 1 + before("d_scores", l))
                    dve.tensor_reduce(d_max[:, u:u + 1], ps[:, u % 3, 0:width], AX, ALU.max, negate=True)\
                        .then_inc(sem("d_max"), 1)

                maximum(0)
                maximum(1)
                for u, (q, h) in enumerate(todo):
                    if u + 2 < len(todo):
                        maximum(u + 2)
                    dve.wait_ge(sem("d_exp"), u + 1 + before("d_exp", l))
                    link(dve.reciprocal(d_den[:, u:u + 1], d_den[:, u:u + 1]))
                    dve.wait_ge(sem("d_pv"), u + 1 + before("d_pv", l))
                    dve.tensor_scalar(ycat[:, q, 3 * GROUP + HEAD * h:3 * GROUP + HEAD * h + HEAD],
                                      ps[:, (6, 3)[u % 2], 0:HEAD], d_den[:, u:u + 1], None, ALU.mult).then_inc(sem("d_out"), 1)

            def y_norm(l, piece):
                tiles = 4 if l == 0 else 2
                lo, heads, at = Y_PIECES[piece]
                dve.wait_ge(sem("y_squares"), piece + 1 + before("y_squares", l))
                ss = y_ss[:, at:at + heads * tiles]
                dve.tensor_reduce(ss, y_sq[:, 0:tiles * heads * HEAD].rearrange("p (g d) -> p g d", d=HEAD), AX, ALU.add)\
                    .then_inc(sem("y_sums"), 1)
                dve.wait_ge(sem("y_std"), piece + 1 + before("y_std", l))
                link(dve.reciprocal(ss, ss))
                for t in range(tiles):
                    y = ycat[:, t, lo:lo + heads * HEAD].rearrange("p (g d) -> p g d", d=HEAD)
                    ins = dve.tensor_tensor(y, y, bc(ss[:, heads * t:heads * t + heads], HEAD), ALU.mult)
                ins.then_inc(sem("y_normed"), 1)

            def merge(l):
                tiles = 4 if l == 0 else 2
                add_gated(l, "mix_out", "mix_added", 2 * KT, 6, 1, tiles // 2)

            def add_gated(l, produced, added, at, banks, first, streams):
                for d in range(KT):
                    dve.wait_ge(sem(produced), d + 1 + before(produced, l))
                    for s in range(streams):
                        x = x_res[:, d, N * s:N * s + N]
                        ins = dve.scalar_tensor_tensor(x, ps[:, first + d % banks, N * s:N * s + N],
                                                       mod[:, l, at + d, s:s + 1], x, ALU.mult, ALU.add)
                    ins.then_inc(sem(added), 1)

            def route(l):
                tiles = 4 if l == 0 else 2
                streams = tiles // 2
                rows_ = 48 if l == 0 else 16
                for j in range(1, 2 * tiles, 2):
                    dve.wait_ge(sem("h_turned"), j + 1 + before("h_turned", l))
                    dve.tensor_copy(h_tok[:, j // 2, 512:1024], ps[:, 1 + j % 4, :]).then_inc(sem("h_tok_dve"), 1)
                dve.wait_ge(sem("logits"), 1 + before("logits", l))
                raw = ps[:, 0, 0:EXPERTS * tiles].rearrange("p (t e) -> p t e", t=tiles)
                lg = logit[:, 0:EXPERTS * tiles].rearrange("p (t e) -> p t e", t=tiles)
                link(dve.tensor_reduce(r_max[:, 0:tiles], raw, AX, ALU.max))
                dve.tensor_tensor(lg, raw, bc(r_max[:, 0:tiles], EXPERTS), ALU.subtract).then_inc(sem("logits_shifted"), 1)
                dve.wait_ge(sem("logits_exp"), 1 + before("logits_exp", l))
                link(dve.tensor_reduce(r_sum[:, 0:tiles], lg, AX, ALU.add))
                link(dve.reciprocal(r_sum[:, 0:tiles], r_sum[:, 0:tiles]))
                dve.tensor_tensor(lg, lg, bc(r_sum[:, 0:tiles], EXPERTS), ALU.mult).then_inc(sem("aff"), 1)
                if l == 0:
                    link(dve.memset(aff_t[0:48, :], 0.0))
                dve.wait_ge(sem("aff_turned"), 1 + before("aff_turned", l))
                for s in range(streams):
                    link(dve.tensor_copy(aff_t[32 * s:32 * s + EXPERTS, :], ps[0:EXPERTS, 0, N * s:N * s + N]))
                src = aff_t
                for r in range(CAP // 8):
                    link(dve.max(top8[0:rows_, :], src[0:rows_, :]))
                    link(dve.match_replace(work[0:rows_, :], top8[0:rows_, :], src[0:rows_, :], -1.0))
                    src = work
                link(dve.tensor_scalar(sel[0:rows_, :], work[0:rows_, :], -1.0, None, ALU.is_equal))
                link(dve.tensor_scalar(work[0:rows_, :], work[0:rows_, :], 0.0, 1.0, ALU.mult, ALU.add))
                link(dve.tensor_tensor_scan(cum[0:rows_, :], work[0:rows_, :], sel[0:rows_, :], 0.0, ALU.mult, ALU.add))
                dve.tensor_tensor(slot_id[0:rows_, :], cum[0:rows_, :], sel[0:rows_, :], ALU.mult).then_inc(sem("slots"), 1)
                dve.wait_ge(sem("slots_turned"), 1 + before("slots_turned", l))
                turned = ps[:, 0, 0:96].rearrange("p (a r) -> p a r", a=2)
                for s in range(streams):
                    ins = dve.tensor_copy(slot_tokens[:, 2 * s:2 * s + 2, :], turned[:, :, 32 * s:32 * s + EXPERTS])
                    link(ins)
                for t in range(tiles):
                    ins = dve.tensor_tensor(gather[:, t, :, :], bc(slot_tokens[:, t, :], CAP), bc_mid(slot_row, EXPERTS),
                                            ALU.is_equal)
                ins.then_inc(sem("gather_ready"), 1)
                for s in range(streams):
                    dve.wait_ge(sem("slots_spread"), s + 1 + before("slots_spread", l))
                    dve.wait_ge(sem("aff_bc"), s + 1 + before("aff_bc", l))
                    for half in range(2):
                        dve.scalar_tensor_tensor(scatter[:, s, 2 * half:2 * half + 2, :].rearrange("p g t -> p (g t)"),
                                                 ps[:, 3 + half, :], slot_col, aff_bc[:, 512 * half:512 * half + 512],
                                                 ALU.is_equal, ALU.mult).then_inc(sem("scatter_ready"), 1)
                for j in range(1, KT * streams, 2):
                    s, k = divmod(j, KT)
                    dve.wait_ge(sem("gathered"), j + 1 + before("gathered", l))
                    dve.tensor_copy(picked_of(l)[:, k, :, CAP * s:CAP * s + CAP],
                                    ps[:, j % 6, :].rearrange("p (e s) -> p e s", e=EXPERTS)).then_inc(sem("picked_dve"), 1)

            def experts(l):
                m = 2 * CAP if l == 0 else CAP
                dve.wait_ge(sem("picked_act"), KT // 2 * (m // CAP) + before("picked_act", l))
                dve.wait_ge(sem("picked_dve"), KT // 2 * (m // CAP) + before("picked_dve", l))
                dve.wait_ge(sem("gathered"), KT * (m // CAP) + before("gathered", l))

                def tokens(e, j):
                    dst = x_exp[:, 512 * (j % 2):512 * (j % 2) + KT * m].rearrange("p (k m) -> p k m", k=KT)
                    dve.tensor_copy(dst, picked_of(l)[:, :, e, :]).then_inc(sem("x_exp"), 1)

                first = chunk_at["experts", l]
                with dve.Fori(0, EXPERTS // 4) as it:
                    tokens(it * 4, 0)
                    for j in range(4):
                        dve.wait_ge(sem("exp_silu"), it * 4 + (j + 1) + before("exp_silu", l))
                        dve.wait_ge(weights_used, it * 24 + (first + 6 * j + 4))
                        hid = hid_exp[0:2 * m, :]
                        dve.tensor_tensor(hid, hid, ps[0:2 * m, 1, :], ALU.mult).then_inc(sem("exp_hid"), 1)
                        if j < 3:
                            tokens(it * 4 + (j + 1), j + 1)
                        dve.wait_ge(weights_used, it * 24 + (first + 6 * j + 6))
                        for s in range(m // CAP):
                            o = (o_lat, o_ctx)[s]
                            ins = dve.tensor_copy(o[32 * j:32 * j + 32, it, 512:1024], ps[m + 32 * s:m + 32 * s + 32, 3, :])
                        ins.then_inc(sem("o_dve"), 1)

            def ffn(i):
                def one(f, n, it):
                    dve.wait_ge(sem("ffn_silu"), it * 8 + (n + 1) if it is not None else n + 1)
                    dve.tensor_tensor(hid_f[:, f, :], silu_f[:, f, :], ps[:, f, N:2 * N], ALU.mult).then_inc(sem("ffn_hid"), 1)

                with dve.Fori(0, FT // 8) as it:
                    for f in range(8):
                        one(f % 4, FT * i + f, it)
                for f in range(FT // 8 * 8, FT):
                    one(f % 4, FT * i + f, None)
                dve.wait_ge(weights_used, chunk_at["ffn", i] + FFN_CHUNKS)
                add_sums(0.5, "ffn_added")

            def add_sums(scale, added):
                for b in range(4):
                    x = x_res[:, 2 * b:2 * b + 2, 0:N]
                    dve.scalar_tensor_tensor(x, ps[:, 4 + b, :].rearrange("p (d t) -> p d t", d=2), scale, x,
                                             ALU.mult, ALU.add).then_inc(sem(added), 1)

            def softplus_rate():
                a = vec2[:, columns(VEC2, "a_param")]
                s = [t[:, :] for t in lru_s]
                link(dve.tensor_scalar(s[2], a, -1.0, None, ALU.mult))
                dve.tensor_tensor(s[0], a, s[2], ALU.max).then_inc(sem("lru_abs"), 1)
                link(dve.tensor_scalar(s[2], s[2], 0.0, None, ALU.max))
                dve.wait_ge(sem("lru_exp"), 1)
                link(dve.tensor_scalar(s[3], s[1], 2.0, None, ALU.add))
                link(dve.reciprocal(s[3], s[3]))
                link(dve.tensor_tensor(s[1], s[1], s[3], ALU.mult))
                link(dve.tensor_tensor(s[3], s[1], s[1], ALU.mult))
                link(dve.tensor_scalar(s[4], s[3], 1.0 / 17, None, ALU.mult))
                for c in range(15, 2, -2):
                    link(dve.scalar_tensor_tensor(s[4], s[4], 1.0 / c, s[3], ALU.add, ALU.mult))
                link(dve.scalar_tensor_tensor(s[4], s[4], 1.0, s[1], ALU.add, ALU.mult))
                link(dve.scalar_tensor_tensor(s[4], s[4], 2.0, s[2], ALU.mult, ALU.add))
                link(dve.tensor_scalar(s[4], s[4], 8.0, None, ALU.mult))
                dve.tensor_scalar(s[5], s[4], -1.0, None, ALU.mult).then_inc(sem("lru_rate"), 1)

            def lru():
                v = lambda name: vec2[:, columns(VEC2, name)]
                link(dve.memset(l_pad[:, :, 0:CONV - 1], 0.0))
                w = v("conv_w")
                for o in range(RT):
                    dve.wait_ge(sem("lru_in"), o + 1)
                    dve.tensor_copy(l_pad[:, o, CONV - 1:CONV - 1 + N], ps[:, o % 8, 0:N]).then_inc(sem("lru_read_dve"), 1)
                    dve.wait_ge(sem("lru_read_dve"), o + 1)
                    link(dve.tensor_scalar(l_x[:, o, :], l_pad[:, o, 0:N], w[:, o:o + 1], v("conv_b")[:, o:o + 1],
                                           ALU.mult, ALU.add))
                    for tap in range(1, CONV):
                        ins = dve.scalar_tensor_tensor(l_x[:, o, :], l_pad[:, o, tap:tap + N], w[:, RT * tap + o:RT * tap + o + 1],
                                                       l_x[:, o, :], ALU.mult, ALU.add)
                        if tap < CONV - 1:
                            link(ins)
                    ins.then_inc(sem("lru_conv"), 1)
                for o in range(RT):
                    dve.wait_ge(sem("lru_gates"), 2 * o + 2)
                    ins = dve.tensor_tensor(l_i[:, o, :], l_i[:, o, :], l_x[:, o, :], ALU.mult)
                link(ins)
                dve.wait_ge(sem("lru_gate_in"), RT)
                for o in range(RT):
                    dve.wait_ge(sem("lru_decay"), o + 1)
                    link(dve.tensor_scalar(l_x[:, o, :], l_r[:, o, :], 1.0, None, ALU.add))
                    link(dve.reciprocal(l_x[:, o, :], l_x[:, o, :]))
                    dve.tensor_tensor(l_r[:, o, :], l_r[:, o, :], l_x[:, o, :], ALU.mult).then_inc(sem("lru_square"), 1)
                for o in range(RT):
                    dve.wait_ge(sem("lru_mult"), o + 1)
                    link(dve.tensor_tensor(l_i[:, o, :], l_i[:, o, :], l_r[:, o, :], ALU.mult))
                    ins = dve.tensor_tensor_scan(l_x[:, o, :], l_a[:, o, :], l_i[:, o, :], 0.0, ALU.mult, ALU.add)
                link(ins)
                for o in range(RT):
                    dve.wait_ge(sem("lru_read_act"), o + 1)
                    dve.tensor_tensor(l_gate[:, o, :], l_gate[:, o, :], l_x[:, o, :], ALU.mult).then_inc(sem("lru_y"), 1)
                dve.wait_ge(weights_used, chunk_at["lru", 0] + 11)
                add_sums(1.0, "lru_added")

            def pooling():
                norm = h_buf
                norm_ready(dve, 9)
                dve.wait_ge(sem("pool_inv_loaded"), 16)
                src = norm[:, :, 0:N]
                for g, win in enumerate(POOLS):
                    lo = 2 * g
                    back = win // 2
                    dst = (pool_a, pool_b)[g % 2]
                    link(dve.tensor_copy(dst[:, lo:KT, 0:back], src[:, lo:KT, 0:back]))
                    link(dve.tensor_tensor(dst[:, lo:KT, back:N], src[:, lo:KT, back:N], src[:, lo:KT, 0:N - back], ALU.add))
                    inv = bc_mid(pool_inv[:, g, :], 2)
                    link(dve.tensor_tensor(pool_u[:, lo:lo + 2, :], dst[:, lo:lo + 2, :], inv, ALU.mult))
                    src = dst
                dve.tensor_tensor(pool_u, pool_u, norm[:, :, 0:N], ALU.subtract).then_inc(sem("pool_ready"), 1)
                b, s = (vec2[:, columns(VEC2, n)] for n in ("pool_b", "pool_scale"))
                for d in range(KT):
                    dve.wait_ge(sem("pool_mapped"), d // 2 + 1)
                    y = pool_a[:, d, :]
                    link(dve.tensor_scalar(y, ps[:, 4 + d // 2, N * (d % 2):N * (d % 2) + N], b[:, d:d + 1], s[:, d:d + 1],
                                           ALU.add, ALU.mult))
                    x = x_res[:, d, 0:N]
                    dve.tensor_tensor(x, x, y, ALU.add).then_inc(sem("pool_added"), 1)

            def ple(l):
                for d in range(KT):
                    dve.wait_ge(sem("ple_gate"), KT * l + d + 1)
                    y = hid_f[:, d % 4, :]
                    link(dve.tensor_tensor(y, silu_f[:, d % 4, :], ps[:, 1 + d % 6, N:2 * N], ALU.mult))
                    x = x_res[:, d, 0:N]
                    dve.tensor_tensor(x, x, y, ALU.add).then_inc(sem("ple_added"), 1)

            link(dve.memset(mean_w[:, :], 1.0 / D))
            link(dve.memset(eps_col[:, :], EPS))
            dve.memset(cond[:, :, :], 0.0).then_inc(sem("cond_ready"), 1)
            dve.memset(zeros[:, :], 0.0).then_inc(sem("memsets"), 1)
            dve.wait_ge(sem("setup_loaded"), 16 * 6)
            softplus_rate()
            for l in range(LAYERS):
                if l == 0:
                    ada_group(0)
                gains(l, 0)
                norm_dve(dve, link, 2 * l, rstd, lambda k, s: gain1[:, k, s:s + 1])
                head_gains(l)
                row_constants(l)
                qk_norms(l)
                gate_norm(l)
                projection(l)
                lam_value(l)
                read_qk_t(l, 0)
                spatial_gating(l)
                if l == 0:
                    ada_group(1)
                read_fourier(l)
                if l == 0:
                    ada_group(2)
                y_norm(l, 0)
                attention_c(l)
                read_qk_t(l, 1)
                if l == 0:
                    ada_group(3)
                y_norm(l, 1)
                attention_d(l)
                if l == 0:
                    ada_group(4)
                y_norm(l, 2)
                merge(l)
                if l == 0:
                    ada_group(5)
                gains(l, 1)
                norm_dve(dve, link, 2 * l + 1, rstd, lambda k, s: gain2[:, k, s:s + 1])
                route(l)
                experts(l)
                add_gated(l, "moe_out", "moe_added", 5 * KT, 4, 4, 2 if l == 0 else 1)
            for l in range(LAYERS):
                i = 4 + 4 * l

                def gain(name, l=l):
                    g = vec2[:, columns(VEC2, name)]
                    return lambda k, s: g[:, KT * l + k:KT * l + k + 1]

                norm_dve(dve, link, i, rstd2, gain("ffn1_norm"))
                ffn(2 * l)
                norm_dve(dve, link, i + 1, rstd2, gain("mix_norm"))
                if l == 0:
                    lru()
                else:
                    pooling()
                norm_dve(dve, link, i + 2, rstd2, gain("ffn2_norm"))
                ffn(2 * l + 1)
                norm_dve(dve, link, i + 3, rstd2, gain("ple_norm"))
                ple(l)
            final = vec2[:, columns(VEC2, "final_norm")]
            norm_dve(dve, link, 12, rstd2, lambda k, s: final[:, k:k + 1])


def host_constants():
    f = np.float32
    tok = np.arange(N)
    const = {
        "ident": np.eye(P, dtype=f),
        "slot_row": np.broadcast_to(np.arange(1, CAP + 1, dtype=f), (P, CAP)),
        "slot_col": (np.arange(P) % CAP + 1).astype(f)[:, None],
    }
    const["band_c"] = np.kron(np.eye(P // DIFF), np.ones((DIFF, 1)))
    const["band_d"] = np.kron(np.eye(P // HEAD), np.ones((HEAD, 1)))
    half = DIFF // 2
    inv = (1.0 / (10000.0 ** (np.arange(0, half, 2, dtype=f) / f(half)))).astype(f)
    row, col = ((a.astype(f)[:, None] * inv).astype(f) for a in (tok // GRID_W, tok % GRID_W))
    cos = np.concatenate([np.cos(row), np.cos(row), np.cos(col), np.cos(col)], 1).astype(f)
    sin = np.concatenate([-np.sin(row), np.sin(row), -np.sin(col), np.sin(col)], 1).astype(f)
    cos = np.concatenate([cos, np.ones_like(cos)]).reshape(4, P, DIFF)
    sin = np.concatenate([sin, np.zeros_like(sin)]).reshape(4, P, DIFF)
    const["cos"] = cos.transpose(1, 0, 2).reshape(P, 4 * DIFF)
    const["sin"] = sin.transpose(1, 0, 2).reshape(P, 4 * DIFF)
    q, k = np.arange(P) % GRID_W, tok % GRID_W
    start = np.clip(q - NA_COLS // 2, 0, GRID_W - NA_COLS)
    inside = (k[None] >= start[:, None]) & (k[None] < start[:, None] + NA_COLS)
    turn = 2 * np.pi * np.outer(tok, tok) / N
    scale = 1.0 / math.sqrt(N * HEAD)
    turn_d = 2 * np.pi * np.outer(np.arange(HEAD), np.arange(HEAD)) / HEAD
    two = np.eye(P // HEAD)

    def on_partitions(a):
        return a.reshape(2, P, N).transpose(1, 0, 2).reshape(P, 2 * N)

    att = {
        "mask": np.where(inside, 0.0, NEG),
        "cos_n": on_partitions(np.cos(turn) * scale),
        "sin_n": on_partitions(-np.sin(turn) * scale),
        "cs_d": np.concatenate([np.kron(two, np.cos(turn_d)), np.kron(two, np.sin(turn_d))], 1),
    }
    expand = np.zeros((48, 4, 4, CAP), f)
    for e in range(EXPERTS):
        expand[e, e // 4, e % 4] = expand[32 + e, e // 4, e % 4] = 1
    count = np.stack([1.0 / np.minimum(tok + 1, w).astype(f) for w in POOLS]).astype(f)

    def packed(parts, widths):
        return np.ascontiguousarray(np.concatenate([parts[n] for n in widths], 1).astype(f))

    return {
        "const": packed(const, CONST), "att": packed(att, ATT),
        "expand": np.ascontiguousarray(expand.reshape(48, 512)),
        "pool_inv": np.ascontiguousarray(np.broadcast_to(count.reshape(1, -1), (P, 4 * N))),
    }


def host_layout(a):
    def feat(v):
        return v.reshape(-1, P).T

    vec1 = np.stack([np.concatenate([feat(a["ada_b"][l]), feat(a["norm1_g"][l]), feat(a["norm2_g"][l]),
                                     feat(a["head_out_g"][l]), a["sgu_b"][l].T], 1) for l in range(LAYERS)], 1)
    both = [np.concatenate([feat(a[n + "_2"][l]) for l in range(LAYERS)], 1)
            for n in ("ffn1_norm", "mix_norm", "ffn2_norm", "ple_norm")]
    vec2 = np.concatenate(both + [
        feat(a["lru_conv_w_2"][0].reshape(-1)), feat(a["lru_conv_b_2"][0]), feat(a["lru_b_a_2"][0]), feat(a["lru_b_x_2"][0]),
        feat(a["lru_a_param_2"][0]), feat(a["pool_b_2"][0]), feat(a["pool_scale_2"][0]), feat(a["final_norm_2"])], 1)
    partner = np.arange(DIFF).reshape(2, 2, 8)[:, ::-1].reshape(-1)
    qg, kg = a["diff_qn_g"], a["diff_kn_g"]
    rows = np.concatenate([qg, kg, qg[:, partner], kg[:, partner], a["na_qn_g"], a["na_kn_g"],
                           a["diff_lambda"].reshape(LAYERS, -1)], 1)

    def blocks(w):
        full = np.zeros((D_RNN, D_RNN), w.dtype)
        for h in range(D_RNN // LRU_HEAD):
            at = slice(h * LRU_HEAD, (h + 1) * LRU_HEAD)
            full[at, at] = w[h]
        return np.concatenate([full[k * P:k * P + P, o * P:o * P + P] for o, k in PAIRS], 1)

    row, col = np.divmod(np.arange(N), GRID_W)
    row_off = row[None] - row[:, None] + NA_ROWS - 1
    col_off = np.clip(col[None] - col[:, None], 1 - NA_COLS, NA_COLS - 1) + NA_COLS - 1
    rel_bias = a["na_rpb"][:, :, row_off, col_off].reshape(LAYERS, HEADS, 2, P, N).transpose(0, 3, 2, 1, 4)
    cond = np.stack([a["c"][0], a["c_ctx"]]).reshape(2, KT, P).transpose(2, 1, 0)
    router = a["router_w"].reshape(LAYERS, KT, P, EXPERTS).transpose(2, 0, 1, 3).reshape(P, -1)
    return {
        "x_t": a["x"][0].T, "ctx_t": a["ctx"][0].T, "cond_t": cond, "vec1": vec1, "vec2": vec2,
        "rows": np.broadcast_to(rows[:, None, :], (LAYERS, P, ROWS_W)), "router": router,
        "sgu_t": a["sgu_w"].transpose(0, 3, 1, 2), "rel_bias": rel_bias,
        "ada_w": a["ada_w"], "w_in": a["w_in"], "w_out": a["w_out"],
        "exp_gate": a["exp_w_gate"], "exp_up": a["exp_w_up"], "exp_down": a["exp_w_down"],
        "ffn1_gate": a["ffn1_w_gate_2"], "ffn1_up": a["ffn1_w_up_2"], "ffn1_down": a["ffn1_w_down_2"],
        "ffn2_gate": a["ffn2_w_gate_2"], "ffn2_up": a["ffn2_w_up_2"], "ffn2_down": a["ffn2_w_down_2"],
        "lru_in": a["lru_w_in_2"][0], "lru_a": blocks(a["lru_w_a_2"][0]), "lru_x": blocks(a["lru_w_x_2"][0]),
        "lru_out": a["lru_w_out_2"][0], "pool_w": a["pool_w_2"][0].reshape(D, GROUP),
        "ple_gate": a["ple_w_gate_2"], "ple_proj": a["ple_w_proj_2"], "p_t": a["p_2"][:, 0].transpose(0, 2, 1),
    }


def kernel(**inputs):
    import concourse.bacc as bacc
    from concourse.bass_utils import run_bass_kernel_spmd

    nc = bacc.Bacc("TRN2", target_bir_lowering=False, num_devices=1)
    arrays = {**host_layout({k: np.asarray(v) for k, v in inputs.items()}), **host_constants()}
    arrays = {f"in_{k}": np.ascontiguousarray(v) for k, v in arrays.items()}
    dram = {k[3:]: nc.dram_tensor(k, v.shape, F32, kind="ExternalInput").ap() for k, v in arrays.items()}
    out_t = nc.dram_tensor("out_t", (D, N), F32, kind="ExternalOutput").ap()
    build(nc, dram, out_t)
    r = run_bass_kernel_spmd(nc, [arrays], core_ids=[0])
    return np.ascontiguousarray(r.results[0]["out_t"].T)[None]
```

```python
from contextlib import ExitStack
import math

import numpy as np

import concourse.bass as bass
from concourse import mybir

F32 = mybir.dt.float32
F32R = mybir.dt.float32r
BF16 = mybir.dt.bfloat16
ALU = mybir.AluOpType
ACT = mybir.ActivationFunctionType
AX = mybir.AxisListType.X

P = 128
D = 1024
KT = D // P
N = 256
LAYERS = 2
POOL_NORM, LAST_NORM = 2 * LAYERS + 4 + 1, 2 * LAYERS + 4 * LAYERS
EPS = 1e-6
HEADS, HEAD = 4, 64
GROUP = HEADS * HEAD
DIFF = HEAD // 2
GRID_W = 64
NA_ROWS, NA_COLS = 8, 16
EXPERTS = 16
CAP = 2 * N // EXPERTS
D_FF = 11 * D // 4
FT = D_FF // P
D_RNN = 5 * D // 4
RT = D_RNN // P
LRU_HEAD = D_RNN // 16
CONV = 4
POOLS = (2, 4, 8, 16)
NEG = -1e30

SLOTS = 6
SLOT = 4096

VEC1 = {"ada_b": 48, "norm1_g": 8, "norm2_g": 8, "head_out_g": 8, "sgu_b": 4}
VEC1_W = sum(VEC1.values())
VEC2 = {"ffn1_norm": 16, "mix_norm": 16, "ffn2_norm": 16, "ple_norm": 16, "conv_w": 40, "conv_b": 10,
        "b_a": 10, "b_x": 10, "a_param": 10, "pool_b": 8, "pool_scale": 8, "final_norm": 8}
VEC2_W = sum(VEC2.values())
ROWS = {"c_gain": 2 * DIFF, "c_gain_swapped": 2 * DIFF, "d_gain": 2 * HEAD, "lambda": 4 * DIFF}
ROWS_W = sum(ROWS.values())
CONST = {"ident": P, "slot_row": CAP, "slot_col": 1, "band_c": P // DIFF, "band_d": P // HEAD, "cos": 4 * DIFF, "sin": 4 * DIFF}
CONST_W = sum(CONST.values())
ATT = {"cs_d": 2 * P, "cos_n": 2 * N, "sin_n": 2 * N, "mask": N}
ATT_W = sum(ATT.values())


def columns(parts, name):
    at = 0
    for key, width in parts.items():
        if key == name:
            return slice(at, at + width)
        at += width
    raise KeyError(name)


def lru_pairs():
    out = []
    for o in range(RT):
        first = o * P // LRU_HEAD * LRU_HEAD
        last = (o * P + P - 1) // LRU_HEAD * LRU_HEAD + LRU_HEAD - 1
        out += [(o, k) for k in range(first // P, last // P + 1)]
    return out


PAIRS = lru_pairs()

COUNTS = {
    "rows_loaded": 32, "cs_loaded": 16, "att_loaded": 16, "rel_bias_loaded": 16,
    "proj_done": 18, "proj_read_act": 14, "proj_read_dve": 4, "bias_ready": 1,
    "mix_squares": 3, "mix_sums": 3, "mix_std": 3, "c_normed": 1, "c_swapped": 2, "v_normed": 1, "qk_ready": 2,
    "qk_turned": 8, "qk_t_act": 4, "qk_t_dve": 4, "sgu_mixed": 1, "sgu_done": 1,
    "fourier_uv": 4, "uv_ready": 4, "fourier_done": 4, "fourier_read": 2,
    "c_bands": 16, "d_bands": 16, "c_scores": 32, "c_max": 32, "c_exp": 32, "c_weights": 16, "c_turned": 16, "c_wt": 16, "c_pv": 16, "c_out": 4,
    "d_scores": 16, "d_max": 16, "d_exp": 16, "d_turned": 16, "d_wt": 16, "d_pv": 16, "d_out": 16,
    "y_squares": 4, "y_sums": 4, "y_std": 4, "y_normed": 4, "y_turned": 8, "y_t": 8, "y_rest": 8, "mix_out": 8, "mix_added": 8,
    "logits": 1, "logits_copied": 1, "logits_turned": 1, "logits_shifted": 1, "logits_exp": 1,
    "h_turned": 8, "h_tok_lead": 8, "h_tok_rest": 8,
    "aff": 1, "aff_turned": 1, "slots": 1, "slots_turned": 1, "spread_rows": 2, "spread": 2, "aff_copied": 2,
    "gather_ready": 1, "scatter_ready": 2, "gathered": 16, "picked_act": 8, "picked_dve": 8,
    "x_exp": 16, "exp_silu": 16, "exp_hid": 16, "exp_turned": 16, "exp_hid_t": 16, "o_act": 16, "o_dve": 16,
    "moe_out": 8, "moe_added": 8,
}


def before(name, layer):
    return COUNTS[name] * layer


def proj_jobs(layer):
    tiles = range(4)
    own = range(4) if layer == 0 else range(2)
    jobs = [(0, t, 0, 512, "act") if t in own else (0, t, 256, 256, "act") for t in tiles]
    jobs += [(1, t, 0, 512, "act") if t in own else (1, t, 256, 256, "act") for t in tiles]
    jobs += [(2, t, 0, 512, "act") for t in own]
    jobs += [(3, t, 0, 512, "dve") for t in tiles]
    jobs += [(4, c, 0, P, "act") for c in range(2)]
    return jobs


def build(nc, dram, out_t):
    ctx = ExitStack()
    with ctx:
        def sb(name, shape, dt=F32):
            return ctx.enter_context(nc.sbuf_tensor(name, shape, dt))

        sems = {}

        def sem(name):
            if name not in sems:
                sems[name] = ctx.enter_context(nc.semaphore(name))
            return sems[name]

        def large(stack, suffix, dt):
            return [stack.enter_context(nc.sbuf_tensor(name + suffix, shape, dt)) for name, shape in (
                ("ring", [P, SLOTS, SLOT]), ("h_buf", [P, KT, 2 * N]), ("arena", [P, 16384]))]

        with ExitStack() as first:
            ring, h_buf, arena = large(first, "", F32)
        ring_r, h_buf_r, arena_r = large(ctx, "_r", F32R)
        x_res = sb("x_res", [P, KT, 2 * N])
        const = sb("const", [P, CONST_W])
        vec1 = sb("vec1", [P, LAYERS, VEC1_W])
        vec2 = sb("vec2", [P, VEC2_W])
        rows = sb("rows", [P, ROWS_W])
        router_sb = sb("router_sb", [P, LAYERS, KT, EXPERTS])
        cond_in = sb("cond_in", [P, KT, 2])
        cond = sb("cond", [P, KT, 32])
        mod = sb("mod", [P, LAYERS, 48, 2])
        gain1 = sb("gain1", [P, KT, 2])
        gain2 = sb("gain2", [P, KT, 2])
        rope_cos = sb("rope_cos", [P, 4, 2, DIFF])
        rope_sin = sb("rope_sin", [P, 4, 2, DIFF])
        mean_w = sb("mean_w", [P, P])
        zeros = sb("zeros", [P, 512], BF16)
        eps_col = sb("eps_col", [P, 1])
        small = sb("small", [P, 512])
        expand = sb("expand", [64, 4 * P], F32R)
        ps = ctx.enter_context(nc.psum_tensor("ps", [P, 8, 512], F32))

        def part(lo, hi):
            return arena[:, lo:hi]

        ycat = part(0, 4096).rearrange("p (t f) -> p t f", t=4)
        gated = part(4096, 6144).rearrange("p (t f) -> p t f", t=4)
        uv = part(4096, 6144).rearrange("p (t c w f) -> p t c w f", t=4, c=2, w=2)
        qk_c = part(6144, 8192).rearrange("p (t f) -> p t f", t=4)
        expo = part(4096, 7168).rearrange("p (b f) -> p b f", b=6)
        q_band = part(7168, 8192).rearrange("p (b f) -> p b f", b=8)
        qk_d = part(8192, 10240).rearrange("p (t f) -> p t f", t=4)
        vals = part(10240, 12288).rearrange("p (t f) -> p t f", t=4)
        fourier_in = part(12288, 13312).rearrange("p (c f) -> p c f", c=2)
        w_t = part(12288, 13312).rearrange("p (b k f) -> p b k f", b=2, k=4)
        qk_t = part(13312, 15360).rearrange("p (b f) -> p b f", b=4)
        sgu_t = part(15360, 15872).rearrange("p (h f) -> p h f", h=HEADS)

        def ada_rows(step):
            return part(15872, 16384) if step < 5 else part(5120, 5632)

        sq_c = sq_d = sq_v = swapped = part(13312, 15360)
        rstd = part(4096, 4608)
        in_lead, out_lead = h_buf_r, h_buf_r
        in_exact = part(0, 4096).rearrange("p (k t) -> p k t", k=KT)
        in_rest, out_rest = (arena_r[:, a:a + 4096].rearrange("p (k t) -> p k t", k=KT) for a in (0, 4096))
        h_flat = h_buf[:, :, :].rearrange("p k t -> p (k t)")
        rel_bias = h_flat[:, 0:2048].rearrange("p (q h f) -> p q h f", q=2, h=HEADS)
        att = h_flat[:, 2048:2048 + ATT_W]
        y_sq = att[:, columns(ATT, "cos_n").start:columns(ATT, "sin_n").stop]
        logits_t = part(2560, 3072)
        aff_t, work, slot_id, cum = (h_flat[:, a:a + N] for a in range(2048, 3072, N))
        h_flat_r = h_buf_r[:, :, :].rearrange("p k t -> p (k t)")
        spread_rows = h_flat_r[:, 3072:4096].rearrange("p (s w t) -> p s w t", s=2, w=2)
        aff_bc = part(8192, 9216).rearrange("p (g t) -> p g t", g=4)
        expand_in = part(8192, 8704)[0:64, :]
        h_tok = arena_r[:, 8192:12288].rearrange("p (t f) -> p t f", t=4)
        h_tok_rest = [a.rearrange("p (t f) -> p t f", t=4) for a in (arena_r[:, 12288:14336], h_flat_r[:, 0:2048])]
        o_lat = part(8192, 12288).rearrange("p (g f) -> p g f", g=4)
        o_ctx = h_flat.rearrange("p (g f) -> p g f", g=4)
        scatter = part(12288, 14336).rearrange("p (s g t) -> p s g t", s=2, g=4)
        gather = arena_r[:, 14336:16384].rearrange("p (t e s) -> p t e s", t=4, e=EXPERTS)
        x_exp = part(14336, 15360)
        hid_exp = part(15360, 15872)
        hid_exp_t = part(15872, 16384)
        h_lead, h_rest = h_buf_r[:, :, 0:N], h_buf_r[:, :, N:2 * N]
        rstd2 = part(0, 256)
        silu_f = part(512, 1536).rearrange("p (f t) -> p f t", f=4)
        hid_f = part(1536, 2560).rearrange("p (f t) -> p f t", f=4)
        hid_lead, hid_rest = (arena_r[:, a:a + 1024].rearrange("p (f t) -> p f t", f=4) for a in (512, 1536))
        l_gate = part(2560, 5120).rearrange("p (o t) -> p o t", o=RT)
        l_pad = part(5120, 5120 + RT * 260).rearrange("p (o t) -> p o t", o=RT)
        l_a = part(5120, 7680).rearrange("p (o t) -> p o t", o=RT)
        l_x = part(7760, 10320).rearrange("p (o t) -> p o t", o=RT)
        l_r = part(10320, 12880).rearrange("p (o t) -> p o t", o=RT)
        l_i = part(12880, 15440).rearrange("p (o t) -> p o t", o=RT)
        y_lead, y_rest = (arena_r[:, a:a + RT * N].rearrange("p (o t) -> p o t", o=RT) for a in (12880, 2560))
        pool_a = part(2560, 4608).rearrange("p (k t) -> p k t", k=KT)
        pool_b = part(4608, 6656).rearrange("p (k t) -> p k t", k=KT)
        pool_u = part(6656, 8704).rearrange("p (k t) -> p k t", k=KT)
        pool_y = part(9728, 11776).rearrange("p (k t) -> p k t", k=KT)
        pool_inv = part(8704, 9728).rearrange("p (g t) -> p g t", g=4)

        ident = const[:, columns(CONST, "ident")]
        slot_row = const[:, columns(CONST, "slot_row")]
        slot_col = const[:, columns(CONST, "slot_col")]

        mix_ss = small[:, 0:112]
        c_max, c_den = small[:, 112:144], small[:, 144:176]
        d_max, d_den = small[:, 176:192], small[:, 192:208]
        y_ss = small[:, 208:272]
        logit = small[:, 320:384]
        Y_PIECES = [(GROUP * i, HEADS, 4 * HEADS * i) for i in range(4)]
        r_max, r_sum = small[:, 384:388], small[:, 388:392]
        lam_tmp = small[:, 392:456]
        lam_sum, neg_lam = small[:, 456:458], small[:, 458:459]
        pool_bias = small[:, 460:468]
        lru_s = [sb(f"lru_s{i}", [P, RT]) for i in range(6)]
        slot_tokens = sb("slot_tokens", [P, 4, EXPERTS])
        top8 = sb("top8", [P, 8])

        def picked_of(l):
            m = 2 * CAP if l == 0 else CAP
            return part(0, KT * EXPERTS * m).rearrange("p (k e m) -> p k e m", k=KT, e=EXPERTS)

        norms = []
        for l in range(LAYERS):
            norms += [(2 * N, 2, False), (2 * N, 2, True) if l == 0 else (N, 1, True)]
        norms += [(N, 1, False)] * (4 * LAYERS + 1)

        def in_halves(i):
            return i >= 2 * LAYERS and i not in (POOL_NORM, LAST_NORM)

        scaled_before = [sum(KT * s for j, (_, s, _) in enumerate(norms[:i]) if not in_halves(j))
                         for i in range(len(norms) + 1)]
        shifted_before = [sum(KT * s for _, s, sh in norms[:i] if sh) for i in range(len(norms) + 1)]
        NORM_END = scaled_before[-1]

        weights_used = sem("weights_used")
        slot_loaded = [sem(f"slot_loaded{i}") for i in range(SLOTS)]
        chunk_at = {}
        loads, halved = [], []

        def stream(key, *chunks):
            chunk_at[key] = len(loads)
            for dmas, floats in chunks:
                loads.append(dmas)
                halved.append(floats)

        PLAIN, HALVED = (1, 0), (1, SLOT)
        for l in range(LAYERS):
            if l == 0:
                stream(("ada", 0), *[PLAIN] * 4)
            stream(("w_in", l), HALVED, HALVED, HALVED, (2, SLOT), (1, KT * GROUP))
            if l == 0:
                for step in range(1, 5):
                    stream(("ada", step), *[PLAIN] * 4)
            stream(("w_out", l), HALVED, HALVED)
            if l == 0:
                stream(("ada", 5), *[PLAIN] * 4)
            stream(("experts", l), *[PLAIN] * 6 * EXPERTS)
        GROUPS = [min(4, FT - f) for f in range(0, FT, 4)]
        FFN_CHUNKS = [(1, D * g) for g in GROUPS[:-1] for _ in range(3)] + [(2, 2 * D * GROUPS[-1]), (1, D * GROUPS[-1])]
        FFN_BANKS = 2 * len(GROUPS)
        RNN_PARTS = [min(4, RT - o) for o in range(0, RT, 4)]
        for l in range(LAYERS):
            stream(("ffn", 2 * l), *FFN_CHUNKS)
            if l == 0:
                parts = [(1, D * o) for o in RNN_PARTS]
                stream(("lru", 0), *parts, PLAIN, PLAIN, *parts, *parts)
            else:
                stream(("pool", 0), PLAIN)
            stream(("ffn", 2 * l + 1), *FFN_CHUNKS)
            stream(("ple", l), HALVED, (2, 2 * D + 2 * N), HALVED)

        slot_of, rest_of = [], []
        slot_free, rest_free = [], []
        halved_before = []
        last_user, at = {}, 0
        for n, floats in enumerate(halved):
            halved_before.append(sum(f > 0 for f in halved[:n]))
            slots = [at % SLOTS, (at + 1) % SLOTS][:2 if floats else 1]
            at += len(slots)
            slot_of.append(slots[0])
            rest_of.append(slots[-1])
            slot_free.append(last_user.get(slots[0], -1) + 1)
            rest_free.append(last_user.get(slots[-1], -1) + 1)
            last_user.update({i: n for i in slots})

        def slot(n):
            return ring[:, slot_of[n], :]

        def halves(n):
            return ring_r[:, rest_of[n], :], ring_r[:, slot_of[n], :]

        def loaded_value(n):
            return 16 * sum(d for d, i in zip(loads[:n + 1], slot_of) if i == slot_of[n])

        def halve_lead(act, n, it=None):
            per_load, per_chunk = (32 * it, 6 * it) if it is not None else (0, 0)
            free = max(rest_free[n], n - 2) if it is not None else rest_free[n]
            act.wait_ge(slot_loaded[slot_of[n]], per_load + loaded_value(n))
            act.wait_ge(weights_used, per_chunk + free)
            act.activation(halves(n)[0][:, 0:halved[n]], slot(n)[:, 0:halved[n]], ACT.Copy).then_inc(sem("chunk_lead"), 1)

        def halve_rest(dve, n, it=None):
            per_chunk = 6 * it if it is not None else 0
            dve.wait_ge(sem("chunk_lead"), per_chunk + (halved_before[n] + 1))
            lead, rest = (a[:, 0:halved[n]] for a in halves(n))
            dve.tensor_tensor(rest, slot(n)[:, 0:halved[n]], lead, ALU.subtract).then_inc(sem("chunk_halved"), 1)

        def units(l):
            return [(q, h) for q in (range(4) if l == 0 else range(2)) for h in range(HEADS)]

        def keys(q):
            return (0, 512) if q < 2 else (256, 256)

        block = ctx.enter_context(nc.Block())

        @block.sync
        def _(sp):
            loaded = sem("setup_loaded")
            sp.dma_start(cond_in[:, :, :], dram["cond_t"]).then_inc(loaded, 16)
            sp.dma_start(const[:, :], dram["const"]).then_inc(loaded, 16)
            sp.dma_start(vec1[:, :, :], dram["vec1"]).then_inc(loaded, 16)
            sp.dma_start(vec2[:, :], dram["vec2"]).then_inc(loaded, 16)
            sp.dma_start(expand_in, dram["expand"]).then_inc(loaded, 16)
            sp.dma_start(router_sb[:, :, :, :].rearrange("p l k e -> p l (k e)"), dram["router"]).then_inc(loaded, 16)
            sp.dma_start(x_res[:, :, 0:N], dram["x_t"].rearrange("(k p) t -> p k t", p=P)).then_inc(sem("x_loaded"), 16)
            sp.dma_start(x_res[:, :, N:2 * N], dram["ctx_t"].rearrange("(k p) t -> p k t", p=P)).then_inc(sem("x_loaded"), 16)

            def load(n, src, lo=0, first=True):
                width = 1
                for d in src.shape[1:]:
                    width *= d
                if first and slot_free[n]:
                    sp.wait_ge(weights_used, slot_free[n])
                dst = slot(n)[:, lo:lo + width]
                if len(src.shape) == 3:
                    dst = dst.rearrange("p (a b) -> p a b", a=src.shape[1])
                sp.dma_start(dst, src).then_inc(slot_loaded[slot_of[n]], 16)

            def cols(w, lo, hi):
                return w[:, lo:hi].rearrange("(k p) n -> p k n", p=P)

            def krows(w, lo, hi):
                return w[lo * P:hi * P, :].rearrange("(k p) n -> p k n", p=P)

            def ada(step):
                l, i = divmod(step, 3)
                for j in range(4):
                    rows_of = dram["ada_w"][l][2 * P * j:2 * P * j + 2 * P, 2048 * i:2048 * i + 2048]
                    load(chunk_at["ada", step] + j, rows_of.rearrange("(k p) n -> p k n", p=P))

            def ffn(i):
                l, which = divmod(i, 2)
                n = chunk_at["ffn", i]
                gate, up, down = (dram[f"ffn{which + 1}_{w}"][l] for w in ("gate", "up", "down"))

                for g in range((FT + 3) // 4):
                    lo, hi = 4 * g, min(4 * g + 4, FT)
                    load(n + 3 * g, cols(gate, lo * P, hi * P))
                    if hi < FT:
                        load(n + 3 * g + 1, cols(up, lo * P, hi * P))
                        load(n + 3 * g + 2, krows(down, lo, hi))
                    else:
                        load(n + 3 * g, cols(up, lo * P, hi * P), lo=D * (hi - lo), first=False)
                        load(n + 3 * g + 1, krows(down, lo, hi))

            for l in range(LAYERS):
                if l == 0:
                    ada(0)
                n, w = chunk_at["w_in", l], dram["w_in"][l]
                load(n, cols(w, 3 * GROUP, 5 * GROUP))
                load(n + 1, cols(w, 6 * GROUP, 8 * GROUP))
                load(n + 2, cols(w, 0, 2 * GROUP))
                load(n + 3, cols(w, 5 * GROUP, 6 * GROUP))
                load(n + 3, cols(w, 8 * GROUP, 9 * GROUP), lo=KT * GROUP, first=False)
                load(n + 4, cols(w, 2 * GROUP, 3 * GROUP))
                if l == 0:
                    for step in range(1, 5):
                        ada(step)
                for i in range(2):
                    load(chunk_at["w_out", l] + i, cols(dram["w_out"][l], 512 * i, 512 * i + 512))
                if l == 0:
                    for step in range(5, 6):
                        ada(step)
                n = chunk_at["experts", l]
                early = [slot_free[n + c] for c in range(SLOTS) if slot_free[n + c] > n + c - SLOTS + 1]
                if early:
                    sp.wait_ge(weights_used, max(early))
                with sp.Fori(0, EXPERTS // 4) as it:
                    for c in range(24):
                        w = dram[("exp_gate", "exp_up", "exp_down")[c % 6 // 2]]
                        sp.wait_ge(weights_used, it * 24 + (n + c - SLOTS + 1))
                        half = c % 2
                        src = w[l, it * 4 + c // 6, half * 512:half * 512 + 512, :].rearrange("(k p) n -> p k n", p=P)
                        sp.dma_start(slot(n + c).rearrange("p (k n) -> p k n", k=4), src)\
                            .then_inc(slot_loaded[slot_of[n + c]], 16)
            for l in range(LAYERS):
                ffn(2 * l)
                if l == 0:
                    n = chunk_at["lru", 0]
                    for first, branch in ((n, D_RNN), (n + 5, 0)):
                        for i in range(0, RT, 4):
                            at, end = branch + P * i, branch + P * min(i + 4, RT)
                            load(first + i // 4, cols(dram["lru_in"], at, end))
                        if branch:
                            load(n + 3, dram["lru_a"])
                            load(n + 4, dram["lru_x"])
                    for i in range(3):
                        load(n + 8 + i, krows(dram["lru_out"], 4 * i, min(4 * i + 4, RT)))
                else:
                    load(chunk_at["pool", 0], dram["pool_w"].rearrange("(j p) n -> p j n", p=P))
                ffn(2 * l + 1)
                n = chunk_at["ple", l]
                load(n, cols(dram["ple_gate"][l], 0, 512))
                load(n + 1, krows(dram["ple_proj"][l], 0, 2))
                load(n + 1, krows(dram["p_t"][l], 0, 2), lo=2 * D, first=False)
                load(n + 2, cols(dram["ple_gate"][l], 512, 1024))
            sp.wait_ge(sem("norm_scaled"), NORM_END)
            sp.dma_start(out_t.rearrange("(k p) t -> p k t", p=P), h_buf[:, :, 0:N]).then_inc(sem("out_stored"), 16)
            sp.wait_ge(sem("out_stored"), 16)

        @block.gpsimd
        def _(pool):
            for l in range(LAYERS):
                if l > 0:
                    pool.wait_ge(sem("qk_ready"), 2 + before("qk_ready", l - 1))
                    pool.wait_ge(sem("sgu_done"), 1 + before("sgu_done", l - 1))
                    pool.wait_ge(sem("moe_added"), KT + before("moe_added", l - 1))
                pool.dma_start(rows[:, :], dram["rows"][l]).then_inc(sem("rows_loaded"), 16)
                pool.dma_start(sgu_t, dram["sgu_t"][l]).then_inc(sem("rows_loaded"), 16)
                pool.wait_ge(sem("proj_done"), len(proj_jobs(l)) + before("proj_done", l))
                first = ATT["cs_d"]
                pool.dma_start(att[:, 0:first], dram["att"][:, 0:first]).then_inc(sem("cs_loaded"), 16)
                pool.dma_start(att[:, first:ATT_W], dram["att"][:, first:ATT_W]).then_inc(sem("att_loaded"), 16)
                pool.dma_start(rel_bias, dram["rel_bias"][l]).then_inc(sem("rel_bias_loaded"), 16)
                pool.wait_ge(sem("qk_t_act"), 1 + before("qk_t_act", l))
                pool.wait_ge(sem("qk_t_dve"), 1 + before("qk_t_dve", l))
                band = const[:, columns(CONST, "band_c")]
                for u, (q, h) in enumerate(units(l)):
                    if u == 0:
                        pool.wait_ge(sem("qk_turned"), 4 + before("qk_turned", l))
                    if u >= 4:
                        pool.wait_ge(sem("c_scores"), 2 * (u - 3) + before("c_scores", l))
                    for m in range(2):
                        g = 2 * h + m
                        ins = pool.tensor_scalar(q_band[:, 2 * (u % 4) + m, :], qk_t[:, g // 4, P * q:P * q + P],
                                                 band[:, g % 4:g % 4 + 1], None, ALU.mult)
                    ins.then_inc(sem("c_bands"), 1)
                pool.wait_ge(sem("att_loaded"), 16 + before("att_loaded", l))
                pool.wait_ge(sem("rel_bias_loaded"), 16 + before("rel_bias_loaded", l))
                biases = rel_bias.rearrange("p q h f -> p (q h) f")
                mask = att[:, columns(ATT, "mask")]
                masks = bass.AP(mask.tensor, mask.offset, [list(mask.ap[0]), [0, 2 * HEADS], list(mask.ap[1])])
                pool.tensor_tensor(biases, biases, masks, ALU.add).then_inc(sem("bias_ready"), 1)
                pool.wait_ge(sem("qk_t_act"), 3 + before("qk_t_act", l))
                pool.wait_ge(sem("qk_t_dve"), 3 + before("qk_t_dve", l))
                pool.wait_ge(sem("c_scores"), 2 * len(units(l)) + before("c_scores", l))
                band = const[:, columns(CONST, "band_d")]
                for u, (q, h) in enumerate(units(l)):
                    if u >= 8:
                        pool.wait_ge(sem("d_scores"), u - 7 + before("d_scores", l))
                    pool.tensor_scalar(q_band[:, u % 8, :], qk_t[:, h // 2, P * q:P * q + P],
                                       band[:, h % 2:h % 2 + 1], None, ALU.mult).then_inc(sem("d_bands"), 1)
            pool.wait_ge(sem("ple_added"), KT)
            pool.dma_start(pool_inv, dram["pool_inv"]).then_inc(sem("pool_inv_loaded"), 16)
            count = [0]

            def link(ins):
                count[0] += 1
                ins.then_inc(sem("pool_chain"), 1)
                pool.wait_ge(sem("pool_chain"), count[0])

            pool.wait_ge(sem("norm_scaled"), scaled_before[POOL_NORM] + 2)
            pool.wait_ge(sem("pool_inv_loaded"), 16)
            lo = KT - 2
            src = normed = h_buf[:, lo:KT, 0:N]
            for g, win in enumerate(POOLS):
                back = win // 2
                dst = (pool_a, pool_b)[g % 2][:, lo:KT, :]
                pool.tensor_copy(dst[:, :, 0:back], src[:, :, 0:back])
                link(pool.tensor_tensor(dst[:, :, back:N], src[:, :, back:N], src[:, :, 0:N - back], ALU.add))
                src = dst
            inv = pool_inv[:, len(POOLS) - 1, :]
            invs = bass.AP(inv.tensor, inv.offset, [list(inv.ap[0]), [0, 2], list(inv.ap[1])])
            u = pool_u[:, lo:KT, :]
            link(pool.tensor_tensor(u, src, invs, ALU.mult))
            pool.tensor_tensor(u, u, normed, ALU.subtract).then_inc(sem("pool_wide_ready"), 1)

        def squares(i):
            return part(0, 4096).rearrange("p (k t) -> p k t", k=KT) if i < 4 else \
                part(2560, 4608).rearrange("p (k t) -> p k t", k=KT)

        def norm_pe(pe, release, i):
            width = norms[i][0]
            for k in range(KT):
                pe.wait_ge(sem("norm_squares"), KT * i + k + 1)
                mm = pe.matmul(ps[:, 0, 0:width], mean_w[:, :], squares(i)[:, k, 0:width], start=k == 0, stop=k == KT - 1)
                if k == 0:
                    release(mm)
            mm.then_inc(sem("norm_mean"), 1)

        def norm_squares(act, i, added):
            width = norms[i][0]
            name, start, tiles = added
            for k in range(KT):
                if k % tiles == 0:
                    act.wait_ge(sem(name), start + k // tiles + 1)
                act.activation(squares(i)[:, k, 0:width], x_res[:, k, 0:width], ACT.Square).then_inc(sem("norm_squares"), 1)

        def norm_act(act, i, rs):
            width = norms[i][0]
            act.wait_ge(sem("norm_mean"), i + 1)
            act.activation(rs[:, 0:width], ps[:, 0, 0:width], ACT.Sqrt, bias=eps_col[:, 0:1]).then_inc(sem("norm_std"), 1)

        def norm_shift(act, i, shift):
            for k in range(KT):
                for s in range(norms[i][1]):
                    act.wait_ge(sem("norm_scaled"), scaled_before[i] + k * norms[i][1] + s + 1)
                    part_ = h_buf[:, k, s * N:s * N + N]
                    act.activation(part_, part_, ACT.Identity, bias=shift[:, k, s:s + 1]).then_inc(sem("norm_shifted"), 1)

        def norm_squares_lead(act, i, gain, added):
            name, start, tiles = added
            for k in range(0, KT, 2):
                act.wait_ge(sem(name), start + (k + 1) // tiles + 1)
                act.activation(squares(i)[:, k:k + 2, :], x_res[:, k:k + 2, 0:N], ACT.Square).then_inc(sem("norm_squares"), 2)
                for j in (k, k + 1):
                    act.activation(h_lead[:, j, :], x_res[:, j, 0:N], ACT.Copy, scale=gain(j)).then_inc(sem("norm_led"), 1)

        def norm_gain(name, l):
            g = vec2[:, columns(VEC2, name)]
            return lambda k: g[:, KT * l + k:KT * l + k + 1]

        def head_gain(l):
            return vec1[:, l, columns(VEC1, "head_out_g")]

        def norm_in_lead(act, i, shift):
            for s in range(2):
                for k in range(KT):
                    act.wait_ge(sem("norm_scaled"), scaled_before[i] + KT * s + k + 1)
                    act.activation(in_lead[:, k, N * s:N * s + N], in_exact[:, k, N * s:N * s + N], ACT.Identity,
                                   bias=shift[:, k, s:s + 1]).then_inc(sem("norm_in_led"), 1)

        def norm_factors(dve, link, i, rs):
            width = N if i else 2 * N
            dve.wait_ge(sem("norm_std"), i + 1)
            link(dve.reciprocal(rs[:, 0:width], rs[:, 0:width]))

        def norm_in_dve(dve, link, i, rs, gain, shift):
            todo = [(s, k) for s in range(2) for k in range(KT)]
            start = 2 * KT * (i // 2)

            def rest(j):
                s, k = todo[j]
                at = slice(N * s, N * s + N)
                dve.wait_ge(sem("norm_in_led"), start + j + 1)
                dve.scalar_tensor_tensor(in_rest[:, k, at], in_exact[:, k, at], shift[:, k, s:s + 1], in_lead[:, k, at],
                                         ALU.add, ALU.subtract).then_inc(sem("norm_in_halved"), 1)

            for j, (s, k) in enumerate(todo):
                at = slice(N * s, N * s + N)
                if k == 0 and s == 1 and i:
                    link(dve.reciprocal(rs[:, at], rs[:, at]))
                dve.scalar_tensor_tensor(in_exact[:, k, at], x_res[:, k, at], gain[:, k, s:s + 1], rs[:, at],
                                         ALU.mult, ALU.mult).then_inc(sem("norm_scaled"), 1)
                dve.wait_ge(sem("norm_scaled"), scaled_before[i] + j + 1)
                if j:
                    rest(j - 1)
            rest(len(todo) - 1)

        def norm_rest(dve, link, i, rs, gain):
            start = KT * sum(in_halves(j) for j in range(i))
            for k in range(KT):
                dve.wait_ge(sem("norm_led"), start + k + 1)
                dve.scalar_tensor_tensor(h_rest[:, k, :], x_res[:, k, 0:N], gain(k), h_lead[:, k, :],
                                         ALU.mult, ALU.subtract).then_inc(sem("norm_halved"), 1)
            dve.wait_ge(sem("norm_std"), i + 1)
            link(dve.reciprocal(rs, rs))

        def norm_dve(dve, link, i, rs, gain):
            width = norms[i][0]
            dve.wait_ge(sem("norm_std"), i + 1)
            link(dve.reciprocal(rs[:, 0:width], rs[:, 0:width]))
            norm_tiles(dve, i, rs, gain, range(KT))

        def norm_tiles(dve, i, rs, gain, tiles):
            for k in tiles:
                for s in range(norms[i][1]):
                    lo = s * N
                    dve.scalar_tensor_tensor(h_buf[:, k, lo:lo + N], x_res[:, k, lo:lo + N], gain(k, s),
                                             rs[:, lo:lo + N], ALU.mult, ALU.mult).then_inc(sem("norm_scaled"), 1)

        def norm_tile(eng, i, k):
            _, streams, shifted = norms[i]
            if in_halves(i):
                eng.wait_ge(sem("norm_halved"), KT * sum(in_halves(j) for j in range(i)) + k + 1)
                return
            name, done = ("norm_shifted", shifted_before) if shifted else ("norm_scaled", scaled_before)
            eng.wait_ge(sem(name), done[i] + (k + 1) * streams)

        SC = GROUP // P

        @block.tensor
        def _(pe):
            owed = [0]

            def release(mm):
                if owed[0]:
                    mm.then_inc(weights_used, owed[0])
                    owed[0] = 0

            def exact(out, a, b, start, stop):
                release(pe.matmul(out, a[0], b[0], start=start, stop=False, skip_group_check=True))
                pe.matmul(out, a[0], b[1], start=False, stop=False, skip_group_check=True)
                return pe.matmul(out, a[1], b[0], start=False, stop=stop, skip_group_check=True)

            def half_cols(pair, lo, hi):
                return pair[0][:, lo:hi], pair[1][:, lo:hi]

            def h_tile(k):
                return h_lead[:, k, :], h_rest[:, k, :]

            def halved_chunk(n, it=None):
                pe.wait_ge(sem("chunk_halved"), (6 * it if it is not None else 0) + (halved_before[n] + 1))

            def chunk(n):
                pe.wait_ge(slot_loaded[slot_of[n]], loaded_value(n))

            def ada_group(step):
                n = chunk_at["ada", step]
                pe.wait_ge(sem("cond_ready"), 2)
                if step:
                    pe.wait_ge(sem("ada_mod"), step)
                for k in range(KT):
                    if k % 2 == 0:
                        chunk(n + k // 2)
                    for j in range(4):
                        at = 2048 * (k % 2) + 512 * j
                        mm = pe.matmul(ps[32 * j:32 * j + 32, 7, :], cond[:, k, :], slot(n + k // 2)[:, at:at + 512],
                                       start=k == 0, stop=k == KT - 1)
                        if k == 0 and j == 0:
                            release(mm)
                    if k % 2:
                        mm.then_inc(weights_used, 1)
                pe.wait_ge(sem("ada_rows"), step + 1)
                for b in range(4):
                    mm = pe.transpose(ps[:, 7, P * b:P * b + P], ada_rows(step)[:, P * b:P * b + P], ident)
                mm.then_inc(sem("ada_turned"), 1)

            def projection(l):
                base = chunk_at["w_in", l]
                jobs = proj_jobs(l)
                seen, ordinal = {"act": 0, "dve": 0}, []
                for j, (c, t, lo, width, engine) in enumerate(jobs):
                    seen[engine] += 1
                    ordinal.append(seen[engine])
                    if j == 0 or jobs[j - 1][0] != c:
                        halved_chunk(base + c)
                    if j >= 6:
                        pe.wait_ge(sem(f"proj_read_{jobs[j - 6][4]}"), ordinal[j - 6] + before(f"proj_read_{jobs[j - 6][4]}", l))
                    w = halves(base + c)
                    tokens = 2 * N if l == 0 else N
                    for k in range(KT):
                        if c == 0 and t % 2 == 0:
                            pe.wait_ge(sem("norm_in_halved"), KT * (2 * l + t // 2) + k + 1)
                        own = slice(P * t, P * t + P)
                        h = (in_lead[:, k, own], in_rest[:, k, own])
                        start, stop = k == 0, k == KT - 1
                        if c == 4:
                            mm = exact(ps[:, j % 6, 0:tokens], half_cols(w, GROUP * k + P * t, GROUP * k + P * t + P),
                                       (in_lead[:, k, 0:tokens], in_rest[:, k, 0:tokens]), start, stop)
                        elif c == 3:
                            both = [a.rearrange("p (h k n) -> p k h n", h=2, k=KT)[:, k, :, :] for a in w]
                            mm = exact(ps[:, j % 6, :].rearrange("p (h n) -> p h n", h=2), h, both, start, stop)
                        else:
                            mm = exact(ps[:, j % 6, 0:width], h, half_cols(w, 512 * k + lo, 512 * k + lo + width), start, stop)
                    mm.then_inc(sem("proj_done"), 1)
                    if j == len(jobs) - 1 or jobs[j + 1][0] != c:
                        owed[0] += 1

            def fourier_channels(l):
                pe.wait_ge(sem("cs_loaded"), 16 + before("cs_loaded", l))
                tiles = 4 if l == 0 else 2
                pe.wait_ge(sem("qk_t_act"), 2 + before("qk_t_act", l))
                pe.wait_ge(sem("qk_t_dve"), 2 + before("qk_t_dve", l))
                cs = att[:, columns(ATT, "cs_d")]
                for t in range(tiles):
                    for c in range(SC):
                        mm = pe.matmul(ps[:, t, 2 * P * c:2 * P * c + 2 * P], fourier_in[:, c, P * t:P * t + P], cs,
                                       start=True, stop=True)
                    mm.then_inc(sem("fourier_uv"), 1)

            def fourier_tokens(l):
                pe.wait_ge(sem("att_loaded"), 16 + before("att_loaded", l))
                cos_n = att[:, columns(ATT, "cos_n")].rearrange("p (a n) -> p a n", a=2)
                sin_n = att[:, columns(ATT, "sin_n")].rearrange("p (a n) -> p a n", a=2)
                for s in range(2 if l == 0 else 1):
                    if s == 0:
                        pe.wait_ge(sem("sgu_done"), 1 + before("sgu_done", l))
                    for nt in range(2):
                        pe.wait_ge(sem("uv_ready"), 2 * s + 2 + before("uv_ready", l))
                        step = 0
                        for a in range(2):
                            for w, table in enumerate((cos_n, sin_n)):
                                mm = pe.matmul(ps[:, 4 + s, N * nt:N * nt + N], table[:, a, P * nt:P * nt + P],
                                               uv[:, 2 * s + a, :, w, :], start=step == 0, stop=step == 3)
                                step += 1
                        mm.then_inc(sem("fourier_done"), 1)

            def spatial_gating(l):
                tiles = 4 if l == 0 else 2
                pe.wait_ge(sem("v_normed"), 1 + before("v_normed", l))
                pe.wait_ge(sem("rows_loaded"), 32 + before("rows_loaded", l))
                for h in range(HEADS):
                    v = gated[:, 0:tiles, GROUP + HEAD * h:GROUP + HEAD * h + HEAD]
                    out = ps[:, 4 + h // 2, N * (h % 2):N * (h % 2) + HEAD * tiles]
                    mm = pe.matmul(out.rearrange("p (t c) -> p t c", t=tiles), sgu_t[:, h, :], v, start=True, stop=True)
                mm.then_inc(sem("sgu_mixed"), 1)

            def turn_qk(l, which):
                src = (qk_c, qk_d)[which]
                if which == 0:
                    for engine in ("act", "dve"):
                        pe.wait_ge(sem(f"proj_read_{engine}"), sum(j[4] == engine for j in proj_jobs(l)) + before(f"proj_read_{engine}", l))
                pe.wait_ge(sem("qk_ready"), which + 1 + before("qk_ready", l))
                for b in range(4):
                    for t in range(4 if l == 0 or b >= 2 else 2):
                        mm = pe.transpose(ps[:, b, P * t:P * t + P], src[:, t, P * b:P * b + P], ident)
                        if t == 0:
                            release(mm)
                    mm.then_inc(sem("qk_turned"), 1)

            def attention_c(l):
                todo = units(l)
                pe.wait_ge(sem("qk_t_act"), 2 + before("qk_t_act", l))
                pe.wait_ge(sem("qk_t_dve"), 2 + before("qk_t_dve", l))

                def scores(u):
                    q, h = todo[u]
                    lo, width = keys(q)
                    if u >= 3:
                        pe.wait_ge(sem("c_exp"), 2 * (u - 2) + before("c_exp", l))
                    if u == 2:
                        pe.wait_ge(sem("fourier_read"), (2 if l == 0 else 1) + before("fourier_read", l))
                    pe.wait_ge(sem("c_bands"), u + 1 + before("c_bands", l))
                    for m in range(2):
                        pe.matmul(ps[:, 2 * (u % 3) + m, 0:width], q_band[:, 2 * (u % 4) + m, :],
                                  qk_t[:, 2 + (2 * h + m) // 4, lo:lo + width], start=True, stop=True)\
                            .then_inc(sem("c_scores"), 1)

                for u in range(3):
                    scores(u)
                for u, (q, h) in enumerate(todo):
                    lo, width = keys(q)
                    tiles = width // P
                    pe.wait_ge(sem("c_weights"), u + 1 + before("c_weights", l))
                    if u >= 1:
                        pe.wait_ge(sem("c_wt"), u + before("c_wt", l))
                    for j in range(tiles):
                        mm = pe.transpose(ps[:, 6, P * j:P * j + P], expo[:, 2 * (u % 3), P * j:P * j + P], ident)
                    mm.then_inc(sem("c_turned"), 1)
                    if u + 3 < len(todo):
                        scores(u + 3)
                    pe.wait_ge(sem("c_wt"), u + 1 + before("c_wt", l))
                    if h == 0 and q >= 1:
                        pe.wait_ge(sem("c_out"), q + before("c_out", l))
                    at = HEAD * h
                    for j in range(tiles):
                        mm = pe.matmul(ps[:, 7, at:at + HEAD], w_t[:, u % 2, j, :],
                                       vals[:, lo // P + j, HEAD * h:HEAD * h + HEAD], start=j == 0, stop=j == tiles - 1)
                    mm.then_inc(sem("c_pv"), 1)

            def attention_d(l):
                todo = units(l)
                pe.wait_ge(sem("qk_t_act"), 4 + before("qk_t_act", l))
                pe.wait_ge(sem("qk_t_dve"), 4 + before("qk_t_dve", l))
                pe.wait_ge(sem("bias_ready"), 1 + before("bias_ready", l))

                def scores(u):
                    q, h = todo[u]
                    lo, width = keys(q)
                    if u >= 3:
                        pe.wait_ge(sem("d_exp"), u - 2 + before("d_exp", l))
                    pe.wait_ge(sem("d_bands"), u + 1 + before("d_bands", l))
                    mm = pe.matmul(ps[:, u % 3, 0:width], q_band[:, u % 8, :], qk_t[:, 2 + h // 2, lo:lo + width],
                                   start=True, stop=q >= 2)
                    if q < 2:
                        mm = pe.matmul(ps[:, u % 3, 0:N], ident, rel_bias[:, q, h, :], start=False, stop=True)
                    mm.then_inc(sem("d_scores"), 1)

                scores(0)
                scores(1)
                def turn(u):
                    pe.wait_ge(sem("d_exp"), u + 1 + before("d_exp", l))
                    if u >= 2:
                        pe.wait_ge(sem("d_wt"), u - 1 + before("d_wt", l))
                    for j in range(keys(todo[u][0])[1] // P):
                        mm = pe.transpose(ps[:, 4 + u % 2, P * j:P * j + P], expo[:, u % 4, P * j:P * j + P], ident)
                    mm.then_inc(sem("d_turned"), 1)

                turn(0)
                for u, (q, h) in enumerate(todo):
                    if u + 2 < len(todo):
                        scores(u + 2)
                    if u + 1 < len(todo):
                        turn(u + 1)
                    lo, width = keys(q)
                    tiles = width // P
                    pe.wait_ge(sem("d_wt"), u + 1 + before("d_wt", l))
                    if u >= 2:
                        pe.wait_ge(sem("d_out"), u - 1 + before("d_out", l))
                    for j in range(tiles):
                        mm = pe.matmul(ps[:, (6, 3)[u % 2], 0:HEAD], w_t[:, u % 2, j, :],
                                       vals[:, lo // P + j, GROUP + HEAD * h:GROUP + HEAD * h + HEAD],
                                       start=j == 0, stop=j == tiles - 1)
                    mm.then_inc(sem("d_pv"), 1)

            def merge(l):
                tiles = 4 if l == 0 else 2
                width = P * tiles
                pe.wait_ge(sem("y_normed"), 4 + before("y_normed", l))
                for k in range(KT):
                    if k >= 6:
                        pe.wait_ge(sem("y_rest"), k - 5 + before("y_rest", l))
                    for t in range(tiles):
                        mm = pe.transpose(ps[:, k % 6, P * t:P * t + P], ycat[:, t, P * k:P * k + P], ident)
                    mm.then_inc(sem("y_turned"), 1)
                for d in range(KT):
                    n = chunk_at["w_out", l] + d // 4
                    if d % 4 == 0:
                        halved_chunk(n)
                    if d == 0:
                        pe.wait_ge(sem("y_rest"), KT + before("y_rest", l))
                    if d >= 6:
                        pe.wait_ge(sem("mix_added"), d - 5 + before("mix_added", l))
                    for k in range(KT):
                        at = 512 * k + P * (d % 4)
                        mm = exact(ps[:, 1 + d % 6, 0:width], half_cols(halves(n), at, at + P),
                                   (out_lead[:, k, 0:width], out_rest[:, k, 0:width]), k == 0, k == KT - 1)
                    mm.then_inc(sem("mix_out"), 1)
                    if d % 4 == 3:
                        owed[0] += 1

            def route(l):
                tiles = 4 if l == 0 else 2
                streams = tiles // 2
                rows_ = 48 if l == 0 else 16
                for k in range(KT):
                    norm_tile(pe, 2 * l + 1, k)
                    mm = pe.matmul(ps[0:EXPERTS, 5, 0:P * tiles], router_sb[:, l, k, :], h_buf[:, k, 0:P * tiles],
                                   start=k == 0, stop=k == KT - 1)
                mm.then_inc(sem("logits"), 1)
                for j in range(2 * tiles):
                    half, t = divmod(j, tiles)
                    if j >= 4:
                        pe.wait_ge(sem("h_tok_rest"), j - 3 + before("h_tok_rest", l))
                    for k in range(4):
                        mm = pe.transpose(ps[:, 1 + j % 4, P * k:P * k + P], h_buf[:, 4 * half + k, P * t:P * t + P], ident)
                    mm.then_inc(sem("h_turned"), 1)
                    if j == 1:
                        pe.wait_ge(sem("logits_copied"), 1 + before("logits_copied", l))
                        for t in range(tiles):
                            mm = pe.transpose(ps[:, 0, EXPERTS * t:EXPERTS * t + EXPERTS],
                                              logits_t[0:EXPERTS, P * t:P * t + P], ident[0:EXPERTS, 0:EXPERTS])
                        mm.then_inc(sem("logits_turned"), 1)
                pe.wait_ge(sem("aff"), 1 + before("aff", l))
                for t in range(tiles):
                    mm = pe.transpose(ps[0:EXPERTS, 0, P * t:P * t + P], logit[:, EXPERTS * t:EXPERTS * t + EXPERTS], ident)
                mm.then_inc(sem("aff_turned"), 1)
                if l == 0:
                    ada_group(5)
                pe.wait_ge(sem("slots"), 1 + before("slots", l))
                for a in range(2):
                    mm = pe.transpose(ps[:, 0, 48 * a:48 * a + rows_], slot_id[0:rows_, P * a:P * a + P],
                                      ident[0:rows_, 0:rows_])
                mm.then_inc(sem("slots_turned"), 1)
                pe.wait_ge(sem("h_tok_rest"), 2 * tiles + before("h_tok_rest", l))
                pe.wait_ge(sem("gather_ready"), 1 + before("gather_ready", l))
                for j in range(KT * streams):
                    s, k = divmod(j, KT)
                    if j >= 6:
                        pe.wait_ge(sem(f"picked_{('act', 'dve')[j % 2]}"), (j - 6) // 2 + 1 + before(f"picked_{('act', 'dve')[j % 2]}", l))
                    for a in range(2):
                        one_hot = gather[:, 2 * s + a, :, :].rearrange("p e s -> p (e s)")
                        at = P * (k % 4)
                        for i, h in enumerate((h_tok[:, 2 * s + a, P * k:P * k + P],
                                               h_tok_rest[k // 4][:, 2 * s + a, at:at + P])):
                            mm = pe.matmul(ps[:, j % 6, :], h, one_hot, start=a == 0 and i == 0, stop=a == 1 and i == 1)
                    mm.then_inc(sem("gathered"), 1)
                for s in range(streams):
                    pe.wait_ge(sem("expand_ready"), 1)
                    pe.wait_ge(sem("spread_rows"), s + 1 + before("spread_rows", l))
                    if s == 0:
                        pe.wait_ge(sem("picked_act"), KT // 2 * streams + before("picked_act", l))
                        pe.wait_ge(sem("picked_dve"), KT // 2 * streams + before("picked_dve", l))
                    else:
                        pe.wait_ge(sem("scatter_ready"), s + before("scatter_ready", l))
                    for g in range(4):
                        mm = pe.matmul(ps[:, 4 + g, :], expand[:, P * g:P * g + P],
                                       spread_rows[0:64, s, :, :].rearrange("p w t -> p (w t)"), start=True, stop=True)
                    mm.then_inc(sem("spread"), 1)

            def experts(l):
                m = 2 * CAP if l == 0 else CAP
                n = chunk_at["experts", l]
                pe.wait_ge(sem("picked_act"), KT // 2 * (m // CAP) + before("picked_act", l))
                pe.wait_ge(sem("picked_dve"), KT // 2 * (m // CAP) + before("picked_dve", l))
                hid_t = hid_exp_t[:, 0:8 * m].rearrange("p (j h m) -> p j h m", j=4, h=2)
                with pe.Fori(0, EXPERTS // 4) as it:
                    for j in range(4):
                        xe = x_exp[:, 512 * (j % 2):512 * (j % 2) + KT * m].rearrange("p (k m) -> p k m", k=KT)
                        pe.wait_ge(sem("x_exp"), it * 4 + (j + 1) + before("x_exp", l))
                        for which in range(2):
                            for k in range(KT):
                                c = 6 * j + 2 * which + k // 4
                                if k % 4 == 0:
                                    pe.wait_ge(slot_loaded[slot_of[n + c]], it * 64 + (loaded_value(n + c)))
                                for half in range(2):
                                    mm = pe.matmul(ps[half * m:half * m + m, which, :], xe[:, k, :],
                                                   slot(n + c)[:, D * (k % 4) + 512 * half:D * (k % 4) + 512 * half + 512],
                                                   start=k == 0, stop=k == KT - 1)
                                if k % 4 == 3:
                                    mm.then_inc(weights_used, 1)
                        pe.wait_ge(sem("exp_hid"), it * 4 + (j + 1) + before("exp_hid", l))
                        for b in range(4):
                            mm = pe.transpose(ps[:, 2, P * b:P * b + P], hid_exp[:, P * b:P * b + P], ident)
                        mm.then_inc(sem("exp_turned"), 1)
                        pe.wait_ge(sem("exp_hid_t"), it * 4 + (j + 1) + before("exp_hid_t", l))
                        for k in range(KT):
                            c = 6 * j + 4 + k // 4
                            if k % 4 == 0:
                                pe.wait_ge(slot_loaded[slot_of[n + c]], it * 64 + (loaded_value(n + c)))
                            for half in range(2):
                                mm = pe.matmul(ps[half * m:half * m + m, 3, :], hid_t[:, k % 4, k // 4, :],
                                               slot(n + c)[:, D * (k % 4) + 512 * half:D * (k % 4) + 512 * half + 512],
                                               start=k == 0, stop=k == KT - 1)
                            if k % 4 == 3:
                                mm.then_inc(weights_used, 1)

            def scatter_back(l):
                streams = 2 if l == 0 else 1
                pe.wait_ge(sem("o_act"), EXPERTS + before("o_act", l))
                pe.wait_ge(sem("o_dve"), EXPERTS + before("o_dve", l))
                for d in range(KT):
                    if d >= 4:
                        pe.wait_ge(sem("moe_added"), d - 3 + before("moe_added", l))
                    for s in range(streams):
                        for g in range(4):
                            o = (o_lat, o_ctx)[s]
                            mm = pe.matmul(ps[:, 4 + d % 4, N * s:N * s + N], o[:, g, P * d:P * d + P],
                                           scatter[:, s, g, :], start=g == 0, stop=g == 3)
                    mm.then_inc(sem("moe_out"), 1)

            def ffn_group(i, norm, n, it, step, tiles):
                width = P * tiles
                last = step + tiles == FT
                size = tiles // 2
                for which in range(2):
                    c, start = (n, D * tiles * which) if last else (n + which, 0)
                    if start == 0:
                        halved_chunk(c, it)
                    w = halves(c)
                    for f in range(tiles):
                        if which and f == size:
                            pe.wait_ge(sem("norm_std"), norm + 1)
                        bank = ((1, 2), (3, 0))[which][f // size]
                        lo = N * (f % size)
                        for k in range(KT):
                            if step == 0 and f == 0 and which == 0:
                                norm_tile(pe, norm, k)
                            at = start + width * k + P * f
                            mm = exact(ps[:, bank, lo:lo + N], half_cols(w, at, at + P),
                                       h_tile(k), k == 0, k == KT - 1)
                        if f % size == size - 1:
                            mm.then_inc(sem(("ffn_gate", "ffn_up")[which]), 1)
                    if which or not last:
                        owed[0] += 1
                halved_chunk(c + 1, it)
                w = halves(c + 1)
                for f in range(tiles):
                    if f % size == 0:
                        pe.wait_ge(sem("ffn_halved"), (4 * it if it is not None else 0) + (FFN_BANKS * i + step // 2 + f // size + 1))
                    for d in range(KT):
                        at = D * f + P * d
                        mm = exact(ps[:, 4 + d // 2, N * (d % 2):N * (d % 2) + N], half_cols(w, at, at + P),
                                   (hid_lead[:, f, :], hid_rest[:, f, :]), False, False)
                        if last and f == tiles - 1 and d % 2:
                            mm.then_inc(sem("ffn_summed"), 1)
                if last:
                    owed[0] += 1
                else:
                    mm.then_inc(weights_used, 1)

            def open_sums():
                for b in range(4, 8):
                    release(pe.matmul(ps[:, b, :], zeros[:, 0:P], zeros[:, :], start=True, stop=False, skip_group_check=True))

            def ffn(i, norm):
                n = chunk_at["ffn", i]
                open_sums()
                with pe.Fori(0, FT // 8) as it:
                    ffn_group(i, norm, n, it, 0, 4)
                    ffn_group(i, norm, n + 3, it, 4, 4)
                at = FT // 8 * 8
                ffn_group(i, norm, n + 3 * at // 4, None, at, 4)
                ffn_group(i, norm, n + 3 * at // 4 + 3, None, at + 4, 2)

            def lru(norm):
                n = chunk_at["lru", 0]
                for o in range(RT):
                    if o == 1:
                        norm_pe(pe, release, norm)
                    c, wide = n + o // 4, P * min(4, RT - o // 4 * 4)
                    if o % 4 == 0:
                        halved_chunk(c)
                    if o == 7:
                        pe.wait_ge(sem("norm_std"), norm + 1)
                    if o >= 8:
                        pe.wait_ge(sem("lru_read_dve"), o - 7)
                    for k in range(KT):
                        if o == 0:
                            norm_tile(pe, norm, k)
                        at = wide * k + P * (o % 4)
                        mm = exact(ps[:, (1 + o) % 8, 0:N], half_cols(halves(c), at, at + P), h_tile(k), k == 0, k == KT - 1)
                    mm.then_inc(sem("lru_in"), 1)
                    if o % 4 == 3 or o == RT - 1:
                        owed[0] += 1
                chunk(n + 3)
                chunk(n + 4)
                pe.wait_ge(sem("lru_read_dve"), 6)
                for o in range(RT):
                    mine = [i for i, (a, _) in enumerate(PAIRS) if a == o]
                    pe.wait_ge(sem("lru_conv"), PAIRS[mine[-1]][1] + 1)
                    if o >= 4:
                        pe.wait_ge(sem("lru_gates"), 2 * (o - 3))
                    for which in range(2):
                        for i in mine:
                            mm = pe.matmul(ps[:, 3 + o % 4, N * which:N * which + N],
                                           slot(n + 3 + which)[:, P * i:P * i + P],
                                           l_x[:, PAIRS[i][1], :], start=i == mine[0], stop=i == mine[-1])
                            if i == mine[0]:
                                release(mm)
                    mm.then_inc(sem("lru_gate_in"), 1)
                owed[0] += 2
                for o in range(RT):
                    c, wide = n + 5 + o // 4, P * min(4, RT - o // 4 * 4)
                    if o % 4 == 0:
                        halved_chunk(c)
                    if o == 0:
                        pe.wait_ge(sem("lru_read_dve"), RT)
                    if o == 4:
                        pe.wait_ge(sem("lru_gates"), 2 * RT)
                    if o >= 8:
                        pe.wait_ge(sem("lru_branch_scaled"), o - 7)
                    for k in range(KT):
                        at = wide * k + P * (o % 4)
                        mm = exact(ps[:, (7 + o) % 8, 0:N], half_cols(halves(c), at, at + P), h_tile(k), k == 0, k == KT - 1)
                    mm.then_inc(sem("lru_branch"), 1)
                    if o % 4 == 3 or o == RT - 1:
                        owed[0] += 1
                pe.wait_ge(sem("lru_branch_scaled"), RT)
                open_sums()
                for k in range(RT):
                    c = n + 8 + k // 4
                    if k % 4 == 0:
                        halved_chunk(c)
                    pe.wait_ge(sem("lru_y"), k + 1)
                    for d in range(KT):
                        at = D * (k % 4) + P * d
                        mm = exact(ps[:, 4 + d // 2, N * (d % 2):N * (d % 2) + N], half_cols(halves(c), at, at + P),
                                   (y_lead[:, k, :], y_rest[:, k, :]), False, False)
                        if k == RT - 1 and d % 2:
                            mm.then_inc(sem("lru_summed"), 1)
                    if k % 4 == 3:
                        mm.then_inc(weights_used, 1)
                owed[0] += 1

            def pooling():
                n = chunk_at["pool", 0]
                chunk(n)
                for d in range(KT):
                    g, half = divmod(d, 2)
                    if g < len(POOLS) - 1:
                        pe.wait_ge(sem("pool_ready"), g + 1)
                    else:
                        pe.wait_ge(sem("pool_wide_ready"), 1)
                    for k in range(2):
                        at = GROUP * (2 * g + k) + P * half
                        mm = pe.matmul(ps[:, 4 + d // 2, N * half:N * half + N], slot(n)[:, at:at + P],
                                       pool_u[:, 2 * g + k, :], start=k == 0, stop=k == 1)
                    if half:
                        mm.then_inc(sem("pool_mapped"), 1)
                owed[0] += 1

            def ple(l, norm):
                n = chunk_at["ple", l]
                p_lead, p_rest = (a[:, 2 * D:2 * D + 2 * N].rearrange("p (k t) -> p k t", k=2) for a in halves(n + 1))
                for part_ in range(2):
                    c = n + 2 * part_
                    halved_chunk(c)
                    tiles = range(4 * part_, 4 * part_ + 4)
                    for d in tiles:
                        if d == 1:
                            norm_pe(pe, release, norm)
                        if d >= 6:
                            pe.wait_ge(sem("ple_added"), KT * l + d - 5)
                        for k in range(KT):
                            if d == 0:
                                norm_tile(pe, norm, k)
                            at = 512 * k + P * (d % 4)
                            exact(ps[:, 1 + d % 6, 0:N], half_cols(halves(c), at, at + P), h_tile(k), k == 0, k == KT - 1)
                    if part_ == 0:
                        owed[0] += 1
                        halved_chunk(n + 1)
                    for d in tiles:
                        for k in range(2):
                            at = D * k + P * d
                            mm = exact(ps[:, 1 + d % 6, N:2 * N], half_cols(halves(n + 1), at, at + P),
                                       (p_lead[:, k, :], p_rest[:, k, :]), k == 0, k == 1)
                        mm.then_inc(sem("ple_products"), 1)
                owed[0] += 2

            pe.wait_ge(sem("setup_loaded"), 16 * 6)
            pe.wait_ge(sem("memsets"), 1)
            for l in range(LAYERS):
                norm_pe(pe, release, 2 * l)
                if l == 0:
                    ada_group(0)
                projection(l)
                turn_qk(l, 0)
                spatial_gating(l)
                if l == 0:
                    ada_group(1)
                fourier_channels(l)
                fourier_tokens(l)
                if l == 0:
                    ada_group(2)
                attention_c(l)
                pe.wait_ge(sem("c_exp"), 2 * len(units(l)) + before("c_exp", l))
                turn_qk(l, 1)
                pe.wait_ge(sem("c_out"), (4 if l == 0 else 2) + before("c_out", l))
                if l == 0:
                    ada_group(3)
                attention_d(l)
                if l == 0:
                    ada_group(4)
                merge(l)
                norm_pe(pe, release, 2 * l + 1)
                route(l)
                experts(l)
                scatter_back(l)
            for l in range(LAYERS):
                i = 4 + 4 * l
                norm_pe(pe, release, i)
                ffn(2 * l, i)
                if l == 0:
                    lru(i + 1)
                else:
                    norm_pe(pe, release, i + 1)
                    pooling()
                norm_pe(pe, release, i + 2)
                ffn(2 * l + 1, i + 2)
                ple(l, i + 3)
            norm_pe(pe, release, LAST_NORM)

        @block.scalar
        def _(act):
            count = [0]

            def link(ins):
                count[0] += 1
                ins.then_inc(sem("act_chain"), 1)
                act.wait_ge(sem("act_chain"), count[0])

            def ada_group(step):
                act.wait_ge(weights_used, chunk_at["ada", step] + 4)
                act.activation(ada_rows(step), ps[:, 7, :], ACT.Copy).then_inc(sem("ada_rows"), 1)

            def projection(l, chunks):
                for j, (c, t, lo, width, engine) in enumerate(proj_jobs(l)):
                    if engine != "act" or c not in chunks:
                        continue
                    act.wait_ge(sem("proj_done"), j + 1 + before("proj_done", l))
                    if c == 2:
                        ins = act.activation(gated[:, t, :], ps[:, j % 6, :], ACT.Gelu_apprx_tanh)
                    elif c < 2:
                        ins = act.activation((qk_c, qk_d)[c][:, t, lo:lo + width], ps[:, j % 6, 0:width], ACT.Copy)
                    else:
                        tokens = 2 * N if l == 0 else N
                        ins = act.activation(fourier_in[:, t, 0:tokens], ps[:, j % 6, 0:tokens], ACT.Copy)
                    ins.then_inc(sem("proj_read_act"), 1)

            def mix_std(lo, hi, width):
                act.activation(mix_ss[:, lo:hi], mix_ss[:, lo:hi], ACT.Sqrt, bias=eps_col[:, 0:1], scale=1.0 / width)\
                    .then_inc(sem("mix_std"), 1)

            def qk_stats(l):
                act.wait_ge(sem("proj_read_act"), 8 + before("proj_read_act", l))
                act.activation(sq_c, qk_c.rearrange("p t f -> p (t f)"), ACT.Square).then_inc(sem("mix_squares"), 1)
                act.wait_ge(sem("mix_sums"), 1 + before("mix_sums", l))
                act.activation(sq_d, qk_d.rearrange("p t f -> p (t f)"), ACT.Square).then_inc(sem("mix_squares"), 1)
                act.wait_ge(sem("mix_sums"), 2 + before("mix_sums", l))
                mix_std(0, 64, DIFF)
                mix_std(64, 96, HEAD)
                halve_lead(act, chunk_at["w_in", l] + 4)
                act.wait_ge(sem("c_normed"), 1 + before("c_normed", l))
                src = qk_c.rearrange("p t f -> p (t f)").rearrange("p (g w e) -> p g w e", w=2, e=8)
                dst = swapped.rearrange("p (g w e) -> p g w e", w=2, e=8)
                for w in range(2):
                    act.activation(dst[:, :, w, :], src[:, :, 1 - w, :], ACT.Copy).then_inc(sem("c_swapped"), 1)

            def gate_stats(l):
                tiles = 4 if l == 0 else 2
                act.wait_ge(sem("proj_read_act"), 8 + tiles + before("proj_read_act", l))
                act.wait_ge(sem("qk_ready"), 1 + before("qk_ready", l))
                act.activation(sq_v[:, 0:GROUP * tiles].rearrange("p (t f) -> p t f", t=tiles),
                               gated[:, 0:tiles, GROUP:2 * GROUP], ACT.Square).then_inc(sem("mix_squares"), 1)
                act.wait_ge(sem("mix_sums"), 3 + before("mix_sums", l))
                mix_std(96, 96 + 4 * tiles, HEAD)

            def read_fourier_uv(l):
                for t in range(4 if l == 0 else 2):
                    act.wait_ge(sem("fourier_uv"), t + 1 + before("fourier_uv", l))
                    if t == 0:
                        act.wait_ge(sem("sgu_done"), 1 + before("sgu_done", l))
                    act.activation(uv_flat[:, t, :], ps[:, t, :], ACT.Copy).then_inc(sem("uv_ready"), 1)

            uv_flat = part(4096, 6144).rearrange("p (t f) -> p t f", t=4)

            def read_qk_t(l, which):
                for b in (0, 2):
                    act.wait_ge(sem("qk_turned"), 4 * which + b + 1 + before("qk_turned", l))
                    width = 512 if l == 0 or b >= 2 else N
                    act.activation(qk_t[:, b, 0:width], ps[:, b, 0:width], ACT.Copy).then_inc(sem("qk_t_act"), 1)

            def attention_c(l):
                todo = units(l)

                def softmax(u):
                    width = keys(todo[u][0])[1]
                    if u >= 3:
                        act.wait_ge(sem("c_turned"), u - 2 + before("c_turned", l))
                    for m in range(2):
                        i = 2 * u + m
                        act.wait_ge(sem("c_max"), i + 1 + before("c_max", l))
                        act.activation(expo[:, 2 * (u % 3) + m, 0:width], ps[:, 2 * (u % 3) + m, 0:width], ACT.Exp,
                                       bias=c_max[:, i:i + 1], accum_out=c_den[:, i:i + 1]).then_inc(sem("c_exp"), 1)

                act.wait_ge(sem("qk_turned"), 4 + before("qk_turned", l))
                for u in range(3):
                    softmax(u)
                for u, (q, h) in enumerate(todo):
                    width = keys(q)[1]
                    act.wait_ge(sem("c_turned"), u + 1 + before("c_turned", l))
                    if u >= 2:
                        act.wait_ge(sem("c_pv"), u - 1 + before("c_pv", l))
                    act.activation(w_t[:, u % 2, 0:width // P, :].rearrange("p k f -> p (k f)"), ps[:, 6, 0:width],
                                   ACT.Copy).then_inc(sem("c_wt"), 1)
                    if u + 3 < len(todo):
                        softmax(u + 3)

            def attention_d(l):
                todo = units(l)

                def softmax(u):
                    width = keys(todo[u][0])[1]
                    act.wait_ge(sem("d_max"), u + 1 + before("d_max", l))
                    if u >= 4:
                        act.wait_ge(sem("d_turned"), u - 3 + before("d_turned", l))
                    act.activation(expo[:, u % 4, 0:width], ps[:, u % 3, 0:width], ACT.Exp, bias=d_max[:, u:u + 1],
                                   accum_out=d_den[:, u:u + 1]).then_inc(sem("d_exp"), 1)

                softmax(0)
                for u in range(len(todo)):
                    if u in (2, 4, 6):
                        y_std(l, u // 2 - 1)
                    if u in (0, 2, 4):
                        y_squares(l, u // 2)
                    if u == len(todo) // 2:
                        halve_lead(act, chunk_at["w_out", l])
                    if u + 1 < len(todo):
                        softmax(u + 1)
                    width = keys(todo[u][0])[1]
                    act.wait_ge(sem("d_turned"), u + 1 + before("d_turned", l))
                    if u >= 2:
                        act.wait_ge(sem("d_pv"), u - 1 + before("d_pv", l))
                    act.activation(w_t[:, u % 2, 0:width // P, :].rearrange("p k f -> p (k f)"), ps[:, 4 + u % 2, 0:width],
                                   ACT.Copy).then_inc(sem("d_wt"), 1)

            def y_squares(l, piece):
                tiles = 4 if l == 0 else 2
                lo, heads, _ = Y_PIECES[piece]
                if piece == 0:
                    act.wait_ge(sem("sgu_done"), 1 + before("sgu_done", l))
                    act.wait_ge(sem("fourier_read"), tiles // 2 + before("fourier_read", l))
                elif piece == 2:
                    act.wait_ge(sem("c_out"), tiles + before("c_out", l))
                elif piece == 3:
                    act.wait_ge(sem("d_out"), len(units(l)) + before("d_out", l))
                act.activation(y_sq[:, 0:tiles * heads * HEAD].rearrange("p (t f) -> p t f", t=tiles),
                               ycat[:, 0:tiles, lo:lo + heads * HEAD], ACT.Square).then_inc(sem("y_squares"), 1)

            def y_std(l, piece):
                tiles = 4 if l == 0 else 2
                _, heads, at = Y_PIECES[piece]
                act.wait_ge(sem("y_sums"), piece + 1 + before("y_sums", l))
                ss = y_ss[:, at:at + heads * tiles]
                act.activation(ss, ss, ACT.Sqrt, bias=eps_col[:, 0:1], scale=1.0 / HEAD).then_inc(sem("y_std"), 1)

            def merge(l):
                tiles = 4 if l == 0 else 2
                for k in range(KT):
                    act.wait_ge(sem("y_turned"), k + 1 + before("y_turned", l))
                    act.activation(out_lead[:, k, 0:P * tiles], ps[:, k % 6, 0:P * tiles], ACT.Copy,
                                   scale=head_gain(l)[:, k:k + 1]).then_inc(sem("y_t"), 1)
                halve_lead(act, chunk_at["w_out", l] + 1)

            def route(l):
                tiles = 4 if l == 0 else 2
                act.wait_ge(sem("logits"), 1 + before("logits", l))
                act.activation(logits_t[0:EXPERTS, 0:P * tiles], ps[0:EXPERTS, 5, 0:P * tiles], ACT.Copy)\
                    .then_inc(sem("logits_copied"), 1)
                for j in range(2 * tiles):
                    half, t = divmod(j, tiles)
                    act.wait_ge(sem("h_turned"), j + 1 + before("h_turned", l))
                    act.activation(h_tok[:, t, 512 * half:512 * half + 512], ps[:, 1 + j % 4, :], ACT.Copy)\
                        .then_inc(sem("h_tok_lead"), 1)
                    if j == tiles - 1:
                        act.wait_ge(sem("logits_shifted"), 1 + before("logits_shifted", l))
                        act.activation(logit[:, 0:EXPERTS * tiles], logit[:, 0:EXPERTS * tiles], ACT.Exp)\
                            .then_inc(sem("logits_exp"), 1)
                if l == 0:
                    ada_group(5)
                for j in range(0, KT * tiles // 2, 2):
                    s, k = divmod(j, KT)
                    act.wait_ge(sem("gathered"), j + 1 + before("gathered", l))
                    act.activation(picked_of(l)[:, k, :, CAP * s:CAP * s + CAP],
                                   ps[:, j % 6, :].rearrange("p (e s) -> p e s", e=EXPERTS), ACT.Copy)\
                        .then_inc(sem("picked_act"), 1)
                for s in range(tiles // 2):
                    act.wait_ge(sem("spread"), s + 1 + before("spread", l))
                    act.activation(aff_bc, ps[:, 4:8, 0:N], ACT.Copy).then_inc(sem("aff_copied"), 1)

            def experts(l):
                m = 2 * CAP if l == 0 else CAP
                first = chunk_at["experts", l]
                with act.Fori(0, EXPERTS // 4) as it:
                    for j in range(4):
                        act.wait_ge(weights_used, it * 24 + (first + 6 * j + 2))
                        act.activation(hid_exp[0:2 * m, :], ps[0:2 * m, 0, :], ACT.Silu).then_inc(sem("exp_silu"), 1)
                        act.wait_ge(sem("exp_turned"), it * 4 + (j + 1) + before("exp_turned", l))
                        turned = ps[:, 2, :].rearrange("p (b m) -> p b m", b=4)[:, :, 0:2 * m]
                        act.activation(hid_exp_t[:, 0:8 * m].rearrange("p (b m) -> p b m", b=4), turned, ACT.Copy).then_inc(sem("exp_hid_t"), 1)
                        act.wait_ge(weights_used, it * 24 + (first + 6 * j + 6))
                        for s in range(m // CAP):
                            o = (o_lat, o_ctx)[s]
                            ins = act.activation(o[32 * j:32 * j + 32, it, 0:512], ps[32 * s:32 * s + 32, 3, :], ACT.Copy)
                        ins.then_inc(sem("o_act"), 1)

            def ffn_group(i, n, it, step, tiles, following):
                per = 4 * it if it is not None else 0
                done, size = FFN_BANKS * i + step // 2, tiles // 2
                halve_lead(act, n + 2 if tiles == 4 else n + 1, it)
                for b in range(2):
                    act.wait_ge(sem("ffn_gate_scaled"), per + (done + b + 1))
                    gates = silu_f[:, size * b:size * b + size, :]
                    act.activation(gates, gates, ACT.Silu).then_inc(sem("ffn_silu"), 1)
                for b in range(2):
                    act.wait_ge(sem("ffn_hid"), per + (done + b + 1))
                    act.activation(hid_lead[:, size * b:size * b + size, :], hid_f[:, size * b:size * b + size, :], ACT.Copy)\
                        .then_inc(sem("ffn_led"), 1)
                    if b < len(following):
                        halve_lead(act, following[b], it)

            def ffn(i, following):
                n = chunk_at["ffn", i]
                halve_lead(act, n + 1)
                with act.Fori(0, FT // 8) as it:
                    ffn_group(i, n, it, 0, 4, (n + 3, n + 4))
                    ffn_group(i, n + 3, it, 4, 4, (n + 6, n + 7))
                at = FT // 8 * 8
                n += 3 * at // 4
                ffn_group(i, n, None, at, 4, (n + 3,))
                ffn_group(i, n + 3, None, at + 4, 2, (following,))

            def lru():
                v = lambda name: vec2[:, columns(VEC2, name)]
                n = chunk_at["lru", 0]
                for c in (1, 2, 5):
                    halve_lead(act, n + c)
                for o in range(RT):
                    if o == 4:
                        halve_lead(act, n + 6)
                    act.wait_ge(sem("lru_gate_in"), o + 1)
                    act.activation(l_r[:, o, :], ps[:, 3 + o % 4, 0:N], ACT.Sigmoid, bias=v("b_a")[:, o:o + 1])\
                        .then_inc(sem("lru_gates"), 1)
                    act.activation(l_i[:, o, :], ps[:, 3 + o % 4, N:2 * N], ACT.Sigmoid, bias=v("b_x")[:, o:o + 1])\
                        .then_inc(sem("lru_gates"), 1)
                act.wait_ge(sem("lru_gates"), 2 * RT)
                act.wait_ge(sem("lru_rate"), 1)
                act.wait_ge(sem("lru_conv"), RT)
                for o in range(RT):
                    act.activation(l_a[:, o, :], l_r[:, o, :], ACT.Exp, scale=lru_s[5][:, o:o + 1]).then_inc(sem("lru_a"), 1)
                for o in range(RT):
                    act.activation(l_r[:, o, :], l_r[:, o, :], ACT.Tanh, scale=lru_s[4][:, o:o + 1])\
                        .then_inc(sem("lru_decay"), 1)
                for o in range(RT):
                    act.wait_ge(sem("lru_square"), o + 1)
                    act.activation(l_r[:, o, :], l_r[:, o, :], ACT.Sqrt).then_inc(sem("lru_mult"), 1)
                halve_lead(act, n + 7)
                for o in range(RT):
                    act.wait_ge(sem("lru_branch_scaled"), o + 1)
                    act.activation(l_gate[:, o, :], l_gate[:, o, :], ACT.Gelu_apprx_tanh).then_inc(sem("lru_gelu"), 1)
                    if o == 3:
                        halve_lead(act, n + 8)
                for o in range(RT):
                    act.wait_ge(sem("lru_out"), o + 1)
                    act.activation(y_lead[:, o, :], l_gate[:, o, :], ACT.Copy).then_inc(sem("lru_led"), 1)
                halve_lead(act, n + 9)
                halve_lead(act, n + 10)
                halve_lead(act, chunk_at["ffn", 1])

            def pooling():
                scale = vec2[:, columns(VEC2, "pool_scale")]
                for d in range(KT):
                    act.wait_ge(sem("pool_mapped"), d // 2 + 1)
                    act.activation(pool_y[:, d, :], ps[:, 4 + d // 2, N * (d % 2):N * (d % 2) + N], ACT.Identity,
                                   bias=pool_bias[:, d:d + 1], scale=scale[:, d:d + 1]).then_inc(sem("pool_scaled"), 1)

            def ple(l):
                n = chunk_at["ple", l]
                halve_lead(act, n + 1)
                halve_lead(act, n + 2)
                for d in range(KT):
                    if d == 4 and l + 1 < LAYERS:
                        halve_lead(act, chunk_at["ffn", 2 * l + 2])
                    act.wait_ge(sem("ple_scaled"), KT * l + d + 1)
                    act.activation(silu_f[:, d % 4, :], silu_f[:, d % 4, :], ACT.Sigmoid).then_inc(sem("ple_gate"), 1)

            act.wait_ge(sem("setup_loaded"), 16 * 6)
            act.wait_ge(sem("cond_ready"), 1)
            act.activation(cond[:, :, 0:2], cond_in[:, :, :], ACT.Silu).then_inc(sem("cond_ready"), 1)
            act.wait_ge(sem("lru_abs"), 1)
            act.activation(lru_s[1][:, :], lru_s[0][:, :], ACT.Exp, scale=-1.0).then_inc(sem("lru_exp"), 1)
            act.wait_ge(sem("memsets"), 1)
            for l in range(LAYERS):
                norm_squares(act, 2 * l, ("moe_added", before("moe_added", l - 1), 1) if l else ("x_loaded", 31, KT))
                norm_act(act, 2 * l, rstd)
                n = chunk_at["w_in", l]
                if l == 0:
                    ada_group(0)
                    halve_lead(act, n)
                norm_in_lead(act, 2 * l, mod[:, l, 0:KT, :])
                if l == 0:
                    halve_lead(act, n + 1)
                projection(l, (0,))
                halve_lead(act, n + 2)
                projection(l, (1,))
                halve_lead(act, n + 3)
                act.wait_ge(sem("lam_sum"), l + 1)
                act.activation(lam_sum, lam_sum, ACT.Exp).then_inc(sem("lam_exp"), 1)
                qk_stats(l)
                projection(l, (2,))
                gate_stats(l)
                projection(l, (4,))
                read_qk_t(l, 0)
                if l == 0:
                    ada_group(1)
                read_fourier_uv(l)
                if l == 0:
                    ada_group(2)
                attention_c(l)
                read_qk_t(l, 1)
                if l == 0:
                    ada_group(3)
                attention_d(l)
                if l == 0:
                    ada_group(4)
                y_squares(l, 3)
                y_std(l, 3)
                merge(l)
                norm_squares(act, 2 * l + 1, ("mix_added", before("mix_added", l), 1))
                norm_act(act, 2 * l + 1, rstd)
                norm_shift(act, 2 * l + 1, mod[:, l, 3 * KT:4 * KT, :])
                route(l)
                experts(l)
                following = chunk_at["w_in", 1] if l == 0 else chunk_at["ffn", 0]
                halve_lead(act, following)
                if l == 0:
                    halve_lead(act, following + 1)
            for l in range(LAYERS):
                i = 4 + 4 * l
                norm_squares_lead(act, i, norm_gain("ffn1_norm", l),
                                  ("ple_added", KT * (l - 1), 1) if l else ("moe_added", before("moe_added", 1), 1))
                norm_act(act, i, rstd2)
                ffn(2 * l, chunk_at["lru", 0] if l == 0 else chunk_at["ffn", 3])
                if l == 0:
                    norm_squares_lead(act, i + 1, norm_gain("mix_norm", l), ("ffn_added", 0, 2))
                    norm_act(act, i + 1, rstd2)
                    lru()
                else:
                    norm_squares(act, i + 1, ("ffn_added", 4 * 2 * l, 2))
                    norm_act(act, i + 1, rstd2)
                    pooling()
                norm_squares_lead(act, i + 2, norm_gain("ffn2_norm", l),
                                  ("lru_added", 0, 2) if l == 0 else ("pool_added", 0, 1))
                norm_act(act, i + 2, rstd2)
                ffn(2 * l + 1, chunk_at["ple", l])
                norm_squares_lead(act, i + 3, norm_gain("ple_norm", l), ("ffn_added", 4 * (2 * l + 1), 2))
                norm_act(act, i + 3, rstd2)
                ple(l)
            norm_squares(act, LAST_NORM, ("ple_added", KT * (LAYERS - 1), 1))
            norm_act(act, LAST_NORM, rstd2)

        @block.vector
        def _(dve):
            count = [0]

            def link(ins):
                count[0] += 1
                ins.then_inc(sem("dve_chain"), 1)
                dve.wait_ge(sem("dve_chain"), count[0])

            def bc(ap, n):
                return bass.AP(ap.tensor, ap.offset, [list(x) for x in ap.ap] + [[0, n]])

            def bc_mid(ap, n):
                a = [list(x) for x in ap.ap]
                return bass.AP(ap.tensor, ap.offset, a[:-1] + [[0, n]] + a[-1:])

            def ada_group(step):
                l, i = divmod(step, 3)
                dve.wait_ge(sem("ada_turned"), step + 1)
                turned = ps[:, 7, :].rearrange("p (b j s) -> p j b s", b=4, j=4)[:, :, :, 0:2]
                bias = vec1[:, l, 16 * i:16 * i + 16].rearrange("p (j b) -> p j b", b=4)
                dst = mod[:, l, 16 * i:16 * i + 16, :].rearrange("p (j b) s -> p j b s", b=4)
                for s in range(2):
                    ins = dve.tensor_tensor(dst[:, :, :, s], turned[:, :, :, s], bias, ALU.add)
                    if s == 0:
                        link(ins)
                ins.then_inc(sem("ada_mod"), 1)
                dve.wait_ge(sem("ada_mod"), step + 1)

            def gains(l, which):
                dst, at, name = ((gain1, KT, "norm1_g"), (gain2, 4 * KT, "norm2_g"))[which]
                g = vec1[:, l, columns(VEC1, name)]
                link(dve.scalar_tensor_tensor(dst[:, :, :], mod[:, l, at:at + KT, :], 1.0, bc(g, 2), ALU.add, ALU.mult))

            def head_gains(l):
                lam_init = 0.8 - 0.6 * math.exp(-0.3 * l)
                hg = vec1[:, l, columns(VEC1, "head_out_g")][:, 4:6]
                dve.tensor_scalar(hg, hg, 1.0 - lam_init, None, ALU.mult).then_inc(sem("head_gain"), 1)
                dve.wait_ge(sem("head_gain"), l + 1)

            def row_constants(l):
                lam_init = 0.8 - 0.6 * math.exp(-0.3 * l)
                dve.wait_ge(sem("rows_loaded"), 32 + before("rows_loaded", l))
                for dst, table, name in ((rope_cos, "cos", "c_gain"), (rope_sin, "sin", "c_gain_swapped")):
                    t = const[:, columns(CONST, table)].rearrange("p (t d) -> p t d", t=4)
                    g = rows[:, columns(ROWS, name)].rearrange("p (w d) -> p w d", w=2)
                    for w in range(2):
                        gain = bc_mid(g[:, w, :], 4)
                        link(dve.tensor_tensor(dst[:, :, w, :], t, gain, ALU.mult))
                lam = rows[:, columns(ROWS, "lambda")].rearrange("p (a b d) -> p a b d", a=2, b=2)
                link(dve.tensor_tensor(lam_tmp.rearrange("p (a d) -> p a d", a=2), lam[:, :, 0, :], lam[:, :, 1, :], ALU.mult))
                dve.tensor_reduce(lam_sum, lam_tmp.rearrange("p (a d) -> p a d", a=2), AX, ALU.add).then_inc(sem("lam_sum"), 1)

            def lam_value(l):
                lam_init = 0.8 - 0.6 * math.exp(-0.3 * l)
                dve.wait_ge(sem("lam_exp"), l + 1)
                link(dve.tensor_tensor(neg_lam, lam_sum[:, 1:2], lam_sum[:, 0:1], ALU.subtract))
                link(dve.tensor_scalar(neg_lam, neg_lam, -lam_init, None, ALU.add))

            def projection(l):
                for j, (c, t, lo, width, engine) in enumerate(proj_jobs(l)):
                    if engine != "dve":
                        continue
                    dve.wait_ge(sem("proj_done"), j + 1 + before("proj_done", l))
                    dve.tensor_copy(vals[:, t, :], ps[:, j % 6, 0:width]).then_inc(sem("proj_read_dve"), 1)

            def group_sums(l, i, src, lo, n, width):
                dve.wait_ge(sem("mix_squares"), i + 1 + before("mix_squares", l))
                dve.tensor_reduce(mix_ss[:, lo:lo + n], src.rearrange("p (g d) -> p g d", d=width), AX, ALU.add)\
                    .then_inc(sem("mix_sums"), 1)

            def qk_norms(l):
                group_sums(l, 0, sq_c, 0, 64, DIFF)
                group_sums(l, 1, sq_d, 64, 32, HEAD)
                dve.wait_ge(sem("mix_std"), 2 + before("mix_std", l))
                link(dve.reciprocal(mix_ss[:, 0:96], mix_ss[:, 0:96]))
                for lo, groups, scale in ((0, 8, DIFF ** -0.5), (64, 4, HEAD ** -0.5)):
                    q = mix_ss[:, lo:lo + 8 * groups].rearrange("p (t w g) -> p t w g", t=4, w=2)[:, :, 0, :]
                    link(dve.tensor_scalar(q, q, scale, None, ALU.mult))
                c = qk_c.rearrange("p t f -> p (t f)").rearrange("p (g d) -> p g d", d=DIFF)
                dve.tensor_tensor(c, c, bc(mix_ss[:, 0:64], DIFF), ALU.mult).then_inc(sem("c_normed"), 1)
                dve.wait_ge(sem("c_normed"), 1 + before("c_normed", l))
                halve_rest(dve, chunk_at["w_in", l] + 4)
                dve.wait_ge(sem("c_swapped"), 2 + before("c_swapped", l))
                sw = swapped.rearrange("p (t f) -> p t f", t=4)
                for t in range(4):
                    for src, table in ((qk_c[:, t, :], rope_cos), (sw[:, t, :], rope_sin)):
                        v = src.rearrange("p (w g d) -> p w g d", w=2, d=DIFF)
                        ins = dve.tensor_tensor(v, v, bc_mid(table[:, t, :, :], 8), ALU.mult)
                link(ins)
                c = qk_c.rearrange("p t f -> p (t f)")
                dve.tensor_tensor(c, c, swapped, ALU.add).then_inc(sem("qk_ready"), 1)
                d = qk_d.rearrange("p t f -> p (t f)").rearrange("p (g d) -> p g d", d=HEAD)
                link(dve.tensor_tensor(d, d, bc(mix_ss[:, 64:96], HEAD), ALU.mult))
                g = rows[:, columns(ROWS, "d_gain")].rearrange("p (w d) -> p w d", w=2)
                for t in range(4):
                    v = qk_d[:, t, :].rearrange("p (w h d) -> p w h d", w=2, d=HEAD)
                    ins = dve.tensor_tensor(v, v, bc_mid(g, HEADS), ALU.mult)
                ins.then_inc(sem("qk_ready"), 1)

            def gate_norm(l):
                tiles = 4 if l == 0 else 2
                group_sums(l, 2, sq_v[:, 0:GROUP * tiles], 96, 4 * tiles, HEAD)
                dve.wait_ge(sem("mix_std"), 3 + before("mix_std", l))
                link(dve.reciprocal(mix_ss[:, 96:96 + 4 * tiles], mix_ss[:, 96:96 + 4 * tiles]))
                for t in range(tiles):
                    v = gated[:, t, GROUP:2 * GROUP].rearrange("p (g d) -> p g d", d=HEAD)
                    ins = dve.tensor_tensor(v, v, bc(mix_ss[:, 96 + 4 * t:100 + 4 * t], HEAD), ALU.mult)
                ins.then_inc(sem("v_normed"), 1)

            def spatial_gating(l):
                tiles = 4 if l == 0 else 2
                dve.wait_ge(sem("sgu_mixed"), 1 + before("sgu_mixed", l))
                dve.wait_ge(sem("qk_ready"), 2 + before("qk_ready", l))
                b = vec1[:, l, columns(VEC1, "sgu_b")]
                for h in range(HEADS):
                    cols = slice(HEAD * h, HEAD * h + HEAD)
                    mixed = ps[:, 4 + h // 2, N * (h % 2):N * (h % 2) + HEAD * tiles].rearrange("p (t c) -> p t c", t=tiles)
                    ins = dve.scalar_tensor_tensor(ycat[:, 0:tiles, cols], mixed, b[:, h:h + 1], gated[:, 0:tiles, cols],
                                                   ALU.add, ALU.mult)
                ins.then_inc(sem("sgu_done"), 1)

            def read_fourier(l):
                for s in range(2 if l == 0 else 1):
                    dve.wait_ge(sem("fourier_done"), 2 * s + 2 + before("fourier_done", l))
                    dve.tensor_copy(ycat[:, 2 * s:2 * s + 2, GROUP:2 * GROUP],
                                    ps[:, 4 + s, :].rearrange("p (t f) -> p t f", t=2)).then_inc(sem("fourier_read"), 1)

            def read_qk_t(l, which):
                for b in (1, 3):
                    dve.wait_ge(sem("qk_turned"), 4 * which + b + 1 + before("qk_turned", l))
                    width = 512 if l == 0 or b >= 2 else N
                    dve.tensor_copy(qk_t[:, b, 0:width], ps[:, b, 0:width]).then_inc(sem("qk_t_dve"), 1)

            def attention_c(l):
                todo = units(l)

                def maxima(u):
                    width = keys(todo[u][0])[1]
                    for m in range(2):
                        i = 2 * u + m
                        dve.wait_ge(sem("c_scores"), i + 1 + before("c_scores", l))
                        dve.tensor_reduce(c_max[:, i:i + 1], ps[:, 2 * (u % 3) + m, 0:width], AX, ALU.max, negate=True)\
                            .then_inc(sem("c_max"), 1)

                def read_out(q):
                    dve.wait_ge(sem("c_pv"), HEADS * (q + 1) + before("c_pv", l))
                    dve.tensor_copy(ycat[:, q, 2 * GROUP:3 * GROUP], ps[:, 7, 0:GROUP]).then_inc(sem("c_out"), 1)

                def weights(u):
                    width = keys(todo[u][0])[1]
                    den = c_den[:, 2 * u:2 * u + 2]
                    dve.wait_ge(sem("c_exp"), 2 * u + 2 + before("c_exp", l))
                    link(dve.reciprocal(den, den))
                    link(dve.tensor_tensor(den[:, 1:2], den[:, 1:2], neg_lam, ALU.mult))
                    e0, e1 = (expo[:, 2 * (u % 3) + m, 0:width] for m in range(2))
                    link(dve.tensor_scalar(e1, e1, den[:, 1:2], None, ALU.mult))
                    dve.scalar_tensor_tensor(e0, e0, den[:, 0:1], e1, ALU.mult, ALU.add).then_inc(sem("c_weights"), 1)

                for u in range(3):
                    maxima(u)
                weights(0)
                for u, (q, h) in enumerate(todo):
                    if u + 1 < len(todo):
                        weights(u + 1)
                    if u + 3 < len(todo):
                        maxima(u + 3)
                    if h == 0 and q > 0:
                        read_out(q - 1)
                read_out(todo[-1][0])

            def attention_d(l):
                todo = units(l)

                def maximum(u):
                    width = keys(todo[u][0])[1]
                    dve.wait_ge(sem("d_scores"), u + 1 + before("d_scores", l))
                    dve.tensor_reduce(d_max[:, u:u + 1], ps[:, u % 3, 0:width], AX, ALU.max, negate=True)\
                        .then_inc(sem("d_max"), 1)

                def scale_out(u):
                    q, h = todo[u]
                    dve.wait_ge(sem("d_pv"), u + 1 + before("d_pv", l))
                    dve.tensor_scalar(ycat[:, q, 3 * GROUP + HEAD * h:3 * GROUP + HEAD * h + HEAD],
                                      ps[:, (6, 3)[u % 2], 0:HEAD], d_den[:, u:u + 1], None, ALU.mult).then_inc(sem("d_out"), 1)

                maximum(0)
                maximum(1)
                for u in range(len(todo)):
                    if u in (3, 5, 7):
                        y_norm(l, u // 2 - 1)
                    if u in (1, 3, 5):
                        y_sums(l, u // 2)
                    if u == len(todo) // 2:
                        halve_rest(dve, chunk_at["w_out", l])
                    if u + 2 < len(todo):
                        maximum(u + 2)
                    dve.wait_ge(sem("d_exp"), u + 1 + before("d_exp", l))
                    link(dve.reciprocal(d_den[:, u:u + 1], d_den[:, u:u + 1]))
                    if u:
                        scale_out(u - 1)
                scale_out(len(todo) - 1)

            def y_sums(l, piece):
                tiles = 4 if l == 0 else 2
                _, heads, at = Y_PIECES[piece]
                dve.wait_ge(sem("y_squares"), piece + 1 + before("y_squares", l))
                ss = y_ss[:, at:at + heads * tiles]
                dve.tensor_reduce(ss, y_sq[:, 0:tiles * heads * HEAD].rearrange("p (g d) -> p g d", d=HEAD), AX, ALU.add)\
                    .then_inc(sem("y_sums"), 1)

            def y_norm(l, piece):
                tiles = 4 if l == 0 else 2
                lo, heads, at = Y_PIECES[piece]
                ss = y_ss[:, at:at + heads * tiles]
                dve.wait_ge(sem("y_std"), piece + 1 + before("y_std", l))
                link(dve.reciprocal(ss, ss))
                for t in range(tiles):
                    y = ycat[:, t, lo:lo + heads * HEAD].rearrange("p (g d) -> p g d", d=HEAD)
                    ins = dve.tensor_tensor(y, y, bc(ss[:, heads * t:heads * t + heads], HEAD), ALU.mult)
                ins.then_inc(sem("y_normed"), 1)

            def merge(l):
                tiles = 4 if l == 0 else 2
                for k in range(KT):
                    dve.wait_ge(sem("y_t"), k + 1 + before("y_t", l))
                    at = slice(0, P * tiles)
                    dve.scalar_tensor_tensor(out_rest[:, k, at], ps[:, k % 6, at], head_gain(l)[:, k:k + 1], out_lead[:, k, at],
                                             ALU.mult, ALU.subtract).then_inc(sem("y_rest"), 1)
                halve_rest(dve, chunk_at["w_out", l] + 1)
                add_gated(l, "mix_out", "mix_added", 2 * KT, 6, 1, tiles // 2)

            def add_gated(l, produced, added, at, banks, first, streams):
                for d in range(KT):
                    dve.wait_ge(sem(produced), d + 1 + before(produced, l))
                    for s in range(streams):
                        x = x_res[:, d, N * s:N * s + N]
                        ins = dve.scalar_tensor_tensor(x, ps[:, first + d % banks, N * s:N * s + N],
                                                       mod[:, l, at + d, s:s + 1], x, ALU.mult, ALU.add)
                    ins.then_inc(sem(added), 1)

            def route(l):
                tiles = 4 if l == 0 else 2
                streams = tiles // 2
                rows_ = 48 if l == 0 else 16
                raw = ps[:, 0, 0:EXPERTS * tiles].rearrange("p (t e) -> p t e", t=tiles)
                lg = logit[:, 0:EXPERTS * tiles].rearrange("p (t e) -> p t e", t=tiles)
                for j in range(2 * tiles):
                    half, t = divmod(j, tiles)
                    dve.wait_ge(sem("h_tok_lead"), j + 1 + before("h_tok_lead", l))
                    dve.tensor_tensor(h_tok_rest[half][:, t, :], ps[:, 1 + j % 4, :], h_tok[:, t, 512 * half:512 * half + 512],
                                      ALU.subtract).then_inc(sem("h_tok_rest"), 1)
                    if j == 1:
                        dve.wait_ge(sem("logits_turned"), 1 + before("logits_turned", l))
                        link(dve.tensor_reduce(r_max[:, 0:tiles], raw, AX, ALU.max))
                        dve.tensor_tensor(lg, raw, bc(r_max[:, 0:tiles], EXPERTS), ALU.subtract).then_inc(sem("logits_shifted"), 1)
                    if j == tiles:
                        dve.wait_ge(sem("logits_exp"), 1 + before("logits_exp", l))
                        link(dve.tensor_reduce(r_sum[:, 0:tiles], lg, AX, ALU.add))
                        link(dve.reciprocal(r_sum[:, 0:tiles], r_sum[:, 0:tiles]))
                        dve.tensor_tensor(lg, lg, bc(r_sum[:, 0:tiles], EXPERTS), ALU.mult).then_inc(sem("aff"), 1)
                dve.wait_ge(sem("aff_turned"), 1 + before("aff_turned", l))
                if l == 0:
                    link(dve.memset(aff_t[0:48, :], 0.0))
                for s in range(streams):
                    link(dve.tensor_copy(aff_t[32 * s:32 * s + EXPERTS, :], ps[0:EXPERTS, 0, N * s:N * s + N]))
                src = aff_t
                for r in range(CAP // 8):
                    link(dve.max(top8[0:rows_, :], src[0:rows_, :]))
                    link(dve.match_replace(work[0:rows_, :], top8[0:rows_, :], src[0:rows_, :], -1.0))
                    src = work
                link(dve.tensor_scalar(slot_id[0:rows_, :], work[0:rows_, :], -1.0, None, ALU.is_equal))
                link(dve.tensor_scalar(work[0:rows_, :], work[0:rows_, :], 0.0, 1.0, ALU.mult, ALU.add))
                link(dve.tensor_tensor_scan(cum[0:rows_, :], work[0:rows_, :], slot_id[0:rows_, :], 0.0, ALU.mult, ALU.add))
                dve.tensor_tensor(slot_id[0:rows_, :], cum[0:rows_, :], slot_id[0:rows_, :], ALU.mult).then_inc(sem("slots"), 1)
                dve.wait_ge(sem("slots_turned"), 1 + before("slots_turned", l))
                turned = ps[:, 0, 0:96].rearrange("p (a r) -> p a r", a=2)
                for s in range(streams):
                    ins = dve.tensor_copy(slot_tokens[:, 2 * s:2 * s + 2, :], turned[:, :, 32 * s:32 * s + EXPERTS])
                    link(ins)
                for t in range(tiles):
                    ins = dve.tensor_tensor(gather[:, t, :, :], bc(slot_tokens[:, t, :], CAP), bc_mid(slot_row, EXPERTS),
                                            ALU.is_equal)
                ins.then_inc(sem("gather_ready"), 1)
                for s in range(streams):
                    aff, rows_of = aff_t[32 * s:32 * s + EXPERTS, :], spread_rows[:, s, :, :]
                    link(dve.tensor_copy(rows_of[0:64, :, :], zeros[0:64, :].rearrange("p (w t) -> p w t", w=2)))
                    link(dve.tensor_copy(rows_of[0:EXPERTS, 0, :], aff))
                    link(dve.tensor_copy(rows_of[0:EXPERTS, 1, :], slot_id[32 * s:32 * s + EXPERTS, :]))
                    dve.tensor_tensor(rows_of[32:32 + EXPERTS, 0, :], aff, rows_of[0:EXPERTS, 0, :], ALU.subtract)\
                        .then_inc(sem("spread_rows"), 1)
                if l == 0:
                    ada_group(5)
                for j in range(1, KT * streams, 2):
                    s, k = divmod(j, KT)
                    dve.wait_ge(sem("gathered"), j + 1 + before("gathered", l))
                    dve.tensor_copy(picked_of(l)[:, k, :, CAP * s:CAP * s + CAP],
                                    ps[:, j % 6, :].rearrange("p (e s) -> p e s", e=EXPERTS)).then_inc(sem("picked_dve"), 1)
                for s in range(streams):
                    dve.wait_ge(sem("aff_copied"), s + 1 + before("aff_copied", l))
                    for g in range(4):
                        ins = dve.scalar_tensor_tensor(scatter[:, s, g, :], ps[:, 4 + g, N:2 * N], slot_col, aff_bc[:, g, :],
                                                       ALU.is_equal, ALU.mult)
                    ins.then_inc(sem("scatter_ready"), 1)

            def experts(l):
                m = 2 * CAP if l == 0 else CAP
                dve.wait_ge(sem("picked_act"), KT // 2 * (m // CAP) + before("picked_act", l))
                dve.wait_ge(sem("picked_dve"), KT // 2 * (m // CAP) + before("picked_dve", l))
                dve.wait_ge(sem("gathered"), KT * (m // CAP) + before("gathered", l))

                def tokens(e, j):
                    dst = x_exp[:, 512 * (j % 2):512 * (j % 2) + KT * m].rearrange("p (k m) -> p k m", k=KT)
                    dve.tensor_copy(dst, picked_of(l)[:, :, e, :]).then_inc(sem("x_exp"), 1)

                first = chunk_at["experts", l]
                with dve.Fori(0, EXPERTS // 4) as it:
                    tokens(it * 4, 0)
                    for j in range(4):
                        dve.wait_ge(sem("exp_silu"), it * 4 + (j + 1) + before("exp_silu", l))
                        dve.wait_ge(weights_used, it * 24 + (first + 6 * j + 4))
                        hid = hid_exp[0:2 * m, :]
                        dve.tensor_tensor(hid, hid, ps[0:2 * m, 1, :], ALU.mult).then_inc(sem("exp_hid"), 1)
                        if j < 3:
                            tokens(it * 4 + (j + 1), j + 1)
                        dve.wait_ge(weights_used, it * 24 + (first + 6 * j + 6))
                        for s in range(m // CAP):
                            o = (o_lat, o_ctx)[s]
                            ins = dve.tensor_copy(o[32 * j:32 * j + 32, it, 512:1024], ps[m + 32 * s:m + 32 * s + 32, 3, :])
                        ins.then_inc(sem("o_dve"), 1)

            def ffn_group(i, n, it, step, tiles, following):
                per = 4 * it if it is not None else 0
                done, size = FFN_BANKS * i + step // 2, tiles // 2
                halve_rest(dve, n + 2 if tiles == 4 else n + 1, it)

                def bank(b):
                    return ps[:, b, 0:N * size].rearrange("p (f t) -> p f t", f=size)

                factors = bc_mid(rstd2, size)
                for b in range(2):
                    dve.wait_ge(sem("ffn_gate"), per + (done + b + 1))
                    dve.tensor_tensor(silu_f[:, size * b:size * b + size, :], bank(1 + b),
                                      factors, ALU.mult).then_inc(sem("ffn_gate_scaled"), 1)
                for b in range(2):
                    mine = slice(size * b, size * b + size)
                    dve.wait_ge(sem("ffn_up"), per + (done + b + 1))
                    dve.tensor_tensor(hid_f[:, mine, :], bank((3, 0)[b]),
                                      factors, ALU.mult).then_inc(sem("ffn_up_scaled"), 1)
                    dve.wait_ge(sem("ffn_up_scaled"), per + (done + b + 1))
                    dve.wait_ge(sem("ffn_silu"), per + (done + b + 1))
                    dve.tensor_tensor(hid_f[:, mine, :], silu_f[:, mine, :], hid_f[:, mine, :], ALU.mult)\
                        .then_inc(sem("ffn_hid"), 1)
                    dve.wait_ge(sem("ffn_led"), per + (done + b + 1))
                    dve.tensor_tensor(hid_rest[:, mine, :], hid_f[:, mine, :], hid_lead[:, mine, :], ALU.subtract)\
                        .then_inc(sem("ffn_halved"), 1)
                for c in following:
                    halve_rest(dve, c, it)

            def ffn(i, following):
                n = chunk_at["ffn", i]
                halve_rest(dve, n + 1)
                with dve.Fori(0, FT // 8) as it:
                    ffn_group(i, n, it, 0, 4, (n + 3, n + 4))
                    ffn_group(i, n + 3, it, 4, 4, (n + 6, n + 7))
                at = FT // 8 * 8
                n += 3 * at // 4
                ffn_group(i, n, None, at, 4, (n + 3,))
                ffn_group(i, n + 3, None, at + 4, 2, (following,))
                add_sums(0.5, "ffn_summed", 4 * i, "ffn_added")

            def add_sums(scale, summed, start, added):
                for b in range(4):
                    dve.wait_ge(sem(summed), start + b + 1)
                    x = x_res[:, 2 * b:2 * b + 2, 0:N]
                    dve.scalar_tensor_tensor(x, ps[:, 4 + b, :].rearrange("p (d t) -> p d t", d=2), scale, x,
                                             ALU.mult, ALU.add).then_inc(sem(added), 1)

            def softplus_rate():
                a = vec2[:, columns(VEC2, "a_param")]
                s = [t[:, :] for t in lru_s]
                link(dve.tensor_scalar(s[2], a, -1.0, None, ALU.mult))
                dve.tensor_tensor(s[0], a, s[2], ALU.max).then_inc(sem("lru_abs"), 1)
                link(dve.tensor_scalar(s[2], s[2], 0.0, None, ALU.max))
                dve.wait_ge(sem("lru_exp"), 1)
                link(dve.tensor_scalar(s[3], s[1], 2.0, None, ALU.add))
                link(dve.reciprocal(s[3], s[3]))
                link(dve.tensor_tensor(s[1], s[1], s[3], ALU.mult))
                link(dve.tensor_tensor(s[3], s[1], s[1], ALU.mult))
                link(dve.tensor_scalar(s[4], s[3], 1.0 / 17, None, ALU.mult))
                for c in range(15, 2, -2):
                    link(dve.scalar_tensor_tensor(s[4], s[4], 1.0 / c, s[3], ALU.add, ALU.mult))
                link(dve.scalar_tensor_tensor(s[4], s[4], 1.0, s[1], ALU.add, ALU.mult))
                link(dve.scalar_tensor_tensor(s[4], s[4], 2.0, s[2], ALU.mult, ALU.add))
                link(dve.tensor_scalar(s[4], s[4], 8.0, None, ALU.mult))
                dve.tensor_scalar(s[5], s[4], -1.0, None, ALU.mult).then_inc(sem("lru_rate"), 1)

            def lru():
                v = lambda name: vec2[:, columns(VEC2, name)]
                link(dve.memset(l_pad[:, :, 0:CONV - 1], 0.0))
                n = chunk_at["lru", 0]
                halve_rest(dve, n + 1)
                halve_rest(dve, n + 2)
                w = v("conv_w")
                for o in range(RT):
                    dve.wait_ge(sem("lru_in"), o + 1)
                    dve.tensor_tensor(l_pad[:, o, CONV - 1:CONV - 1 + N], ps[:, (1 + o) % 8, 0:N], rstd2, ALU.mult).then_inc(sem("lru_read_dve"), 1)
                    dve.wait_ge(sem("lru_read_dve"), o + 1)
                    link(dve.tensor_scalar(l_x[:, o, :], l_pad[:, o, 0:N], w[:, o:o + 1], v("conv_b")[:, o:o + 1],
                                           ALU.mult, ALU.add))
                    for tap in range(1, CONV):
                        ins = dve.scalar_tensor_tensor(l_x[:, o, :], l_pad[:, o, tap:tap + N], w[:, RT * tap + o:RT * tap + o + 1],
                                                       l_x[:, o, :], ALU.mult, ALU.add)
                        if tap < CONV - 1:
                            link(ins)
                    ins.then_inc(sem("lru_conv"), 1)
                halve_rest(dve, n + 5)
                for o in range(RT):
                    if o == 4:
                        halve_rest(dve, n + 6)
                    dve.wait_ge(sem("lru_gates"), 2 * o + 2)
                    ins = dve.tensor_tensor(l_i[:, o, :], l_i[:, o, :], l_x[:, o, :], ALU.mult)
                link(ins)
                dve.wait_ge(sem("lru_gate_in"), RT)
                for o in range(RT):
                    dve.wait_ge(sem("lru_a"), o + 1)
                    ins = dve.tensor_tensor(l_x[:, o, :], l_a[:, o, :], l_a[:, o, :], ALU.mult)
                link(ins)
                for o in range(RT):
                    dve.wait_ge(sem("lru_decay"), o + 1)
                    dve.scalar_tensor_tensor(l_r[:, o, :], l_x[:, o, :], 1.0, l_r[:, o, :], ALU.add, ALU.mult)\
                        .then_inc(sem("lru_square"), 1)
                for o in range(RT):
                    if o in (4, 8):
                        halve_rest(dve, n + 6 + o // 4)
                    dve.wait_ge(sem("lru_branch"), o + 1)
                    dve.tensor_tensor(l_gate[:, o, :], ps[:, (7 + o) % 8, 0:N], rstd2, ALU.mult)\
                        .then_inc(sem("lru_branch_scaled"), 1)
                    dve.wait_ge(sem("lru_mult"), o + 1)
                    link(dve.tensor_tensor(l_i[:, o, :], l_i[:, o, :], l_r[:, o, :], ALU.mult))
                    ins = dve.tensor_tensor_scan(l_x[:, o, :], l_a[:, o, :], l_i[:, o, :], 0.0, ALU.mult, ALU.add)
                link(ins)

                def rest(o):
                    dve.wait_ge(sem("lru_led"), o + 1)
                    dve.tensor_tensor(y_rest[:, o, :], l_gate[:, o, :], y_lead[:, o, :], ALU.subtract)\
                        .then_inc(sem("lru_y"), 1)

                for o in range(RT):
                    dve.wait_ge(sem("lru_gelu"), o + 1)
                    dve.tensor_tensor(l_gate[:, o, :], l_gate[:, o, :], l_x[:, o, :], ALU.mult).then_inc(sem("lru_out"), 1)
                    if o >= 2:
                        rest(o - 2)
                rest(RT - 2)
                rest(RT - 1)
                halve_rest(dve, n + 9)
                halve_rest(dve, n + 10)
                halve_rest(dve, chunk_at["ffn", 1])
                add_sums(1.0, "lru_summed", 0, "lru_added")

            def pooling(gain):
                norm_factors(dve, link, POOL_NORM, rstd2)
                end = KT - 2
                norm_tiles(dve, POOL_NORM, rstd2, gain, [*range(end, KT), 0, 1])
                dve.wait_ge(sem("norm_scaled"), scaled_before[POOL_NORM] + 4)
                dve.wait_ge(sem("pool_inv_loaded"), 16)

                def double(src, g, lo, hi):
                    back, dst = POOLS[g] // 2, (pool_a, pool_b)[g % 2]
                    dve.tensor_copy(dst[:, lo:hi, 0:back], src[:, lo:hi, 0:back])
                    link(dve.tensor_tensor(dst[:, lo:hi, back:N], src[:, lo:hi, back:N], src[:, lo:hi, 0:N - back], ALU.add))
                    return dst

                def less_own(sums, g):
                    at = slice(2 * g, 2 * g + 2)
                    u = pool_u[:, at, :]
                    link(dve.tensor_tensor(u, sums[:, at, :], bc_mid(pool_inv[:, g, :], 2), ALU.mult))
                    dve.tensor_tensor(u, u, h_buf[:, at, 0:N], ALU.subtract).then_inc(sem("pool_ready"), 1)

                less_own(double(h_buf[:, :, 0:N], 0, 0, 2), 0)
                norm_tiles(dve, POOL_NORM, rstd2, gain, range(2, end))
                dve.wait_ge(sem("norm_scaled"), scaled_before[POOL_NORM + 1])
                src = double(h_buf[:, :, 0:N], 0, 2, end)
                for g in range(1, len(POOLS) - 1):
                    src = double(src, g, 2 * g, end)
                    less_own(src, g)
                for d in range(KT):
                    dve.wait_ge(sem("pool_scaled"), d + 1)
                    x = x_res[:, d, 0:N]
                    dve.tensor_tensor(x, x, pool_y[:, d, :], ALU.add).then_inc(sem("pool_added"), 1)

            def ple(l):
                n = chunk_at["ple", l]
                halve_rest(dve, n + 1)
                halve_rest(dve, n + 2)

                def add(d):
                    dve.wait_ge(sem("ple_gate"), KT * l + d + 1)
                    y = hid_f[:, d % 4, :]
                    link(dve.tensor_tensor(y, silu_f[:, d % 4, :], ps[:, 1 + d % 6, N:2 * N], ALU.mult))
                    x = x_res[:, d, 0:N]
                    dve.tensor_tensor(x, x, y, ALU.add).then_inc(sem("ple_added"), 1)

                for d in range(KT):
                    if d == 4 and l + 1 < LAYERS:
                        halve_rest(dve, chunk_at["ffn", 2 * l + 2])
                    dve.wait_ge(sem("ple_products"), KT * l + d + 1)
                    dve.tensor_tensor(silu_f[:, d % 4, :], ps[:, 1 + d % 6, 0:N], rstd2, ALU.mult).then_inc(sem("ple_scaled"), 1)
                    if d:
                        add(d - 1)
                add(KT - 1)

            link(dve.memset(mean_w[:, :], 1.0 / D))
            link(dve.memset(eps_col[:, :], EPS))
            dve.memset(cond[:, :, :], 0.0).then_inc(sem("cond_ready"), 1)
            dve.memset(zeros[:, :], 0.0).then_inc(sem("memsets"), 1)
            dve.wait_ge(sem("setup_loaded"), 16 * 6)
            dve.tensor_copy(expand[:, :], expand_in).then_inc(sem("expand_ready"), 1)
            softplus_rate()
            link(dve.tensor_tensor(pool_bias, vec2[:, columns(VEC2, "pool_b")], vec2[:, columns(VEC2, "pool_scale")], ALU.mult))
            for l in range(LAYERS):
                n = chunk_at["w_in", l]
                norm_factors(dve, link, 2 * l, rstd)
                if l == 0:
                    ada_group(0)
                gains(l, 0)
                if l == 0:
                    halve_rest(dve, n)
                norm_in_dve(dve, link, 2 * l, rstd, gain1, mod[:, l, 0:KT, :])
                if l == 0:
                    halve_rest(dve, n + 1)
                head_gains(l)
                row_constants(l)
                halve_rest(dve, n + 2)
                halve_rest(dve, n + 3)
                qk_norms(l)
                gate_norm(l)
                projection(l)
                lam_value(l)
                read_qk_t(l, 0)
                spatial_gating(l)
                if l == 0:
                    ada_group(1)
                read_fourier(l)
                if l == 0:
                    ada_group(2)
                attention_c(l)
                read_qk_t(l, 1)
                if l == 0:
                    ada_group(3)
                attention_d(l)
                if l == 0:
                    ada_group(4)
                y_sums(l, 3)
                y_norm(l, 3)
                merge(l)
                gains(l, 1)
                norm_dve(dve, link, 2 * l + 1, rstd, lambda k, s: gain2[:, k, s:s + 1])
                route(l)
                experts(l)
                following = chunk_at["w_in", 1] if l == 0 else chunk_at["ffn", 0]
                halve_rest(dve, following)
                if l == 0:
                    halve_rest(dve, following + 1)
                add_gated(l, "moe_out", "moe_added", 5 * KT, 4, 4, 2 if l == 0 else 1)
            for l in range(LAYERS):
                i = 4 + 4 * l

                norm_rest(dve, link, i, rstd2, norm_gain("ffn1_norm", l))
                ffn(2 * l, chunk_at["lru", 0] if l == 0 else chunk_at["ffn", 3])
                mix_gain = norm_gain("mix_norm", l)
                if l == 0:
                    norm_rest(dve, link, i + 1, rstd2, mix_gain)
                    lru()
                else:
                    pooling(lambda k, s: mix_gain(k))
                norm_rest(dve, link, i + 2, rstd2, norm_gain("ffn2_norm", l))
                ffn(2 * l + 1, chunk_at["ple", l])
                norm_rest(dve, link, i + 3, rstd2, norm_gain("ple_norm", l))
                ple(l)
            final = vec2[:, columns(VEC2, "final_norm")]
            norm_dve(dve, link, LAST_NORM, rstd2, lambda k, s: final[:, k:k + 1])


def host_constants():
    f = np.float32
    tok = np.arange(N)
    const = {
        "ident": np.eye(P, dtype=f),
        "slot_row": np.broadcast_to(np.arange(1, CAP + 1, dtype=f), (P, CAP)),
        "slot_col": (np.arange(P) % CAP + 1).astype(f)[:, None],
    }
    const["band_c"] = np.kron(np.eye(P // DIFF), np.ones((DIFF, 1)))
    const["band_d"] = np.kron(np.eye(P // HEAD), np.ones((HEAD, 1)))
    half = DIFF // 2
    inv = (1.0 / (10000.0 ** (np.arange(0, half, 2, dtype=f) / f(half)))).astype(f)
    row, col = ((a.astype(f)[:, None] * inv).astype(f) for a in (tok // GRID_W, tok % GRID_W))
    cos = np.concatenate([np.cos(row), np.cos(row), np.cos(col), np.cos(col)], 1).astype(f)
    sin = np.concatenate([-np.sin(row), np.sin(row), -np.sin(col), np.sin(col)], 1).astype(f)
    cos = np.concatenate([cos, np.ones_like(cos)]).reshape(4, P, DIFF)
    sin = np.concatenate([sin, np.zeros_like(sin)]).reshape(4, P, DIFF)
    const["cos"] = cos.transpose(1, 0, 2).reshape(P, 4 * DIFF)
    const["sin"] = sin.transpose(1, 0, 2).reshape(P, 4 * DIFF)
    q, k = np.arange(P) % GRID_W, tok % GRID_W
    start = np.clip(q - NA_COLS // 2, 0, GRID_W - NA_COLS)
    inside = (k[None] >= start[:, None]) & (k[None] < start[:, None] + NA_COLS)
    turn = 2 * np.pi * np.outer(tok, tok) / N
    scale = 1.0 / math.sqrt(N * HEAD)
    turn_d = 2 * np.pi * np.outer(np.arange(HEAD), np.arange(HEAD)) / HEAD
    two = np.eye(P // HEAD)

    def on_partitions(a):
        return a.reshape(2, P, N).transpose(1, 0, 2).reshape(P, 2 * N)

    att = {
        "mask": np.where(inside, 0.0, NEG),
        "cos_n": on_partitions(np.cos(turn) * scale),
        "sin_n": on_partitions(-np.sin(turn) * scale),
        "cs_d": np.concatenate([np.kron(two, np.cos(turn_d)), np.kron(two, np.sin(turn_d))], 1),
    }
    expand = np.zeros((64, 4, 4, CAP), f)
    for e in range(EXPERTS):
        expand[e, e // 4, e % 4] = expand[32 + e, e // 4, e % 4] = 1
    count = np.stack([1.0 / np.minimum(tok + 1, w).astype(f) for w in POOLS]).astype(f)

    def packed(parts, widths):
        return np.ascontiguousarray(np.concatenate([parts[n] for n in widths], 1).astype(f))

    return {
        "const": packed(const, CONST), "att": packed(att, ATT),
        "expand": np.ascontiguousarray(expand.reshape(64, 512)),
        "pool_inv": np.ascontiguousarray(np.broadcast_to(count.reshape(1, -1), (P, 4 * N))),
    }


def host_layout(a):
    def feat(v):
        return v.reshape(-1, P).T

    vec1 = np.stack([np.concatenate([feat(a["ada_b"][l]), feat(a["norm1_g"][l]), feat(a["norm2_g"][l]),
                                     feat(a["head_out_g"][l]), a["sgu_b"][l].T], 1) for l in range(LAYERS)], 1)
    both = [np.concatenate([feat(a[n + "_2"][l]) for l in range(LAYERS)], 1)
            for n in ("ffn1_norm", "mix_norm", "ffn2_norm", "ple_norm")]
    vec2 = np.concatenate(both + [
        feat(a["lru_conv_w_2"][0].reshape(-1)), feat(a["lru_conv_b_2"][0]), feat(a["lru_b_a_2"][0]), feat(a["lru_b_x_2"][0]),
        feat(a["lru_a_param_2"][0]), feat(a["pool_b_2"][0]), feat(a["pool_scale_2"][0]), feat(a["final_norm_2"])], 1)
    partner = np.arange(DIFF).reshape(2, 2, 8)[:, ::-1].reshape(-1)
    qg, kg = a["diff_qn_g"], a["diff_kn_g"]
    rows = np.concatenate([qg, kg, qg[:, partner], kg[:, partner], a["na_qn_g"], a["na_kn_g"],
                           a["diff_lambda"].reshape(LAYERS, -1)], 1)

    def blocks(w):
        full = np.zeros((D_RNN, D_RNN), w.dtype)
        for h in range(D_RNN // LRU_HEAD):
            at = slice(h * LRU_HEAD, (h + 1) * LRU_HEAD)
            full[at, at] = w[h]
        return np.concatenate([full[k * P:k * P + P, o * P:o * P + P] for o, k in PAIRS], 1)

    row, col = np.divmod(np.arange(N), GRID_W)
    row_off = row[None] - row[:, None] + NA_ROWS - 1
    col_off = np.clip(col[None] - col[:, None], 1 - NA_COLS, NA_COLS - 1) + NA_COLS - 1
    rel_bias = a["na_rpb"][:, :, row_off, col_off].reshape(LAYERS, HEADS, 2, P, N).transpose(0, 3, 2, 1, 4)
    cond = np.stack([a["c"][0], a["c_ctx"]]).reshape(2, KT, P).transpose(2, 1, 0)
    router = a["router_w"].reshape(LAYERS, KT, P, EXPERTS).transpose(2, 0, 1, 3).reshape(P, -1)
    return {
        "x_t": a["x"][0].T, "ctx_t": a["ctx"][0].T, "cond_t": cond, "vec1": vec1, "vec2": vec2,
        "rows": np.broadcast_to(rows[:, None, :], (LAYERS, P, ROWS_W)), "router": router,
        "sgu_t": a["sgu_w"].transpose(0, 3, 1, 2), "rel_bias": rel_bias,
        "ada_w": a["ada_w"], "w_in": a["w_in"], "w_out": a["w_out"],
        "exp_gate": a["exp_w_gate"], "exp_up": a["exp_w_up"], "exp_down": a["exp_w_down"],
        "ffn1_gate": a["ffn1_w_gate_2"], "ffn1_up": a["ffn1_w_up_2"], "ffn1_down": a["ffn1_w_down_2"],
        "ffn2_gate": a["ffn2_w_gate_2"], "ffn2_up": a["ffn2_w_up_2"], "ffn2_down": a["ffn2_w_down_2"],
        "lru_in": a["lru_w_in_2"][0], "lru_a": blocks(a["lru_w_a_2"][0]), "lru_x": blocks(a["lru_w_x_2"][0]),
        "lru_out": a["lru_w_out_2"][0], "pool_w": a["pool_w_2"][0].reshape(D, GROUP),
        "ple_gate": a["ple_w_gate_2"], "ple_proj": a["ple_w_proj_2"], "p_t": a["p_2"][:, 0].transpose(0, 2, 1),
    }


def kernel(**inputs):
    import concourse.bacc as bacc
    from concourse.bass_utils import run_bass_kernel_spmd

    nc = bacc.Bacc("TRN2", target_bir_lowering=False, num_devices=1)
    arrays = {**host_layout({k: np.asarray(v) for k, v in inputs.items()}), **host_constants()}
    arrays = {f"in_{k}": np.ascontiguousarray(v) for k, v in arrays.items()}
    dram = {k[3:]: nc.dram_tensor(k, v.shape, F32, kind="ExternalInput").ap() for k, v in arrays.items()}
    out_t = nc.dram_tensor("out_t", (D, N), F32, kind="ExternalOutput").ap()
    build(nc, dram, out_t)
    r = run_bass_kernel_spmd(nc, [arrays], core_ids=[0])
    return np.ascontiguousarray(r.results[0]["out_t"].T)[None]
```
